# Optimizing a Trainium2 kernel written in Bass

```python
import math
import jax, jax.numpy as jnp
from jax import lax
import numpy as np

D_MODEL = 1024
BATCH = 1
SEQ = 512
DEPTH = 2

CHUNK = 64
Q_BLOCK = 128
N_MIXERS = 2
N_FOX = (DEPTH + 1) // 2
N_GDN = DEPTH // 2
FOX_HEADS = 16
FOX_HEAD_DIM = D_MODEL // FOX_HEADS
GDN_HEADS = 8
GDN_HEAD_DIM = D_MODEL // GDN_HEADS
CONV_WIDTH = 4
N_EXPERTS = 16
N_GROUPS = 4
EXPERTS_PER_GROUP = N_EXPERTS // N_GROUPS
TOPK_GROUPS = 1
TOP_K = 2
D_EXPERT = D_MODEL // 2
MOE_BLOCK = 256
DN_ALPHA = (2.0 * DEPTH) ** 0.25
DN_BETA = (8.0 * DEPTH) ** -0.25
LN_EPS = 1e-5
RMS_EPS = 1e-6
L2_EPS = 1e-6

kernel_name = 'hybrid_fox_gdn_groupmoe_deepnorm'

def _layer_norm(x, g, b):
    xf = x.astype(jnp.float32)
    mu = jnp.mean(xf, axis=-1, keepdims=True)
    xc = xf - mu
    var = jnp.mean(xc * xc, axis=-1, keepdims=True)
    y = xc * lax.rsqrt(var + LN_EPS) * g.astype(jnp.float32) + b.astype(jnp.float32)
    return y.astype(x.dtype)

def _rms_norm(x, g):
    xf = x.astype(jnp.float32)
    y = xf * lax.rsqrt(jnp.mean(xf * xf, axis=-1, keepdims=True) + RMS_EPS)
    return (y * g.astype(jnp.float32)).astype(x.dtype)

def _l2norm(x):
    xf = x.astype(jnp.float32)
    return xf * lax.rsqrt(jnp.sum(xf * xf, axis=-1, keepdims=True) + L2_EPS)

def fox_mixer(x, w_in, b_f, q_gain, k_gain, w_out):
    bsz, seq, d = x.shape
    h, dh = FOX_HEADS, FOX_HEAD_DIM
    proj = x @ w_in
    q, k, v, og, f_logit = jnp.split(proj, [d, 2 * d, 3 * d, 4 * d], axis=-1)
    q = _rms_norm(q.reshape(bsz, seq, h, dh), q_gain)
    k = _rms_norm(k.reshape(bsz, seq, h, dh), k_gain)
    v = v.reshape(bsz, seq, h, dh)
    log_f = jax.nn.log_sigmoid(f_logit.astype(jnp.float32) + b_f.astype(jnp.float32))
    c = jnp.cumsum(log_f, axis=1).transpose(0, 2, 1)
    scale = dh ** -0.5
    outs = []
    for blk in range(seq // Q_BLOCK):
        lo, hi = blk * Q_BLOCK, (blk + 1) * Q_BLOCK
        s = jnp.einsum('bqhd,bkhd->bhqk', q[:, lo:hi], k[:, :hi],
                       preferred_element_type=jnp.float32) * scale
        s = s + c[:, :, lo:hi, None] - c[:, :, None, :hi]
        qpos = lo + jnp.arange(Q_BLOCK)[:, None]
        kpos = jnp.arange(hi)[None, :]
        s = jnp.where(kpos <= qpos, s, -jnp.inf)
        p = jax.nn.softmax(s, axis=-1).astype(v.dtype)
        outs.append(jnp.einsum('bhqk,bkhd->bqhd', p, v[:, :hi]))
    o = jnp.concatenate(outs, axis=1).reshape(bsz, seq, d)
    return (o * jax.nn.sigmoid(og)) @ w_out

def _causal_conv(x, w):
    kw, ch = w.shape
    return lax.conv_general_dilated(
        x, w.reshape(kw, 1, ch).astype(x.dtype), window_strides=(1,), padding=[(kw - 1, 0)],
        dimension_numbers=('NWC', 'WIO', 'NWC'), feature_group_count=ch)

def _chunk_gated_delta_rule(q, k, v, beta, g):
    bsz, seq, h, dk = q.shape
    dv = v.shape[-1]
    n = seq // CHUNK

    def to_chunks(t):
        t = t.astype(jnp.float32).reshape((bsz, n, CHUNK, h) + t.shape[3:])
        return jnp.moveaxis(t, 3, 1)

    q, k, v, beta, g = (to_chunks(t) for t in (q, k, v, beta, g))
    g = jnp.cumsum(g, axis=-1)
    idx = jnp.arange(CHUNK)
    strict = idx[:, None] > idx[None, :]
    incl = idx[:, None] >= idx[None, :]
    decay = jnp.exp(jnp.where(incl, g[..., :, None] - g[..., None, :], -jnp.inf))
    kb = k * beta[..., None]
    m = jnp.where(strict, jnp.einsum('bhncd,bhnsd->bhncs', kb, k) * decay, 0.0)
    sys_mat = jnp.eye(CHUNK, dtype=jnp.float32) + m
    rhs = jnp.concatenate([v * beta[..., None], kb * jnp.exp(g)[..., None]], axis=-1)
    sol = lax.linalg.triangular_solve(sys_mat, rhs, left_side=True, lower=True, unit_diagonal=True)
    u, w = sol[..., :dv], sol[..., dv:]
    attn = jnp.einsum('bhncd,bhnsd->bhncs', q, k) * decay
    q_dec = q * jnp.exp(g)[..., None]
    k_dec = k * jnp.exp(g[..., -1:] - g)[..., None]
    g_last = jnp.exp(g[..., -1])

    def step(state, xs):
        q_i, k_i, u_i, w_i, a_i, gl_i = xs
        v_new = u_i - jnp.einsum('bhcd,bhde->bhce', w_i, state)
        o_i = jnp.einsum('bhcd,bhde->bhce', q_i, state) + jnp.einsum('bhcs,bhse->bhce', a_i, v_new)
        state = state * gl_i[..., None, None] + jnp.einsum('bhcd,bhce->bhde', k_i, v_new)
        return state, o_i

    xs = tuple(jnp.moveaxis(t, 2, 0) for t in (q_dec, k_dec, u, w, attn, g_last))
    state0 = jnp.zeros((bsz, h, dk, dv), jnp.float32)
    _, o = lax.scan(step, state0, xs)
    return o.transpose(1, 0, 3, 2, 4).reshape(bsz, seq, h, dv)

def gdn_mixer(x, w_in, conv_w, a_log, dt_bias, norm_g, w_out):
    bsz, seq, d = x.shape
    h, dk = GDN_HEADS, GDN_HEAD_DIM
    proj = x @ w_in
    qkv, og, b_logit, a_logit = jnp.split(proj, [3 * d, 4 * d, 4 * d + h], axis=-1)
    qkv = jax.nn.silu(_causal_conv(qkv, conv_w))
    q, k, v = jnp.split(qkv, 3, axis=-1)
    q = _l2norm(q.reshape(bsz, seq, h, dk)) * (dk ** -0.5)
    k = _l2norm(k.reshape(bsz, seq, h, dk))
    v = v.reshape(bsz, seq, h, dk)
    beta = jax.nn.sigmoid(b_logit.astype(jnp.float32))
    g = -jnp.exp(a_log.astype(jnp.float32)) * jax.nn.softplus(
        a_logit.astype(jnp.float32) + dt_bias.astype(jnp.float32))
    o = _chunk_gated_delta_rule(q, k, v, beta, g).astype(x.dtype)
    o = _rms_norm(o, norm_g) * jax.nn.silu(og.reshape(bsz, seq, h, dk))
    return o.reshape(bsz, seq, d) @ w_out

def _route(hf, router_w, router_b):
    ntok = hf.shape[0]
    probs = jax.nn.softmax((hf @ router_w).astype(jnp.float32), axis=-1)
    sel = (probs + router_b.astype(jnp.float32)).reshape(ntok, N_GROUPS, EXPERTS_PER_GROUP)
    grp_score = jnp.sum(lax.top_k(sel, 2)[0], axis=-1)
    _, gidx = lax.top_k(grp_score, TOPK_GROUPS)
    gmask = jnp.sum(jax.nn.one_hot(gidx, N_GROUPS, dtype=jnp.float32), axis=1) > 0
    masked = jnp.where(gmask[:, :, None], sel, -jnp.inf).reshape(ntok, N_EXPERTS)
    _, eidx = lax.top_k(masked, TOP_K)
    gate = jnp.take_along_axis(probs, eidx, axis=-1)
    gate = gate / jnp.sum(gate, axis=-1, keepdims=True)
    return eidx, gate

def moe_ffn(h, router_w, router_b, w_gate, w_up, w_down):
    bsz, seq, d = h.shape
    hf = h.reshape(-1, d)
    ntok = hf.shape[0]
    eidx, gate = _route(hf, router_w, router_b)
    n_assign = ntok * TOP_K
    e_flat = eidx.reshape(-1)
    tok_flat = jnp.repeat(jnp.arange(ntok, dtype=jnp.int32), TOP_K)
    g_flat = gate.reshape(-1)
    order = jnp.argsort(e_flat)
    e_s, tok_s, g_s = e_flat[order], tok_flat[order], g_flat[order]
    counts = jnp.bincount(e_flat, length=N_EXPERTS)
    start = jnp.cumsum(counts) - counts
    padded = (counts + MOE_BLOCK - 1) // MOE_BLOCK * MOE_BLOCK
    pend = jnp.cumsum(padded)
    pstart = pend - padded
    slot = pstart[e_s] + (jnp.arange(n_assign) - start[e_s])
    n_blocks = -(-(n_assign + N_EXPERTS * (MOE_BLOCK - 1)) // MOE_BLOCK)
    n_slots = n_blocks * MOE_BLOCK
    slot_tok = jnp.zeros((n_slots,), jnp.int32).at[slot].set(tok_s)
    slot_gate = jnp.zeros((n_slots,), jnp.float32).at[slot].set(g_s)
    block_expert = jnp.minimum(
        jnp.searchsorted(pend, jnp.arange(n_blocks) * MOE_BLOCK, side='right'), N_EXPERTS - 1)

    def expert_block(args):
        e, toks, gts = args
        xb = hf[toks]
        hid = jax.nn.silu(xb @ w_gate[e]) * (xb @ w_up[e])
        return ((hid @ w_down[e]).astype(jnp.float32) * gts[:, None])

    yb = lax.map(expert_block, (block_expert, slot_tok.reshape(n_blocks, MOE_BLOCK),
                                slot_gate.reshape(n_blocks, MOE_BLOCK)))
    out = jax.ops.segment_sum(yb.reshape(n_slots, d), slot_tok, num_segments=ntok)
    return out.astype(h.dtype).reshape(bsz, seq, d)

def setup_inputs(seed: int = 0) -> dict:
    key = jax.random.key(seed)
    ks = iter(jax.random.split(key, 32))
    d, e, f = D_MODEL, N_EXPERTS, D_EXPERT
    nrm = lambda shape, s: jax.random.normal(next(ks), shape, jnp.float32) * s
    ones_n = lambda shape: 1.0 + 0.02 * jax.random.normal(next(ks), shape, jnp.float32)
    x = jax.random.normal(next(ks), (BATCH, SEQ, d), jnp.float32)
    ln_mix_g = ones_n((DEPTH, d))
    ln_mix_b = nrm((DEPTH, d), 0.02)
    ln_ffn_g = ones_n((DEPTH, d))
    ln_ffn_b = nrm((DEPTH, d), 0.02)
    router_w = nrm((d, e), d ** -0.5)
    router_b = nrm((e,), 0.01)
    fox_w_in = nrm((N_FOX, d, 4 * d + FOX_HEADS), d ** -0.5)
    fox_b_f = jax.random.uniform(next(ks), (N_FOX, FOX_HEADS), jnp.float32, 1.0, 5.0)
    fox_q_gain = ones_n((N_FOX, FOX_HEAD_DIM))
    fox_k_gain = ones_n((N_FOX, FOX_HEAD_DIM))
    fox_w_out = nrm((N_FOX, d, d), d ** -0.5 * DN_BETA)
    gdn_w_in = nrm((N_GDN, d, 4 * d + 2 * GDN_HEADS), d ** -0.5)
    gdn_conv_w = nrm((N_GDN, CONV_WIDTH, 3 * d), CONV_WIDTH ** -0.5)
    gdn_a_log = jnp.log(jax.random.uniform(next(ks), (N_GDN, GDN_HEADS), jnp.float32, 1.0, 16.0))
    dt = jnp.exp(jax.random.uniform(next(ks), (N_GDN, GDN_HEADS), jnp.float32,
                                    math.log(1e-3), math.log(1e-1)))
    gdn_dt_bias = dt + jnp.log(-jnp.expm1(-dt))
    gdn_norm_g = ones_n((N_GDN, GDN_HEAD_DIM))
    gdn_w_out = nrm((N_GDN, d, d), d ** -0.5 * DN_BETA)
    moe_w_gate = nrm((DEPTH, e, d, f), d ** -0.5)
    moe_w_up = nrm((DEPTH, e, d, f), d ** -0.5)
    moe_w_down = nrm((DEPTH, e, f, d), f ** -0.5 * DN_BETA)
    return {'x': x, 'ln_mix_g': ln_mix_g, 'ln_mix_b': ln_mix_b, 'ln_ffn_g': ln_ffn_g,
            'ln_ffn_b': ln_ffn_b, 'router_w': router_w, 'router_b': router_b,
            'fox_w_in': fox_w_in, 'fox_b_f': fox_b_f, 'fox_q_gain': fox_q_gain,
            'fox_k_gain': fox_k_gain, 'fox_w_out': fox_w_out, 'gdn_w_in': gdn_w_in,
            'gdn_conv_w': gdn_conv_w, 'gdn_a_log': gdn_a_log, 'gdn_dt_bias': gdn_dt_bias,
            'gdn_norm_g': gdn_norm_g, 'gdn_w_out': gdn_w_out, 'moe_w_gate': moe_w_gate,
            'moe_w_up': moe_w_up, 'moe_w_down': moe_w_down}

def reference(x, ln_mix_g, ln_mix_b, ln_ffn_g, ln_ffn_b, router_w, router_b,
              fox_w_in, fox_b_f, fox_q_gain, fox_k_gain, fox_w_out,
              gdn_w_in, gdn_conv_w, gdn_a_log, gdn_dt_bias, gdn_norm_g, gdn_w_out,
              moe_w_gate, moe_w_up, moe_w_down):
    h = x
    for i in range(DEPTH):
        j = i // N_MIXERS
        if i % N_MIXERS == 0:
            mix = fox_mixer(h, fox_w_in[j], fox_b_f[j], fox_q_gain[j], fox_k_gain[j], fox_w_out[j])
        else:
            mix = gdn_mixer(h, gdn_w_in[j], gdn_conv_w[j], gdn_a_log[j], gdn_dt_bias[j],
                            gdn_norm_g[j], gdn_w_out[j])
        h = _layer_norm(DN_ALPHA * h + mix, ln_mix_g[i], ln_mix_b[i])
        ffn = moe_ffn(h, router_w, router_b, moe_w_gate[i], moe_w_up[i], moe_w_down[i])
        h = _layer_norm(DN_ALPHA * h + ffn, ln_ffn_g[i], ln_ffn_b[i])
    return h


_drawn_inputs = setup_inputs


def setup_inputs(seed=0):
    import zlib

    import numpy as np

    out = dict(_drawn_inputs(seed))
    spreads = {}
    factors = {'fox_q_gain': 8.0, 'fox_k_gain': 8.0, 'gdn_norm_g': 3.378}
    for name, (base, spread) in spreads.items():
        noise = np.random.default_rng([zlib.crc32(name.encode()), seed]).standard_normal(out[name].shape)
        drawn = base * np.exp(spread * noise) if base else spread * noise
        out[name] = __import__('jax').numpy.asarray(drawn.astype(out[name].dtype))
    for name, factor in factors.items():
        out[name] = (out[name] * factor).astype(out[name].dtype)
    return out
```

```python
import math
from contextlib import ExitStack

import numpy as np

import concourse.bass as bass
from concourse import mybir

D = 1024
SEQ = 512
P = 128
NT = SEQ // P
ND = D // P
WB = 512
FOX_H, FOX_DH = 16, 64
NPAIR = FOX_H // 2
GDN_H = 8
NHP = GDN_H // 2
CONV = 4
NCT = 3 * ND
NE, NG, EPG = 16, 4, 4
DF = D // 2
NFK = DF // P
TB = 128
NB = -(-SEQ // TB)
ALPHA = (2.0 * 2) ** 0.25
LN_EPS, RMS_EPS, L2_EPS = 1e-5, 1e-6, 1e-6
BIG = 1e30
EMPTY = 4 * SEQ
LEVELS = 7

C_ID, C_ONE, C_UP, C_UPS = 0, 128, 256, 384
C_CAUS, C_CAUST = 512, 640
C_LVL = 768
C_GW = C_LVL + LEVELS * P
C_EW = C_GW + NT * NG
C_EI = C_EW + NT * NE
C_EPS = C_EI + NT * NE
C_TOT = C_EPS + 4
SMALL = 1732


def constants():
    c = np.zeros((P, C_TOT), np.float32)
    i, j = np.arange(P)[:, None], np.arange(P)[None, :]
    c[:, C_ID:C_ID + P] = i == j
    c[:, C_ONE:C_ONE + P] = 1.0
    c[:, C_UP:C_UP + P] = i <= j
    c[:, C_UPS:C_UPS + P] = i < j
    c[:, C_CAUS:C_CAUS + P] = np.where(j <= i, 0.0, -BIG)
    c[:, C_CAUST:C_CAUST + P] = np.where(i <= j, 0.0, -BIG)
    for v in range(LEVELS):
        b = 1 << v
        c[:, C_LVL + v * P:C_LVL + (v + 1) * P] = ((i >> v) % 2 == 0) & ((j >> v) == (i >> v) + 1)
    c[:, C_GW:C_EW] = np.tile(np.arange(NG, 0, -1), NT)
    c[:, C_EW:C_EI] = np.tile(np.arange(NE, 0, -1), NT)
    c[:, C_EI:C_EPS] = np.tile(np.arange(NE), NT)
    c[:, C_EPS:] = [LN_EPS, RMS_EPS, L2_EPS, 1.0]
    return c


def row_numbers():
    t = np.arange(P)[:, None, None] + P * np.arange(NT)[None, :, None]
    return (2 * t + np.arange(2)[None, None, :]).reshape(P, 2 * NT).astype(np.int32)


def hybrid_trunk(nc, io, out):
    f32, i32 = mybir.dt.float32, mybir.dt.int32
    ALU, ACT, X = mybir.AluOpType, mybir.ActivationFunctionType, mybir.AxisListType.X
    ctx = ExitStack()
    with ctx:
        def sb(name, cols, dt=f32, rows=P):
            return ctx.enter_context(nc.sbuf_tensor(name, [rows, cols], dt))

        def sem(name):
            return ctx.enter_context(nc.semaphore(name))

        def scratch(name, shape, dt=f32):
            return nc.dram_tensor(name, shape, dt, kind="Internal").ap()

        def as3(ap, n):
            return ap.rearrange("p (a b) -> p a b", a=n)

        def as4(ap, a, n):
            return ap.rearrange("p (a n c) -> p a n c", a=a, n=n)

        h_rows = [scratch(f"h_rows{l}", (SEQ, D)) for l in range(2)]
        h_mid = scratch("h_mid", (SEQ, D))
        y_rows = [scratch(f"y_rows{l}", (2 * SEQ, D)) for l in range(2)]
        tok_list = [scratch(f"tok_list{l}", (P * NE * NB, 1), i32) for l in range(2)]
        c_rows = scratch("c_rows", (FOX_H, SEQ))
        g_rows = scratch("g_rows", (NT * GDN_H, P))

        ring = sb("ring", 6 * 4096)
        area = [sb(f"area{n}", 4096) for n in range(6)]
        con = sb("con", C_TOT)
        small = sb("small", SMALL)
        smalli = sb("smalli", 2 * NE * NB + 2 * 2 * NT + 3, i32)
        ps = [ctx.enter_context(nc.psum_tensor(f"ps{n}", [P, 512], f32)) for n in range(8)]

        def slot(s):
            return ring[:, s * 4096:(s + 1) * 4096]

        def slot_k(s):
            return as3(slot(s), ND)

        ident, ones = con[:, C_ID:C_ID + P], con[:, C_ONE:C_ONE + P]
        upper, upper_strict = con[:, C_UP:C_UP + P], con[:, C_UPS:C_UPS + P]
        causal, causal_t = con[:, C_CAUS:C_CAUS + P], con[:, C_CAUST:C_CAUST + P]
        eps_ln, eps_rms, eps_l2, one = (con[:, C_EPS + n:C_EPS + n + 1] for n in range(4))

        hT = as3(area[0][:, :], ND)
        h = as3(area[1][:, :], NT)
        aoT = hT
        ln_sq, ln_g, ln_b = (area[5][:, 1024 * n:1024 * (n + 1)] for n in range(3))
        qkT = [as3(area[1][:, :], ND), as3(area[2][:, :], ND)]
        v_tok = as3(area[3][:, :], NT)
        ogT = as3(area[4][:, :], ND)
        cT = area[4][0:FOX_H, 0:SEQ]
        sq = as3(area[5][:, 0:1024], 2)
        qn = as3(area[5][:, 1024:2048], 2)
        s_buf = as3(area[5][:, 0:1536], 3)
        pT_buf = as3(area[5][:, 1536:2560], 2)
        c_buf = as3(area[5][:, 2560:4096], 3)
        xg = as3(area[2][:, 0:2048], 2)
        xT = as3(area[2][:, 2048:4096], 2)
        y_sb = as3(area[3][:, 0:2048], 2)
        sil, hid, hidT = (area[3][:, 2048 + 512 * n:2560 + 512 * n] for n in range(3))
        y_got = as3(area[4][:, :], 4)
        over_w = [as3(area[0][:, :], ND), as3(area[4][:, :], ND), as3(area[5][:, :], NFK)]
        qkvT = [as3(area[n][:, :], GDN_H) for n in (1, 2, 3)]
        qT, kT, vT = qkvT
        og_tok = as3(area[4][:, :], NT)
        conv_tmp = as3(area[5][:, 0:1024], 2)
        sq_l2 = as3(area[5][:, 1024:2048], 2)
        r_l2 = as3(area[5][:, 2048:3072], 2)
        conv_raw = area[5][0:CONV * NCT, 3072:3200]
        gT_sb = area[5][0:NT * GDN_H, 3200:3328]
        (inv, invT, tmpT, attnT, dec, q_dec, k_gate, k_tok, v_chunk, g_bc, mT, g_exp) = (
            as4(ring[:, (12 + n) * 1024:(13 + n) * 1024], 2, NT) for n in range(12))
        mlT = [as4(area[5][:, 1024 * n:1024 * (n + 1)], 2, NT) for n in range(2)]
        o_tok = as4(area[5][:, 2048:3072], 2, NT)
        r_sb, vn_sb, st = (as3(area[5][:, 3072 + 256 * n:3328 + 256 * n], 2) for n in range(3))

        at = [0]

        def cols(n):
            at[0] += n
            assert at[0] <= SMALL
            return small[:, at[0] - n:at[0]]

        neg_mean, ssq, rstd, sum2 = cols(NT), cols(NT), cols(NT), cols(2 * NT)
        w_f, w_ab, router_w = (as3(cols(ND * 16), ND) for _ in range(3))
        conv_w = cols(CONV * NCT)
        bf_bc, gain, rb_bc = cols(NT * FOX_H), cols(2), cols(NT * NE)
        dt_bc, al_bc, ng_col = cols(NT * GDN_H), cols(NT * GDN_H), cols(1)
        lf, f_z, f_e, c_tok = (cols(NT * FOX_H) for _ in range(4))
        head_ss, head_r = as3(cols(16), 2), as3(cols(16), 2)
        neg_max, row_sum, row_inv = cols(3), cols(3), cols(3)
        tok_f = small[:, at[0]:at[0] + NE * NB]
        probs, selv, oh0, oh1, rtmp, rkey = (cols(NT * NE) for _ in range(6))
        rmx, rsm = cols(NT), cols(NT)
        gr = [cols(NT * NG) for _ in range(8)]
        gate = [cols(NT), cols(NT)]
        gsum, pos, exp_n, blk, cmax = cols(NT), cols(NT), cols(NT), cols(NT), cols(1)
        gc_tok, beta, g_z, g_e, g_t = (cols(NT * GDN_H) for _ in range(5))
        kd, egl, o_ss, o_r = (cols(8) for _ in range(4))
        i0 = 2 * NE * NB
        row_list, tok_of = smalli[:, 0:NE * NB], smalli[:, NE * NB:i0]
        addr_i, rowno_i = smalli[:, i0:i0 + 8], smalli[:, i0 + 8:i0 + 16]
        cnt_i, row_i, one_tok = (smalli[:, i0 + 16 + n:i0 + 17 + n] for n in range(3))

        con_in, par_in = sem("con_in"), sem("par_in")
        x_in = [sem(f"x_in{t}") for t in range(NT)]
        ring_in = [sem(f"ring_in{s}") for s in range(6)]
        ring_free = [sem(f"ring_free{s}") for s in range(6)]
        act_link, dve_link, pool_link = sem("act_link"), sem("dve_link"), sem("pool_link")
        tr_pe, tr_act, tr_dve = sem("tr_pe"), sem("tr_act"), sem("tr_dve")
        gain_ready, conv_pe, convw_ready = sem("gain_ready"), sem("conv_pe"), sem("convw_ready")
        fox_gates, gdn_gates, routing = sem("fox_gates"), sem("gdn_gates"), sem("routing")
        (F_PE, F_ABS, F_LN, LF_READY, CSUM_PE, C_READY, CT_PE) = range(1, 8)
        (AB_PE, BETA_EXP, G_ABS, G_EXP1, G_READY, GC_PE, GC_READY, GT_PE) = range(1, 9)
        (RT_PE, RT_SUB, RT_EXP, OH_READY, POS_PE, ADDR_READY) = range(1, 7)
        ROUTE = 6
        c_st, g_st = sem("c_st"), sem("g_st")
        proj_pe, sq_done, head_sum, head_rs, qn_done, qT_pe, qT_ev, v_ev, og_exp, og_ready = (
            sem(n) for n in ("proj_pe", "sq_done", "head_sum", "head_rs", "qn_done", "qT_pe", "qT_ev", "v_ev", "og_exp", "og_ready"))
        c_in = [sem(f"c_in{n}") for n in range(3)]
        s_pe, s_sub, max_done, p_exp, p_ready, pT_pe, pT_ev, pv_pe, o_ev = (
            sem(n) for n in ("s_pe", "s_sub", "max_done", "p_exp", "p_ready", "pT_pe", "pT_ev", "pv_pe", "o_ev"))
        res_in, ln_in, out_pe, mix_acc = sem("res_in"), sem("ln_in"), sem("out_pe"), sem("mix_acc")
        mean_ready, rstd_ready, h_ready = sem("mean_ready"), sem("rstd_ready"), sem("h_ready")
        hrow_st, hmid_st, out_st = sem("hrow_st"), sem("hmid_st"), sem("out_st")
        list_zero, list_sc, list_in = sem("list_zero"), sem("list_sc"), sem("list_in")
        xg_in = [sem(f"xg_in{n}") for n in range(2)]
        y_st = [sem(f"y_st{n}") for n in range(2)]
        yg_in = [sem(f"yg_in{n}") for n in range(2)]
        comb_done = sem("comb_done")
        EXPERT = ("gate_pe", "up_pe", "xTa_pe", "xTb_pe", "xTa_ev", "xTb_ev", "sil_done", "hid_done",
                  "hidT_pe", "hidT_ev", "ya_pe", "yb_pe", "ya_ev", "yb_ev")
        ex = {n: (sem(n), 1, 1) for n in EXPERT}
        ov = []
        for l in range(2):
            steps = {"w_in": (sem(f"ov{l}_w_in"), 48, 48)}
            steps |= {n: (sem(f"ov{l}_{n}"), 16, 16) for n in ("x_in", "st")}
            steps["idx"] = (sem(f"ov{l}_idx"), 2, 2)
            for eng, names in (("pe", ("xTa_pe", "xTb_pe", "gate_pe", "up_pe", "hidT_pe", "ya_pe", "yb_pe")),
                               ("act", ("xTa_ev", "sil_done", "hidT_ev", "ya_ev")),
                               ("dve", ("xTb_ev", "hid_done", "yb_ev"))):
                done = sem(f"ov{l}_{eng}")
                steps |= {n: (done, len(names), k + 1) for k, n in enumerate(names)}
            ov.append(steps)
        cv_pe, conv_done, silu_done, sq2_done, ss_pe, rn_done, l2_done, ogg_pe, ogg_ev = (
            sem(n) for n in ("cv_pe", "conv_done", "silu_done", "sq2_done", "ss_pe", "rn_done", "l2_done", "ogg_pe", "ogg_ev"))
        gbc_in, kk_pe, dec_arg, dec_done, gexp_done, mT_done, att_done, kv_pe, kd_arg, k_ev, v_evg = (
            sem(n) for n in ("gbc_in", "kk_pe", "dec_arg", "dec_done", "gexp_done", "mT_done", "att_done", "kv_pe", "kd_arg", "k_ev", "v_evg"))
        ml_done, xT0, T_pe, T_ev, U_pe, X_ev, XT_ev = (
            sem(n) for n in ("ml_done", "xT0", "T_pe", "T_ev", "U_pe", "X_ev", "XT_ev"))
        R_pe, r_done, V_pe, vn_done, O_pe, K_pe, st_done, o_cp, or_done, on_done, oT_pe, gao_ev = (
            sem(n) for n in ("R_pe", "r_done", "V_pe", "vn_done", "O_pe", "K_pe", "st_done", "o_cp", "or_done", "on_done", "oT_pe", "gao_ev"))

        def ge(eng, s, v):
            if not isinstance(v, int) or v > 0:
                eng.wait_ge(s, v)

        def after(eng, v, step, n):
            s, per, first = v[step]
            ge(eng, s, n * per + first)

        def linker(eng, s):
            n = [0]

            def link(ins):
                n[0] += 1
                ins.then_inc(s, 1)
                eng.wait_ge(s, n[0])
            return link

        N_PAR = 14
        MIX_LOADS = (4, 3, 3)

        def ring_no(l, s):
            return l * (8 + (MIX_LOADS[s] if s < 3 else 0))

        def expert_no(l, s):
            return ring_no(l, s) + (MIX_LOADS[s] if s < 3 else 0)

        block = ctx.enter_context(nc.Block())

        @block.sync
        def _(sp):
            sp.dma_start(con[:, :], io["con"]).then_inc(con_in, 16)
            for t in range(NT):
                sp.dma_start(h[:, t, :], io["x"][0, t * P:(t + 1) * P, :]).then_inc(x_in[t], 16)

            def mixer_block(l, b, w_in, w_out):
                s, n = b % 3, ring_no(l, b % 3) + b // 3
                ge(sp, ring_free[s], n)
                w = w_in[0, :, b * WB:(b + 1) * WB] if b < 8 else w_out[0, :, (b - 8) * WB:(b - 7) * WB]
                sp.dma_start(slot_k(s), w.rearrange("(k p) n -> p k n", p=P)).then_inc(ring_in[s], 16)

            def expert_load(l, e, i, par):
                for j, name in enumerate(("moe_w_gate", "moe_w_up", "moe_w_down")):
                    s = 3 * par + j
                    ge(sp, ring_free[s], expert_no(l, s) + i)
                    dst = slot_k(s) if j < 2 else as3(slot(s), NFK)
                    sp.dma_start(dst, io[name][l, e, :, :].rearrange("(k p) n -> p k n", p=P)).then_inc(ring_in[s], 16)

            for l, (w_in, w_out) in enumerate(((io["fox_w_in"], io["fox_w_out"]), (io["gdn_w_in"], io["gdn_w_out"]))):
                for b in range(3):
                    mixer_block(l, b, w_in, w_out)
                if l == 0:
                    expert_load(0, 1, 0, 1)
                else:
                    for t in range(NT):
                        sp.wait_ge(h_ready, 8 * l - 4 + t + 1)
                        sp.dma_start(h_mid[t * P:(t + 1) * P, :], h[:, t, :]).then_inc(hmid_st, 16)
                for b in range(3, 10):
                    mixer_block(l, b, w_in, w_out)
                expert_load(l, 0, 0, 0)
                if l == 1:
                    sp.wait_ge(gao_ev, GDN_H)
                    expert_load(1, 1, 0, 1)
                for t in range(NT):
                    sp.wait_ge(h_ready, 8 * l + t + 1)
                    sp.dma_start(h_rows[l][t * P:(t + 1) * P, :], h[:, t, :]).then_inc(hrow_st, 16)
                with sp.Fori(1, NE // 2) as i:
                    for par in range(2):
                        expert_load(l, 2 * i + par, i, par)
            for t in range(NT):
                sp.wait_ge(h_ready, 12 + t + 1)
                sp.dma_start(out[0, t * P:(t + 1) * P, :], h[:, t, :]).then_inc(out_st, 16)
            sp.wait_ge(out_st, 16 * NT)

        @block.gpsimd
        def _(pool):
            link = linker(pool, pool_link)
            link(nc.gpsimd.memset(row_list, EMPTY))
            for l in range(2):
                pool.dma_start(tok_list[l].rearrange("(p n) a -> p (n a)", p=P), row_list).then_inc(list_zero, 16)

            def layer_norm_params(q, g, b):
                pool.dma_start(ln_g, g.partition_broadcast(P)).then_inc(ln_in, 16)
                pool.dma_start(ln_b, b.partition_broadcast(P)).then_inc(ln_in, 16)

            def moe(l):
                def rows_in(dst, tokens, done):
                    nc.gpsimd.indirect_dma_start(
                        out=dst, out_offset=None, in_=h_rows[l], in_offset=bass.IndirectOffsetOnAxis(ap=tokens, axis=0),
                        bounds_check=SEQ - 1, oob_is_err=False).then_inc(done, 16)

                def rows_back(src, rows, done):
                    nc.gpsimd.indirect_dma_start(
                        out=y_rows[l], out_offset=bass.IndirectOffsetOnAxis(ap=rows, axis=0), in_=src, in_offset=None,
                        bounds_check=2 * SEQ - 1, oob_is_err=False).then_inc(done, 16)

                link(nc.gpsimd.memset(xg, 0.0))
                pool.wait_ge(routing, ROUTE * l + ADDR_READY)
                pool.wait_ge(list_zero, 32)
                for j in range(2 * NT):
                    nc.gpsimd.indirect_dma_start(
                        out=tok_list[l], out_offset=bass.IndirectOffsetOnAxis(ap=addr_i[:, j:j + 1], axis=0),
                        in_=rowno_i[:, j:j + 1], in_offset=None).then_inc(list_sc, 16)
                pool.wait_ge(list_sc, 16 * 2 * NT * (l + 1))
                pool.dma_start(row_list, tok_list[l].rearrange("(p n) a -> p (n a)", p=P)).then_inc(list_in, 16)
                pool.wait_ge(list_in, 16 * (l + 1))
                pool.wait_ge(hrow_st, 64 * (l + 1))
                link(nc.gpsimd.tensor_scalar(tok_f, row_list, 0.5, -0.25, ALU.mult, ALU.add))
                link(nc.gpsimd.tensor_copy(tok_of, tok_f))

                def gather(e):
                    if e >= 2:
                        after(pool, ex, "xTb_pe", NE * l + e - 2)
                    rows_in(xg[:, e % 2, :], tok_of[:, NB * e:NB * e + 1], xg_in[e % 2])

                gather(0)
                gather(1)
                for e in range(NE):
                    if e + 2 < NE:
                        gather(e + 2)
                    after(pool, ex, "ya_ev", NE * l + e)
                    after(pool, ex, "yb_ev", NE * l + e)
                    rows_back(y_sb[:, e % 2, :], row_list[:, NB * e:NB * e + 1], y_st[e % 2])
                v = ov[l]
                more = pool.value_load(cnt_i[0:1, 0:1], min_val=0, max_val=SEQ)
                with pool.If(more > TB):
                    with pool.Fori(0, NE) as e:
                        with pool.Fori(0, NB - 1) as b:
                            r = e * (NB - 1) + b
                            for dst, name in zip(over_w, ("moe_w_gate", "moe_w_up", "moe_w_down")):
                                pool.dma_start(dst, io[name][l, e, :, :].rearrange("(k p) n -> p k n", p=P)).then_inc(v["w_in"][0], 16)
                            nc.gpsimd.tensor_copy(one_tok, tok_of[:, bass.ds(e * NB + b + 1, 1)]).then_inc(v["idx"][0], 1)
                            nc.gpsimd.tensor_copy(row_i, row_list[:, bass.ds(e * NB + b + 1, 1)]).then_inc(v["idx"][0], 1)
                            after(pool, v, "idx", r)
                            pool.nop(nofuse=True)
                            rows_in(xg[:, 0, :], one_tok, v["x_in"][0])
                            after(pool, v, "yb_ev", r)
                            after(pool, v, "ya_ev", r)
                            pool.nop(nofuse=True)
                            rows_back(y_sb[:, 0, :], row_i, v["st"][0])
                            after(pool, v, "st", r)
                pool.wait_ge(hrow_st, 64 * (l + 1))
                layer_norm_params(2 * l + 1, io["ln_ffn_g"][l, :], io["ln_ffn_b"][l, :])
                for n in range(2):
                    pool.wait_ge(y_st[n], 16 * 8 * (l + 1))
                y_by_choice = y_rows[l].rearrange("(t a) d -> t a d", a=2)
                for t in range(NT):
                    ge(pool, comb_done, 4 * l + t - 1 if t >= 2 else 0)
                    for a in range(2):
                        pool.dma_start(y_got[:, 2 * (t % 2) + a, :], y_by_choice[t * P:(t + 1) * P, a, :]).then_inc(yg_in[t % 2], 16)

            pool.wait_ge(c_st, 16)
            pool.wait_ge(qT_ev, 16)
            for hd in range(FOX_H):
                ge(pool, s_sub, NT * (hd - 2))
                pool.dma_start(c_buf[:, hd % 3, :], c_rows[hd, :].partition_broadcast(P)).then_inc(c_in[hd % 3], 16)
            pool.wait_ge(pv_pe, FOX_H * NT)
            for t in range(NT):
                pool.dma_start(h[:, t, :], io["x"][0, t * P:(t + 1) * P, :]).then_inc(res_in, 16)
            layer_norm_params(0, io["ln_mix_g"][0, :], io["ln_mix_b"][0, :])
            moe(0)

            pool.wait_ge(g_st, 16)
            g_by_head = g_rows.rearrange("(n a) c -> a n c", a=GDN_H)
            for pr in range(NHP):
                ge(pool, gao_ev, 2 * pr)
                if pr == 0:
                    after(pool, ex, "yb_pe", NE - 1)
                for a in range(2):
                    pool.dma_start(g_bc[:, a, :, :], g_by_head[2 * pr + a, :, :].partition_broadcast(P)).then_inc(gbc_in, 16)
                pool.wait_ge(mT_done, pr + 1)
                for v in range(LEVELS):
                    ge(pool, T_pe, 14 * pr + 2 * (v - 1) if v >= 2 else 0)
                    if v == 2:
                        pool.wait_ge(xT0, pr + 1)
                    for a in range(2):
                        last = nc.gpsimd.tensor_tensor(
                            mlT[v % 2][:, a, :, :], mT[:, a, :, :],
                            con[:, C_LVL + v * P:C_LVL + (v + 1) * P].unsqueeze(1).broadcast_to([P, NT, P]), ALU.mult)
                    last.then_inc(ml_done, 1)
                    if v == 0:
                        pool.wait_ge(ml_done, 7 * pr + 1)
                        for a in range(2):
                            last = nc.gpsimd.tensor_tensor(invT[:, a, :, :], ident.unsqueeze(1).broadcast_to([P, NT, P]),
                                                           mlT[0][:, a, :, :], ALU.subtract)
                        last.then_inc(xT0, 1)
            pool.wait_ge(gao_ev, GDN_H)
            pool.wait_ge(hmid_st, 64)
            for t in range(NT):
                pool.dma_start(h[:, t, :], h_mid[t * P:(t + 1) * P, :]).then_inc(res_in, 16)
            layer_norm_params(2, io["ln_mix_g"][1, :], io["ln_mix_b"][1, :])
            moe(1)

        @block.tensor
        def _(pe):
            mm = nc.tensor.matmul

            def transposes(k):
                for t in range(NT):
                    if k == 0:
                        pe.wait_ge(x_in[t], 16)
                    else:
                        pe.wait_ge(h_ready, NT * (k - 1) + t + 1)
                    for g in range(2):
                        ge(pe, (tr_act, tr_dve)[g], NT * k + t)
                        for j in range(4):
                            d = 4 * g + j
                            last = nc.tensor.transpose(ps[6 + g][:, j * P:(j + 1) * P], h[:, t, d * P:(d + 1) * P], ident)
                        last.then_inc(tr_pe, 1)
                pe.wait_ge(tr_act, NT * (k + 1))
                pe.wait_ge(tr_dve, NT * (k + 1))

            def narrow(w, done):
                for t in range(NT):
                    for k in range(ND):
                        last = mm(ps[4][:, 16 * t:16 * t + 16], hT[:, k, t * P:(t + 1) * P], w[:, k, :], start=k == 0, stop=k == ND - 1)
                last.then_inc(done, 1)

            def out_projection(l):
                for t in range(NT):
                    for c in range(2):
                        s, n = (8 + c) % 3, ring_no(l, (8 + c) % 3) + (8 + c) // 3
                        if t == 0:
                            pe.wait_ge(ring_in[s], 16 * (n + 1))
                        j = 2 * t + c
                        ge(pe, mix_acc, 8 * l + j - 3 if l or j > 3 else 0)
                        for k in range(ND):
                            last = mm(ps[j % 4][:, :], aoT[:, k, t * P:(t + 1) * P], slot_k(s)[:, k, :], start=k == 0, stop=k == ND - 1)
                        last.then_inc(out_pe, 1)
                        if t == NT - 1:
                            pe.wait_ge(out_pe, 8 * l + j + 1)
                            pe.sem_inc(ring_free[s], 1)

            def x_transposes(x, v):
                for g, done in enumerate(("xTa_pe", "xTb_pe")):
                    for j in range(4):
                        d = 4 * g + j
                        last = nc.tensor.transpose(ps[4 + g][:, j * TB:(j + 1) * TB], x[0:TB, d * P:(d + 1) * P], ident[0:TB, 0:TB])
                    last.then_inc(v[done][0], 1)

            def gate_up(x_t, w_gate, w_up, v, n, alone=False):
                after(pe, v, "xTa_ev", n)
                after(pe, v, "xTb_ev", n)
                if not alone:
                    after(pe, v, "hid_done", n - 1)
                for bank, w, done in ((0, w_gate, "gate_pe"), (1, w_up, "up_pe")):
                    for k in range(ND):
                        last = mm(ps[bank][0:TB, :], x_t[:, k * TB:(k + 1) * TB], w[:, k, :], start=k == 0, stop=k == ND - 1)
                    last.then_inc(v[done][0], 1)

            def hid_transposes(v, n):
                after(pe, v, "hid_done", n)
                for k in range(NFK):
                    last = nc.tensor.transpose(ps[6][:, k * TB:(k + 1) * TB], hid[0:TB, k * P:(k + 1) * P], ident[0:TB, 0:TB])
                last.then_inc(v["hidT_pe"][0], 1)

            def down(w_down, v, n, alone=False):
                after(pe, v, "hidT_ev", n)
                for c, (ev, done) in enumerate((("ya_ev", "ya_pe"), ("yb_ev", "yb_pe"))):
                    if not alone:
                        after(pe, v, ev, n - 1)
                    for k in range(NFK):
                        last = mm(ps[2 + c][0:TB, :], hidT[:, k * TB:(k + 1) * TB], w_down[:, k, c * WB:(c + 1) * WB], start=k == 0, stop=k == NFK - 1)
                    last.then_inc(v[done][0], 1)

            def moe(l):
                transposes(2 * l + 1)
                narrow(router_w, routing)
                pe.wait_ge(routing, ROUTE * l + OH_READY)
                for t in range(NT):
                    for j in range(t + 1):
                        mm(ps[5][:, 16 * t:16 * t + 16], upper_strict if j == t else ones, rkey[:, 16 * j:16 * j + 16], start=j == 0, stop=j == t)
                for j in range(NT):
                    last = mm(ps[5][:, 64:80], ones, rkey[:, 16 * j:16 * j + 16], start=j == 0, stop=j == NT - 1)
                last.then_inc(routing, 1)
                pe.wait_ge(routing, ROUTE * l + ADDR_READY)
                pe.wait_ge(xg_in[0], 16 * (8 * l + 1))
                x_transposes(xg[:, 0, :], ex)

                def expert(i, par, more=True):
                    n = NE * l + 2 * i + par
                    w = [slot_k(3 * par), slot_k(3 * par + 1), as3(slot(3 * par + 2), NFK)]
                    no = [expert_no(l, 3 * par + j) + i for j in range(3)]
                    pe.wait_ge(ring_in[3 * par], 16 * (no[0] + 1))
                    pe.wait_ge(ring_in[3 * par + 1], 16 * (no[1] + 1))
                    gate_up(xT[:, par, :], w[0], w[1], ex, n)
                    if more:
                        pe.wait_ge(xg_in[1 - par], 16 * (8 * l + i + par + 1))
                        x_transposes(xg[:, 1 - par, :], ex)
                    hid_transposes(ex, n)
                    pe.sem_inc(ring_free[3 * par], 1)
                    pe.sem_inc(ring_free[3 * par + 1], 1)
                    pe.wait_ge(ring_in[3 * par + 2], 16 * (no[2] + 1))
                    down(w[2], ex, n)
                    after(pe, ex, "yb_pe", n)
                    pe.sem_inc(ring_free[3 * par + 2], 1)

                expert(0, 0)
                expert(0, 1)
                with pe.Fori(1, NE // 2 - 1) as i:
                    expert(i, 0)
                    expert(i, 1)
                expert(NE // 2 - 1, 0)
                expert(NE // 2 - 1, 1, more=False)

                v = ov[l]
                more = pe.value_load(cnt_i[0:1, 0:1], min_val=0, max_val=SEQ)
                with pe.If(more > TB):
                    with pe.Fori(0, NE * (NB - 1)) as r:
                        after(pe, v, "x_in", r)
                        x_transposes(xg[:, 0, :], v)
                        after(pe, v, "w_in", r)
                        gate_up(xT[:, 0, :], over_w[0], over_w[1], v, r, alone=True)
                        hid_transposes(v, r)
                        down(over_w[2], v, r, alone=True)

            pe.wait_ge(con_in, 16)
            transposes(0)
            pe.wait_ge(par_in, 16 * N_PAR)
            nc.tensor.transpose(ps[5][:, 0:CONV * NCT], conv_raw, ident[0:CONV * NCT, 0:CONV * NCT]).then_inc(conv_pe, 1)
            narrow(w_f, fox_gates)

            def running_sums():
                pe.wait_ge(fox_gates, LF_READY)
                for t in range(NT):
                    for j in range(t + 1):
                        last = mm(ps[4][:, 64 + 16 * t:80 + 16 * t], upper if j == t else ones, lf[:, 16 * j:16 * j + 16], start=j == 0, stop=j == t)
                last.then_inc(fox_gates, 1)

            def sums_transposed():
                pe.wait_ge(convw_ready, 1)
                pe.wait_ge(fox_gates, C_READY)
                for t in range(NT):
                    last = nc.tensor.transpose(ps[5][0:FOX_H, t * P:(t + 1) * P], c_tok[:, 16 * t:16 * t + 16], ident)
                last.then_inc(fox_gates, 1)

            def head_transposes(n):
                pe.wait_ge(qn_done, n + 1)
                ge(pe, qT_ev, n - 1)
                for j in range(4):
                    last = nc.tensor.transpose(ps[2 + n % 2][:, j * P:(j + 1) * P], qn[:, n % 2, j * P:(j + 1) * P], ident)
                last.then_inc(qT_pe, 1)

            for b in range(8):
                s = b % 3
                pe.wait_ge(ring_in[s], 16 * (b // 3 + 1))
                for t in range(4):
                    n = 4 * b + t
                    if n < 18:
                        ge(pe, qn_done, n - 1)
                    elif n < 26:
                        pe.wait_ge(v_ev, n - 17)
                    else:
                        pe.wait_ge(og_exp, n - 25)
                    for k in range(ND):
                        if b < 6:
                            last = mm(ps[n % 2][:, :], hT[:, k, t * P:(t + 1) * P], slot_k(s)[:, k, :], start=k == 0, stop=k == ND - 1)
                        else:
                            last = mm(ps[n % 2][:, :], slot_k(s)[:, k, t * P:(t + 1) * P], hT[:, k, :], start=k == 0, stop=k == ND - 1)
                    last.then_inc(proj_pe, 1)
                    if 1 <= n <= 16:
                        head_transposes(n - 1)
                    if n == 4:
                        running_sums()
                    if n == 8:
                        sums_transposed()
                pe.wait_ge(proj_pe, 4 * b + 4)
                pe.sem_inc(ring_free[s], 1)

            pe.wait_ge(qT_ev, 16)
            pe.wait_ge(og_exp, 8)

            def scores(m):
                hd, i = m // NT, m % NT
                lo = FOX_DH * (hd % 2)
                ge(pe, s_sub, m - 2)
                mm(ps[m % 3][:, 0:(i + 1) * P], qkT[0][lo:lo + FOX_DH, hd // 2, i * P:(i + 1) * P],
                   qkT[1][lo:lo + FOX_DH, hd // 2, 0:(i + 1) * P], start=True, stop=True).then_inc(s_pe, 1)

            def prob_transposes(m):
                pe.wait_ge(p_ready, m + 1)
                ge(pe, pT_ev, m - 1)
                for j in range(m % NT + 1):
                    last = nc.tensor.transpose(ps[3 + m % 2][:, j * P:(j + 1) * P], s_buf[:, m % 3, j * P:(j + 1) * P], ident)
                last.then_inc(pT_pe, 1)

            def weighted_values(m):
                hd, i = m // NT, m % NT
                lo = FOX_DH * (hd % 2)
                pe.wait_ge(pT_ev, m + 1)
                if i == 0:
                    ge(pe, o_ev, hd // 2 - 1)
                for j in range(i + 1):
                    last = mm(ps[5 + hd // 2 % 2][lo:lo + FOX_DH, i * P:(i + 1) * P], v_tok[:, j, hd * FOX_DH:(hd + 1) * FOX_DH],
                              pT_buf[:, m % 2, j * P:(j + 1) * P], start=j == 0, stop=j == i)
                last.then_inc(pv_pe, 1)

            M = FOX_H * NT
            scores(0)
            scores(1)
            for m in range(M):
                if m + 2 < M:
                    scores(m + 2)
                prob_transposes(m)
                if m >= 1:
                    weighted_values(m - 1)
            weighted_values(M - 1)
            pe.wait_ge(o_ev, NPAIR)
            out_projection(0)
            moe(0)

            transposes(2)
            narrow(w_ab, gdn_gates)
            pe.wait_ge(gdn_gates, G_READY)
            mm(ps[4][:, 64:96], upper, g_t, start=True, stop=True).then_inc(gdn_gates, 1)
            pe.wait_ge(gdn_gates, GC_READY)
            nc.tensor.transpose(ps[5][0:NT * GDN_H, 0:P], gc_tok, ident).then_inc(gdn_gates, 1)

            def square_sums(ct):
                pe.wait_ge(sq2_done, ct + 1)
                ge(pe, rn_done, ct - 1)
                mm(ps[2 + ct % 2][:, :], ones, sq_l2[:, ct % 2, :], start=True, stop=True).then_inc(ss_pe, 1)

            for b in range(8):
                s, n = b % 3, ring_no(1, b % 3) + b // 3
                pe.wait_ge(ring_in[s], 16 * (n + 1))
                for t in range(4):
                    ct = 4 * b + t
                    if b < 6:
                        ge(pe, conv_done, ct - 1)
                        for k in range(ND):
                            last = mm(ps[ct % 2][:, :], slot_k(s)[:, k, t * P:(t + 1) * P], hT[:, k, :], start=k == 0, stop=k == ND - 1)
                        last.then_inc(cv_pe, 1)
                        if 1 <= ct <= 16:
                            square_sums(ct - 1)
                    else:
                        if ct < 26:
                            pe.wait_ge(conv_done, ct - 1)
                        else:
                            pe.wait_ge(ogg_ev, ct - 25)
                        for k in range(ND):
                            last = mm(ps[ct % 2][:, :], hT[:, k, t * P:(t + 1) * P], slot_k(s)[:, k, :], start=k == 0, stop=k == ND - 1)
                        last.then_inc(ogg_pe, 1)
                pe.wait_ge(cv_pe if b < 6 else ogg_pe, 4 * b + 4 if b < 6 else 4 * b - 20)
                pe.sem_inc(ring_free[s], 1)

            pe.wait_ge(l2_done, 16)
            pe.wait_ge(silu_done, NCT)
            pe.wait_ge(ogg_ev, 8)
            for pr in range(NHP):
                ge(pe, gao_ev, 2 * pr)
                for a in range(2):
                    for n in range(NT):
                        c = slice(n * P, (n + 1) * P)
                        mm(ps[a][:, c], kT[:, 2 * pr + a, c], kT[:, 2 * pr + a, c], start=True, stop=True)
                        last = mm(ps[2 + a][:, c], kT[:, 2 * pr + a, c], qT[:, 2 * pr + a, c], start=True, stop=True)
                last.then_inc(kk_pe, 1)
                for a in range(2):
                    for n in range(NT):
                        c = slice(n * P, (n + 1) * P)
                        nc.tensor.transpose(ps[4 + a][:, c], kT[:, 2 * pr + a, c], ident)
                        last = nc.tensor.transpose(ps[6 + a][:, c], vT[:, 2 * pr + a, c], ident)
                last.then_inc(kv_pe, 1)

                pe.wait_ge(mT_done, pr + 1)
                pe.wait_ge(att_done, pr + 1)
                pe.wait_ge(k_ev, pr + 1)
                for v in range(LEVELS):
                    pe.wait_ge(ml_done, 7 * pr + v + 1)
                    for a in range(2):
                        if v:
                            pe.wait_ge(X_ev, 12 * pr + 2 * (v - 1) + a + 1)
                        for n in range(NT):
                            last = mm(ps[a][:, n * P:(n + 1) * P], mlT[v % 2][:, a, n, :], inv[:, a, n, :] if v else ident, start=True, stop=True)
                        last.then_inc(T_pe, 1)
                    if v == 0:
                        continue
                    for a in range(2):
                        pe.wait_ge(T_ev, 12 * pr + 2 * (v - 1) + a + 1)
                        if v == 1:
                            pe.wait_ge(xT0, pr + 1)
                        else:
                            pe.wait_ge(XT_ev, 12 * pr + 2 * (v - 2) + a + 1)
                        for n in range(NT):
                            c = slice(n * P, (n + 1) * P)
                            if v < LEVELS - 1:
                                mm(ps[2 + a][:, c], invT[:, a, n, :], tmpT[:, a, n, :], start=True, stop=True)
                            last = mm(ps[4 + a][:, c], tmpT[:, a, n, :], invT[:, a, n, :], start=True, stop=True)
                        last.then_inc(U_pe, 1)

                pe.wait_ge(v_evg, pr + 1)
                pe.wait_ge(XT_ev, 12 * pr + 12)
                for n in range(NT):
                    for a in range(2):
                        if n:
                            pe.wait_ge(st_done, 6 * pr + 2 * (n - 1) + a + 1)
                            mm(ps[2 + a][:, 0:P], k_gate[:, a, n, :], st[:, a, :], start=True, stop=True).then_inc(R_pe, 1)
                            pe.wait_ge(o_cp, 8 * pr + 2 * (n - 1) + a + 1)
                            mm(ps[a][:, 0:P], q_dec[:, a, n, :], st[:, a, :], start=True, stop=False)
                    for a in range(2):
                        if n:
                            pe.wait_ge(r_done, 6 * pr + 2 * (n - 1) + a + 1)
                        mm(ps[4 + a][:, 0:P], invT[:, a, n, :], r_sb[:, a, :] if n else v_chunk[:, a, n, :], start=True, stop=True).then_inc(V_pe, 1)
                    for a in range(2):
                        pe.wait_ge(vn_done, 8 * pr + 2 * n + a + 1)
                        mm(ps[a][:, 0:P], attnT[:, a, n, :], vn_sb[:, a, :], start=n == 0, stop=True).then_inc(O_pe, 1)
                        if n < NT - 1:
                            mm(ps[6 + a][:, 0:P], k_tok[:, a, n, :], vn_sb[:, a, :], start=True, stop=True).then_inc(K_pe, 1)
                pe.wait_ge(on_done, pr + 1)
                for a in range(2):
                    for n in range(NT):
                        last = nc.tensor.transpose(ps[2 + a][:, n * P:(n + 1) * P], o_tok[:, a, n, :], ident)
                    last.then_inc(oT_pe, 1)
            pe.wait_ge(gao_ev, GDN_H)
            out_projection(1)
            moe(1)

        @block.scalar
        def _(act):
            fn = nc.scalar.activation
            link = linker(act, act_link)
            params = [
                (w_f, io["fox_w_in"][0, :, 4 * D:4 * D + FOX_H].rearrange("(k p) n -> p k n", p=P)),
                (conv_raw, io["gdn_conv_w"][0, :, :].rearrange("w (c p) -> (w c) p", p=P)),
                (as3(bf_bc, NT), io["fox_b_f"][0, :].unsqueeze(0).broadcast_to([NT, FOX_H]).partition_broadcast(P)),
                (gain[0:64, 0:1], io["fox_q_gain"][0, :].unsqueeze(1)),
                (gain[64:128, 0:1], io["fox_q_gain"][0, :].unsqueeze(1)),
                (gain[0:64, 1:2], io["fox_k_gain"][0, :].unsqueeze(1)),
                (gain[64:128, 1:2], io["fox_k_gain"][0, :].unsqueeze(1)),
                (w_ab, io["gdn_w_in"][0, :, 4 * D:4 * D + 2 * GDN_H].rearrange("(k p) n -> p k n", p=P)),
                (router_w, io["router_w"].rearrange("(k p) n -> p k n", p=P)),
                (as3(rb_bc, NT), io["router_b"].unsqueeze(0).broadcast_to([NT, NE]).partition_broadcast(P)),
                (as3(dt_bc, NT), io["gdn_dt_bias"][0, :].unsqueeze(0).broadcast_to([NT, GDN_H]).partition_broadcast(P)),
                (as3(al_bc, NT), io["gdn_a_log"][0, :].unsqueeze(0).broadcast_to([NT, GDN_H]).partition_broadcast(P)),
                (ng_col, io["gdn_norm_g"][0, :].unsqueeze(1)),
                (rowno_i, io["rows"]),
            ]
            assert len(params) == N_PAR
            for dst, src in params:
                act.dma_start(dst, src).then_inc(par_in, 16)
            act.wait_ge(con_in, 16)

            def transposes_out(k):
                for t in range(NT):
                    act.wait_ge(tr_pe, 8 * k + 2 * t + 1)
                    fn(hT[:, 0:4, t * P:(t + 1) * P], as3(ps[6][:, :], 4), ACT.Copy).then_inc(tr_act, 1)

            def inverse_root(dst, src, scale, eps, done):
                link(fn(dst, src, ACT.Ln, scale=scale, bias=eps))
                fn(dst, dst, ACT.Exp, scale=-0.5).then_inc(done, 1)

            def layer_norm(q):
                for t in range(NT):
                    n = NT * q + t
                    act.wait_ge(mean_ready, n + 1)
                    link(fn(ln_sq, h[:, t, :], ACT.Square, bias=neg_mean[:, t:t + 1], accum_out=ssq[:, t:t + 1]))
                    inverse_root(rstd[:, t:t + 1], ssq[:, t:t + 1], 1.0 / D, eps_ln, rstd_ready)

            def x_out(x_t, v, n):
                after(act, v, "xTa_pe", n)
                fn(x_t[:, 0:4 * TB], ps[4][:, 0:4 * TB], ACT.Copy).then_inc(v["xTa_ev"][0], 1)

            def silu_gate(v, n):
                after(act, v, "gate_pe", n)
                fn(sil[0:TB, :], ps[0][0:TB, :], ACT.Silu).then_inc(v["sil_done"][0], 1)

            def hid_out(v, n):
                after(act, v, "hidT_pe", n)
                fn(hidT[:, 0:NFK * TB], ps[6][:, 0:NFK * TB], ACT.Copy).then_inc(v["hidT_ev"][0], 1)

            def rows_out(y, v, n):
                after(act, v, "ya_pe", n)
                fn(y[0:TB, 0:WB], ps[2][0:TB, :], ACT.Copy).then_inc(v["ya_ev"][0], 1)

            def moe(l):
                transposes_out(2 * l + 1)
                act.wait_ge(routing, ROUTE * l + RT_SUB)
                fn(probs, probs, ACT.Exp).then_inc(routing, 1)
                x_out(xT[:, 0, :], ex, NE * l)

                def expert(i, par, more=True):
                    n = NE * l + 2 * i + par
                    after(act, ex, "hid_done", n - 1)
                    silu_gate(ex, n)
                    if more:
                        after(act, ex, "up_pe", n - 1)
                        x_out(xT[:, 1 - par, :], ex, n + 1)
                    after(act, ex, "yb_pe", n - 1)
                    hid_out(ex, n)
                    ge(act, y_st[par], 16 * (8 * l + i))
                    rows_out(y_sb[:, par, :], ex, n)

                expert(0, 0)
                expert(0, 1)
                with act.Fori(1, NE // 2 - 1) as i:
                    expert(i, 0)
                    expert(i, 1)
                expert(NE // 2 - 1, 0)
                expert(NE // 2 - 1, 1, more=False)
                for n in range(2):
                    act.wait_ge(y_st[n], 16 * 8 * (l + 1))
                v = ov[l]
                more = act.value_load(cnt_i[0:1, 0:1], min_val=0, max_val=SEQ)
                with act.If(more > TB):
                    with act.Fori(0, NE * (NB - 1)) as r:
                        x_out(xT[:, 0, :], v, r)
                        silu_gate(v, r)
                        hid_out(v, r)
                        rows_out(y_sb[:, 0, :], v, r)
                layer_norm(2 * l + 1)

            act.wait_ge(par_in, 16 * N_PAR)
            transposes_out(0)
            act.wait_ge(conv_pe, 1)
            fn(conv_w, ps[5][:, 0:CONV * NCT], ACT.Copy).then_inc(convw_ready, 1)

            def log_one_plus_exp(x, done):
                link(fn(x, x, ACT.Exp, scale=-1.0))
                fn(x, x, ACT.Ln, bias=one).then_inc(done, 1)

            act.wait_ge(fox_gates, F_ABS)
            log_one_plus_exp(f_e, fox_gates)

            def head_out(n):
                act.wait_ge(qT_pe, n + 1)
                which, b, t = n // 8, n // 4 % 2, n % 4
                if n == 0:
                    act.wait_ge(gain_ready, 1)
                fn(qkT[which][:, 4 * b:4 * b + 4, t * P:(t + 1) * P], as3(ps[2 + n % 2][:, :], 4), ACT.Copy,
                   scale=gain[:, which:which + 1]).then_inc(qT_ev, 1)

            for n in range(16):
                act.wait_ge(proj_pe, n + 1)
                ge(act, head_sum, n - 1)
                fn(sq[:, n % 2, :], ps[n % 2][:, :], ACT.Square).then_inc(sq_done, 1)
                act.wait_ge(head_sum, n + 1)
                ge(act, qn_done, n - 1)
                inverse_root(head_r[:, n % 2, :], head_ss[:, n % 2, :], 1.0 / FOX_DH, eps_rms, head_rs)
                if n:
                    head_out(n - 1)
                if n == 9:
                    act.wait_ge(fox_gates, CT_PE)
                    link(fn(cT, ps[5][0:FOX_H, :], ACT.Copy))
                    act.dma_start(c_rows, cT).then_inc(c_st, 16)
            for n in range(16, 24):
                act.wait_ge(proj_pe, n + 1)
                fn(v_tok[:, n % 4, (n // 4 - 4) * WB:(n // 4 - 3) * WB], ps[n % 2][:, :], ACT.Copy).then_inc(v_ev, 1)
                if n == 16:
                    head_out(15)
            act.wait_ge(c_st, 16)
            for m in range(8):
                act.wait_ge(proj_pe, 25 + m)
                fn(ogT[:, m, :], ps[m % 2][:, :], ACT.Exp, scale=-1.0).then_inc(og_exp, 1)

            M = FOX_H * NT

            def exps(m):
                cols_m = (m % NT + 1) * P
                act.wait_ge(max_done, m + 1)
                ge(act, p_ready, m - 2)
                s = s_buf[:, m % 3, 0:cols_m]
                fn(s, s, ACT.Exp, bias=neg_max[:, m % 3:m % 3 + 1], accum_out=row_sum[:, m % 3:m % 3 + 1]).then_inc(p_exp, 1)

            def probs_out(m):
                cols_m = (m % NT + 1) * P
                act.wait_ge(pT_pe, m + 1)
                ge(act, pv_pe, m - 1)
                fn(pT_buf[:, m % 2, 0:cols_m], ps[3 + m % 2][:, 0:cols_m], ACT.Copy).then_inc(pT_ev, 1)

            exps(0)
            for m in range(M):
                if m + 1 < M:
                    exps(m + 1)
                probs_out(m)
            layer_norm(0)
            moe(0)

            transposes_out(2)
            act.wait_ge(gdn_gates, AB_PE)
            logits = as3(ps[4][:, 0:NT * 16], NT)
            fn(as3(beta, NT), logits[:, :, 0:GDN_H], ACT.Exp, scale=-1.0).then_inc(gdn_gates, 1)
            link(fn(al_bc, al_bc, ACT.Exp))
            act.wait_ge(gdn_gates, G_ABS)
            log_one_plus_exp(g_e, gdn_gates)
            act.wait_ge(gdn_gates, GT_PE)
            link(fn(gT_sb, ps[5][0:NT * GDN_H, 0:P], ACT.Copy))
            act.dma_start(g_rows, gT_sb).then_inc(g_st, 16)

            def l2_roots(ct):
                act.wait_ge(ss_pe, ct + 1)
                ge(act, l2_done, ct - 1)
                inverse_root(r_l2[:, ct % 2, :], ps[2 + ct % 2][:, :], 1.0, eps_l2, rn_done)

            act.wait_ge(hmid_st, 64)
            for ct in range(NCT):
                act.wait_ge(conv_done, ct + 1)
                dst = qkvT[ct // 8][:, ct % 8, :]
                fn(dst, conv_tmp[:, ct % 2, :], ACT.Silu).then_inc(silu_done, 1)
                if ct < 16:
                    act.wait_ge(silu_done, ct + 1)
                    ge(act, ss_pe, ct - 1)
                    fn(sq_l2[:, ct % 2, :], dst, ACT.Square).then_inc(sq2_done, 1)
                if 1 <= ct <= 16:
                    l2_roots(ct - 1)
            for n in range(8):
                act.wait_ge(ogg_pe, n + 1)
                fn(og_tok[:, n % 4, (n // 4) * WB:(n // 4 + 1) * WB], ps[n % 2][:, :], ACT.Silu).then_inc(ogg_ev, 1)

            for pr in range(NHP):
                act.wait_ge(gbc_in, 32 * (pr + 1))
                fn(g_exp, g_bc, ACT.Exp).then_inc(gexp_done, 1)
                act.wait_ge(dec_arg, pr + 1)
                fn(dec, dec, ACT.Exp).then_inc(dec_done, 1)
                act.wait_ge(kd_arg, pr + 1)
                fn(as3(egl, 2), g_bc[:, :, :, P - 1], ACT.Exp)
                link(fn(kd, kd, ACT.Exp))
                act.wait_ge(kv_pe, pr + 1)
                for a in range(2):
                    for n in range(NT):
                        last = fn(k_tok[:, a, n, :], ps[4 + a][:, n * P:(n + 1) * P], ACT.Copy, scale=kd[:, NT * a + n:NT * a + n + 1])
                last.then_inc(k_ev, 1)
                for a in range(2):
                    last = fn(v_chunk[:, a, :, :], as3(ps[6 + a][:, :], NT), ACT.Copy)
                last.then_inc(v_evg, 1)
                for v in range(1, LEVELS):
                    for a in range(2):
                        act.wait_ge(T_pe, 14 * pr + 2 * v + a + 1)
                        fn(tmpT[:, a, :, :], as3(ps[a][:, :], NT), ACT.Copy).then_inc(T_ev, 1)
                for n in range(NT):
                    for a in range(2):
                        act.wait_ge(V_pe, 8 * pr + 2 * n + a + 1)
                        hd = n * GDN_H + 2 * pr + a
                        fn(vn_sb[:, a, :], ps[4 + a][:, 0:P], ACT.Copy, scale=beta[:, hd:hd + 1]).then_inc(vn_done, 1)
                    for a in range(2):
                        act.wait_ge(O_pe, 8 * pr + 2 * n + a + 1)
                        fn(o_tok[:, a, n, :], ps[a][:, 0:P], ACT.Copy).then_inc(o_cp, 1)
                act.wait_ge(o_cp, 8 * (pr + 1))
                for a in range(2):
                    for n in range(NT):
                        c = NT * a + n
                        last = fn(tmpT[:, a, n, :], o_tok[:, a, n, :], ACT.Square, accum_out=o_ss[:, c:c + 1])
                link(last)
                inverse_root(o_r, o_ss, 1.0 / P, eps_rms, or_done)
                for a in range(2):
                    act.wait_ge(oT_pe, 2 * pr + a + 1)
                    fn(aoT[:, 2 * pr + a, :], ps[2 + a][:, :], ACT.Copy, scale=ng_col).then_inc(gao_ev, 1)
            layer_norm(2)
            moe(1)

        @block.vector
        def _(dve):
            tt, ts, stt = nc.vector.tensor_tensor, nc.vector.tensor_scalar, nc.vector.scalar_tensor_tensor
            red = nc.vector.tensor_reduce
            link = linker(dve, dve_link)

            def transposes_out(k):
                for t in range(NT):
                    dve.wait_ge(tr_pe, 8 * k + 2 * t + 2)
                    nc.vector.tensor_copy(hT[:, 4:8, t * P:(t + 1) * P], as3(ps[7][:, :], 4)).then_inc(tr_dve, 1)

            def mean(t):
                ts(neg_mean[:, t:t + 1], sum2[:, 2 * t:2 * t + 1], sum2[:, 2 * t + 1:2 * t + 2], -1.0 / D,
                   ALU.add, ALU.mult).then_inc(mean_ready, 1)

            def normalise(q, t):
                dve.wait_ge(rstd_ready, NT * q + t + 1)
                dve.wait_ge(ln_in, 32 * (q + 1))
                link(ts(h[:, t, :], h[:, t, :], neg_mean[:, t:t + 1], rstd[:, t:t + 1], ALU.add, ALU.mult))
                link(tt(h[:, t, :], h[:, t, :], ln_g, ALU.mult))
                tt(h[:, t, :], h[:, t, :], ln_b, ALU.add).then_inc(h_ready, 1)

            def mixer_norm(l):
                dve.wait_ge(res_in, 64 * (l + 1))
                for t in range(NT):
                    for c in range(2):
                        dve.wait_ge(out_pe, 8 * l + 2 * t + c + 1)
                        hc = h[:, t, c * WB:(c + 1) * WB]
                        stt(hc, hc, ALPHA, ps[(2 * t + c) % 4][:, :], ALU.mult, ALU.add,
                            accum_out=sum2[:, 2 * t + c:2 * t + c + 1]).then_inc(mix_acc, 1)
                    dve.wait_ge(mix_acc, 8 * l + 2 * t + 2)
                    mean(t)
                    if t:
                        normalise(2 * l, t - 1)
                normalise(2 * l, NT - 1)

            def router(l):
                def grp(x):
                    return as3(x, NT * NG)

                def tok(x):
                    return as3(x, NT)

                def bc(x, n):
                    return x.unsqueeze(2).broadcast_to([P, x.shape[1], n])

                dve.wait_ge(routing, ROUTE * l + RT_PE)
                link(red(rmx, tok(ps[4][:, 0:64]), X, ALU.max))
                tt(tok(probs), tok(ps[4][:, 0:64]), bc(rmx, NE), ALU.subtract).then_inc(routing, 1)
                dve.wait_ge(routing, ROUTE * l + RT_EXP)
                link(red(rsm, tok(probs), X, ALU.add))
                link(nc.vector.reciprocal(rsm, rsm))
                link(tt(tok(probs), tok(probs), bc(rsm, NE), ALU.mult))
                link(tt(selv, probs, rb_bc, ALU.add))
                s = [grp(selv)[:, :, k] for k in range(EPG)]
                link(tt(gr[0], s[0], s[1], ALU.max))
                link(tt(gr[1], s[0], s[1], ALU.min))
                link(tt(gr[2], s[2], s[3], ALU.max))
                link(tt(gr[3], s[2], s[3], ALU.min))
                link(tt(gr[4], gr[0], gr[2], ALU.max))
                link(tt(gr[0], gr[0], gr[2], ALU.min))
                link(tt(gr[1], gr[1], gr[3], ALU.max))
                link(tt(gr[0], gr[0], gr[1], ALU.max))
                link(tt(gr[0], gr[0], gr[4], ALU.add))

                def first_best(oh, val, key, weight, n):
                    link(red(rmx, tok(val), X, ALU.max))
                    link(tt(tok(key), tok(val), bc(rmx, n), ALU.is_equal))
                    link(tt(key, key, weight, ALU.mult))
                    link(red(rmx, tok(key), X, ALU.max))
                    link(tt(tok(oh), tok(key), bc(rmx, n), ALU.is_equal))

                first_best(gr[1], gr[0], gr[2], con[:, C_GW:C_EW], NG)
                link(ts(gr[1], gr[1], 1.0, BIG, ALU.subtract, ALU.mult))
                link(tt(grp(selv), grp(selv), bc(gr[1], EPG), ALU.add))
                first_best(oh0, selv, rkey, con[:, C_EW:C_EI], NE)
                link(stt(selv, oh0, -BIG, selv, ALU.mult, ALU.add))
                first_best(oh1, selv, rkey, con[:, C_EW:C_EI], NE)
                tt(rkey, oh0, oh1, ALU.add).then_inc(routing, 1)
                for a, oh in enumerate((oh0, oh1)):
                    link(tt(rtmp, probs, oh, ALU.mult))
                    link(red(gate[a], tok(rtmp), X, ALU.add))
                link(tt(gsum, gate[0], gate[1], ALU.add))
                link(nc.vector.reciprocal(gsum, gsum))
                for a in range(2):
                    link(tt(gate[a], gate[a], gsum, ALU.mult))
                dve.wait_ge(routing, ROUTE * l + POS_PE)
                for a, oh in enumerate((oh0, oh1)):
                    link(tt(rtmp, ps[5][:, 0:64], oh, ALU.mult))
                    link(red(pos, tok(rtmp), X, ALU.add))
                    link(tt(rtmp, con[:, C_EI:C_EPS], oh, ALU.mult))
                    link(red(exp_n, tok(rtmp), X, ALU.add))
                    link(ts(blk, pos, float(TB), None, ALU.is_ge))
                    for k in range(2, NB):
                        link(stt(blk, pos, float(k * TB), blk, ALU.is_ge, ALU.add))
                    link(stt(exp_n, exp_n, float(NB), blk, ALU.mult, ALU.add))
                    link(stt(pos, blk, -float(TB), pos, ALU.mult, ALU.add))
                    by_a = addr_i.rearrange("p (t a) -> p t a", a=2)[:, :, a]
                    link(stt(by_a, pos, float(NE * NB), exp_n, ALU.mult, ALU.add))
                link(red(cmax, ps[5][:, 64:80], X, ALU.max))
                nc.vector.tensor_copy(cnt_i, cmax).then_inc(routing, 1)

            def x_out(x_t, v, n):
                after(dve, v, "xTb_pe", n)
                nc.vector.tensor_copy(x_t[:, 4 * TB:8 * TB], ps[5][:, 0:4 * TB]).then_inc(v["xTb_ev"][0], 1)

            def hidden(v, n):
                after(dve, v, "sil_done", n)
                after(dve, v, "up_pe", n)
                tt(hid[0:TB, :], ps[1][0:TB, :], sil[0:TB, :], ALU.mult).then_inc(v["hid_done"][0], 1)

            def rows_out(y, v, n):
                after(dve, v, "yb_pe", n)
                nc.vector.tensor_copy(y[0:TB, WB:2 * WB], ps[3][0:TB, :]).then_inc(v["yb_ev"][0], 1)

            def moe(l):
                transposes_out(2 * l + 1)
                router(l)
                x_out(xT[:, 0, :], ex, NE * l)

                def expert(i, par, more=True):
                    n = NE * l + 2 * i + par
                    after(dve, ex, "hidT_pe", n - 1)
                    hidden(ex, n)
                    if more:
                        after(dve, ex, "up_pe", n - 1)
                        x_out(xT[:, 1 - par, :], ex, n + 1)
                    ge(dve, y_st[par], 16 * (8 * l + i))
                    rows_out(y_sb[:, par, :], ex, n)

                expert(0, 0)
                expert(0, 1)
                with dve.Fori(1, NE // 2 - 1) as i:
                    expert(i, 0)
                    expert(i, 1)
                expert(NE // 2 - 1, 0)
                expert(NE // 2 - 1, 1, more=False)
                for n in range(2):
                    dve.wait_ge(y_st[n], 16 * 8 * (l + 1))
                v = ov[l]
                more = dve.value_load(cnt_i[0:1, 0:1], min_val=0, max_val=SEQ)
                with dve.If(more > TB):
                    with dve.Fori(0, NE * (NB - 1)) as r:
                        x_out(xT[:, 0, :], v, r)
                        hidden(v, r)
                        rows_out(y_sb[:, 0, :], v, r)
                q = 2 * l + 1
                for t in range(NT):
                    dve.wait_ge(yg_in[t % 2], 32 * (2 * l + t // 2 + 1))
                    y0, y1 = y_got[:, 2 * (t % 2), :], y_got[:, 2 * (t % 2) + 1, :]
                    link(ts(y0, y0, gate[0][:, t:t + 1], None, ALU.mult))
                    link(stt(h[:, t, :], h[:, t, :], ALPHA, y0, ALU.mult, ALU.add))
                    stt(h[:, t, :], y1, gate[1][:, t:t + 1], h[:, t, :], ALU.mult, ALU.add,
                        accum_out=sum2[:, 2 * t:2 * t + 1]).then_inc(comb_done, 1)
                    dve.wait_ge(comb_done, NT * l + t + 1)
                    link(ts(neg_mean[:, t:t + 1], sum2[:, 2 * t:2 * t + 1], -1.0 / D, None, ALU.mult))
                    nc.vector.tensor_copy(sum2[:, 2 * t + 1:2 * t + 2], neg_mean[:, t:t + 1]).then_inc(mean_ready, 1)
                    if t:
                        normalise(q, t - 1)
                normalise(q, NT - 1)

            dve.wait_ge(con_in, 16)
            dve.wait_ge(par_in, 16 * N_PAR)
            ts(gain[:, 0:1], gain[:, 0:1], FOX_DH ** -0.5, None, ALU.mult).then_inc(gain_ready, 1)
            transposes_out(0)

            dve.wait_ge(fox_gates, F_PE)
            link(tt(f_z, ps[4][:, 0:64], bf_bc, ALU.add))
            stt(f_e, f_z, -1.0, f_z, ALU.mult, ALU.max).then_inc(fox_gates, 1)
            dve.wait_ge(fox_gates, F_LN)
            stt(lf, f_z, 0.0, f_e, ALU.min, ALU.subtract).then_inc(fox_gates, 1)

            def bc64(x):
                return x.unsqueeze(2).broadcast_to([P, 8, FOX_DH])

            for n in range(16):
                dve.wait_ge(sq_done, n + 1)
                red(head_ss[:, n % 2, :], as3(sq[:, n % 2, :], 8), X, ALU.add).then_inc(head_sum, 1)
                if n == 6:
                    dve.wait_ge(fox_gates, CSUM_PE)
                    nc.vector.tensor_copy(c_tok, ps[4][:, 64:128]).then_inc(fox_gates, 1)
                dve.wait_ge(head_rs, n + 1)
                ge(dve, qT_pe, n - 1)
                tt(as3(qn[:, n % 2, :], 8), as3(ps[n % 2][:, :], 8), bc64(head_r[:, n % 2, :]), ALU.mult).then_inc(qn_done, 1)
            for m in range(8):
                dve.wait_ge(og_exp, m + 1)
                link(ts(ogT[:, m, :], ogT[:, m, :], 1.0, None, ALU.add))
                link(nc.vector.reciprocal(ogT[:, m, :], ogT[:, m, :]))

            M = FOX_H * NT

            def shifted(m):
                hd, i = m // NT, m % NT
                n = (i + 1) * P
                s = s_buf[:, m % 3, :]
                dve.wait_ge(s_pe, m + 1)
                if i == 0:
                    dve.wait_ge(c_in[hd % 3], 16 * (hd // 3 + 1))
                ge(dve, pT_pe, m - 2)
                stt(s[:, 0:n], ps[m % 3][:, 0:n], c_tok[:, 16 * i + hd:16 * i + hd + 1], c_buf[:, hd % 3, 0:n],
                    ALU.add, ALU.subtract).then_inc(s_sub, 1)
                dve.wait_ge(s_sub, m + 1)
                link(tt(s[:, n - P:n], s[:, n - P:n], causal, ALU.add))
                red(neg_max[:, m % 3:m % 3 + 1], s[:, 0:n], X, ALU.max, negate=True).then_inc(max_done, 1)

            def normalised(m):
                n = (m % NT + 1) * P
                dve.wait_ge(p_exp, m + 1)
                r = row_inv[:, m % 3:m % 3 + 1]
                link(nc.vector.reciprocal(r, row_sum[:, m % 3:m % 3 + 1]))
                s = s_buf[:, m % 3, 0:n]
                ts(s, s, r, None, ALU.mult).then_inc(p_ready, 1)

            def gated(pr):
                dve.wait_ge(pv_pe, 8 * (pr + 1))
                tt(aoT[:, pr, :], ps[5 + pr % 2][:, :], ogT[:, pr, :], ALU.mult).then_inc(o_ev, 1)

            shifted(0)
            for m in range(M):
                if m + 1 < M:
                    shifted(m + 1)
                normalised(m)
                if m % 8 == 1 and m > 8:
                    gated(m // 8 - 1)
            gated(NPAIR - 1)
            mixer_norm(0)
            moe(0)

            transposes_out(2)
            dve.wait_ge(gdn_gates, BETA_EXP)
            link(ts(beta, beta, 1.0, None, ALU.add))
            link(nc.vector.reciprocal(beta, beta))
            link(tt(as3(g_z, NT), as3(ps[4][:, 0:NT * 16], NT)[:, :, GDN_H:2 * GDN_H], as3(dt_bc, NT), ALU.add))
            stt(g_e, g_z, -1.0, g_z, ALU.mult, ALU.max).then_inc(gdn_gates, 1)
            dve.wait_ge(gdn_gates, G_EXP1)
            link(stt(g_t, g_z, 0.0, g_e, ALU.max, ALU.add))
            stt(g_t, g_t, -1.0, al_bc, ALU.mult, ALU.mult).then_inc(gdn_gates, 1)
            dve.wait_ge(gdn_gates, GC_PE)
            nc.vector.tensor_copy(gc_tok, ps[4][:, 64:96]).then_inc(gdn_gates, 1)

            def l2_apply(ct):
                dve.wait_ge(rn_done, ct + 1)
                x = qkvT[ct // 8][:, ct % 8, :]
                stt(x, r_l2[:, ct % 2, :], P ** -0.5 if ct < 8 else 1.0, x, ALU.mult, ALU.mult).then_inc(l2_done, 1)

            for ct in range(NCT):
                dve.wait_ge(cv_pe, ct + 1)
                ge(dve, silu_done, ct - 1)
                x, y = ps[ct % 2], conv_tmp[:, ct % 2, :]

                def tap(w):
                    return conv_w[:, w * NCT + ct:w * NCT + ct + 1]

                link(ts(y, x[:, :], tap(CONV - 1), None, ALU.mult))
                for d in range(1, CONV):
                    last = stt(y[:, d:SEQ], x[:, 0:SEQ - d], tap(CONV - 1 - d), y[:, d:SEQ], ALU.mult, ALU.add)
                    if d < CONV - 1:
                        link(last)
                last.then_inc(conv_done, 1)
                if 2 <= ct < 18:
                    l2_apply(ct - 2)

            for pr in range(NHP):
                dve.wait_ge(gbc_in, 32 * (pr + 1))
                for a in range(2):
                    for n in range(NT):
                        hd = n * GDN_H + 2 * pr + a
                        last = stt(dec[:, a, n, :], g_bc[:, a, n, :], gc_tok[:, hd:hd + 1], causal_t, ALU.subtract, ALU.add)
                last.then_inc(dec_arg, 1)
                tt(as3(kd, 2), g_bc[:, :, :, P - 1], gc_tok.rearrange("p (n a) -> p a n", a=GDN_H)[:, 2 * pr:2 * pr + 2, :],
                   ALU.subtract).then_inc(kd_arg, 1)
                dve.wait_ge(kk_pe, pr + 1)
                dve.wait_ge(dec_done, pr + 1)
                for a in range(2):
                    for n in range(NT):
                        hd = n * GDN_H + 2 * pr + a
                        last = stt(mT[:, a, n, :], ps[a][:, n * P:(n + 1) * P], beta[:, hd:hd + 1], dec[:, a, n, :], ALU.mult, ALU.mult)
                last.then_inc(mT_done, 1)
                for a in range(2):
                    last = tt(attnT[:, a, :, :], as3(ps[2 + a][:, :], NT), dec[:, a, :, :], ALU.mult)
                last.then_inc(att_done, 1)

                def with_gates():
                    dve.wait_ge(gexp_done, pr + 1)
                    for a in range(2):
                        tt(q_dec[:, a, :, :], as3(qT[:, 2 * pr + a, :], NT), g_exp[:, a, :, :], ALU.mult)
                        tt(k_gate[:, a, :, :], as3(kT[:, 2 * pr + a, :], NT), g_exp[:, a, :, :], ALU.mult)

                for a in range(2):
                    dve.wait_ge(T_pe, 14 * pr + a + 1)
                    tt(inv[:, a, :, :], ident.unsqueeze(1).broadcast_to([P, NT, P]), as3(ps[a][:, :], NT), ALU.subtract).then_inc(X_ev, 1)
                with_gates()
                dve.wait_ge(xT0, pr + 1)
                for v in range(1, LEVELS):
                    for a in range(2):
                        dve.wait_ge(U_pe, 12 * pr + 2 * (v - 1) + a + 1)
                        if v < LEVELS - 1:
                            tt(inv[:, a, :, :], inv[:, a, :, :], as3(ps[2 + a][:, :], NT), ALU.subtract).then_inc(X_ev, 1)
                        tt(invT[:, a, :, :], invT[:, a, :, :], as3(ps[4 + a][:, :], NT), ALU.subtract).then_inc(XT_ev, 1)
                for n in range(NT):
                    for a in range(2):
                        if n:
                            dve.wait_ge(R_pe, 6 * pr + 2 * (n - 1) + a + 1)
                            tt(r_sb[:, a, :], v_chunk[:, a, n, :], ps[2 + a][:, 0:P], ALU.subtract).then_inc(r_done, 1)
                    for a in range(2):
                        if n < NT - 1:
                            dve.wait_ge(K_pe, 6 * pr + 2 * n + a + 1)
                            if n == 0:
                                nc.vector.tensor_copy(st[:, a, :], ps[6 + a][:, 0:P]).then_inc(st_done, 1)
                            else:
                                stt(st[:, a, :], st[:, a, :], egl[:, NT * a + n:NT * a + n + 1], ps[6 + a][:, 0:P],
                                    ALU.mult, ALU.add).then_inc(st_done, 1)
                dve.wait_ge(or_done, pr + 1)
                for a in range(2):
                    for n in range(NT):
                        c, hd = NT * a + n, 2 * pr + a
                        last = stt(o_tok[:, a, n, :], o_tok[:, a, n, :], o_r[:, c:c + 1], og_tok[:, n, hd * P:(hd + 1) * P], ALU.mult, ALU.mult)
                last.then_inc(on_done, 1)
            mixer_norm(1)
            moe(1)


INPUTS = ("x", "ln_mix_g", "ln_mix_b", "ln_ffn_g", "ln_ffn_b", "router_w", "router_b", "fox_w_in", "fox_b_f",
          "fox_q_gain", "fox_k_gain", "fox_w_out", "gdn_w_in", "gdn_conv_w", "gdn_a_log", "gdn_dt_bias",
          "gdn_norm_g", "gdn_w_out", "moe_w_gate", "moe_w_up", "moe_w_down")


def kernel(**inputs):
    import concourse.bacc as bacc
    from concourse.bass_utils import run_bass_kernel_spmd

    nc = bacc.Bacc("TRN2", target_bir_lowering=False, num_devices=1)
    arrays = {name: np.ascontiguousarray(inputs[name]) for name in INPUTS}
    arrays["con"], arrays["rows"] = constants(), row_numbers()
    io = {name: nc.dram_tensor(f"in_{name}", a.shape, mybir.dt.from_np(a.dtype), kind="ExternalInput").ap()
          for name, a in arrays.items()}
    out = nc.dram_tensor("out", (1, SEQ, D), mybir.dt.float32, kind="ExternalOutput").ap()
    hybrid_trunk(nc, io, out)
    result = run_bass_kernel_spmd(nc, [{f"in_{name}": a for name, a in arrays.items()}], core_ids=[0])
    return result.results[0]["out"]
```

```python
import math
from contextlib import ExitStack

import numpy as np

import concourse.bass as bass
from concourse import mybir

D = 1024
SEQ = 512
P = 128
NT = SEQ // P
ND = D // P
WB = 512
FOX_H, FOX_DH = 16, 64
NPAIR = FOX_H // 2
GDN_H = 8
NHP = GDN_H // 2
CONV = 4
NCT = 3 * ND
NE, NG, EPG = 16, 4, 4
DF = D // 2
NFK = DF // P
TB = 128
NB = -(-SEQ // TB)
ALPHA = (2.0 * 2) ** 0.25
LN_EPS, RMS_EPS, L2_EPS = 1e-5, 1e-6, 1e-6
BIG = 1e30
EMPTY = 4 * SEQ
LEVELS = 7

C_ID, C_ONE, C_UP, C_UPS = 0, 128, 256, 384
C_CAUS, C_CAUST = 512, 640
C_LVL = 768
C_GW = C_LVL + LEVELS * P
C_EW = C_GW + NT * NG
C_EI = C_EW + NT * NE
C_EPS = C_EI + NT * NE
C_IOTA = C_EPS + 5
C_ROW = C_IOTA + P
C_TOT = C_ROW + 2 * NT
SMALL = 1800


def constants():
    c = np.zeros((P, C_TOT), np.float32)
    i, j = np.arange(P)[:, None], np.arange(P)[None, :]
    c[:, C_ID:C_ID + P] = i == j
    c[:, C_ONE:C_ONE + P] = 1.0
    c[:, C_UP:C_UP + P] = i <= j
    c[:, C_UPS:C_UPS + P] = i < j
    c[:, C_CAUS:C_CAUS + P] = np.where(j <= i, 0.0, -BIG)
    c[:, C_CAUST:C_CAUST + P] = np.where(i <= j, 0.0, -BIG)
    for v in range(LEVELS):
        b = 1 << v
        c[:, C_LVL + v * P:C_LVL + (v + 1) * P] = ((i >> v) % 2 == 0) & ((j >> v) == (i >> v) + 1)
    c[:, C_GW:C_EW] = np.tile(np.arange(NG, 0, -1), NT)
    c[:, C_EW:C_EI] = np.tile(np.arange(NE, 0, -1), NT)
    c[:, C_EI:C_EPS] = np.tile(np.arange(NE), NT)
    c[:, C_EPS:C_IOTA] = [LN_EPS, RMS_EPS, L2_EPS, 1.0, -0.5]
    c[:, C_IOTA:C_ROW] = j
    c[:, C_ROW:] = row_numbers() + 1
    return c


def row_numbers():
    t = np.arange(P)[:, None, None] + P * np.arange(NT)[None, :, None]
    return (2 * t + np.arange(2)[None, None, :]).reshape(P, 2 * NT).astype(np.int32)


def hybrid_trunk(nc, io, out):
    f32, f32r, i32 = mybir.dt.float32, mybir.dt.float32r, mybir.dt.int32
    ALU, ACT, X = mybir.AluOpType, mybir.ActivationFunctionType, mybir.AxisListType.X
    ctx = ExitStack()
    with ctx:
        def sb(name, cols, dt=f32, rows=P):
            return ctx.enter_context(nc.sbuf_tensor(name, [rows, cols], dt))

        def sem(name):
            return ctx.enter_context(nc.semaphore(name))

        def scratch(name, shape, dt=f32):
            return nc.dram_tensor(name, shape, dt, kind="Internal").ap()

        def as3(ap, n):
            return ap.rearrange("p (a b) -> p a b", a=n)

        def as4(ap, a, n):
            return ap.rearrange("p (a n c) -> p a n c", a=a, n=n)

        h_rows = [scratch(f"h_rows{l}", (SEQ, D)) for l in range(2)]
        h_mid = scratch("h_mid", (SEQ, D))
        y_rows = [scratch(f"y_rows{l}", (2 * SEQ, D)) for l in range(2)]
        tok_list = [scratch(f"tok_list{l}", (P * NE * NB, 1), i32) for l in range(2)]
        c_rows = scratch("c_rows", (FOX_H, SEQ))
        g_rows = scratch("g_rows", (NT * GDN_H, P))

        ring = [sb(f"ring{s}", 4096) for s in range(6)]
        ring_at = [nc.sbuf_base - 4 * 4096 * (6 - s) for s in range(6)]
        area = [sb(f"area{n}", 4096) for n in range(6)]
        area_at = [nc.sbuf_base - 4 * 4096 * (6 - n) for n in range(6)]
        con = sb("con", C_TOT)
        small = sb("small", SMALL)
        smalli = sb("smalli", 2 * NE * NB + 2 * 2 * NT + 3 + 2 * NE, i32)
        ps = [ctx.enter_context(nc.psum_tensor(f"ps{n}", [P, 512], f32)) for n in range(8)]

        sum_banks = (ps[2], ps[3], ps[6], ps[7])
        s_banks = (ps[0], ps[1], ps[2], ps[7])

        def slot(s):
            return ring[s][:, :]

        def slot_k(s):
            return as3(slot(s), ND)

        def split_part(name, cols, at):
            return nc.alloc_sbuf_tensor_at(name, [P, cols], f32r, offset=at)

        w_lo = [split_part(f"w_lo{s}", 4096, ring_at[s]) for s in range(6)]
        w_hi = [split_part(f"w_hi{s}", 4096, ring_at[3 + s]) for s in range(2)]
        hT_lo = as3(split_part("hT_lo", 4096, ring_at[5])[:, :], ND)
        hT_hi = as3(split_part("hT_hi", 4096, area_at[0])[:, :], ND)
        gates_hi = as3(split_part("gates_hi", ND * 16, area_at[5] + 4 * 3328)[:, :], ND)
        gates_lo = as3(split_part("gates_lo", ND * 16, area_at[5] + 4 * 3456)[:, :], ND)
        ex_hi = [split_part(f"ex_hi{j}", 4096, area_at[n]) for j, n in enumerate((4, 5, 0))]
        xT_hi, xT_lo = (split_part(f"xT_{n}", 8 * TB, area_at[2] + 4 * (2048 + 1024 * j)) for j, n in enumerate(("hi", "lo")))
        hidT_hi, hidT_lo = (split_part(f"hidT_{n}", NFK * TB, area_at[3] + 4 * (3072 + 512 * j)) for j, n in enumerate(("hi", "lo")))
        logits_T = area[5][0:16, 3584:4096]
        CHUNKS = 4
        AHEAD = ((0, 1), (2, 3), (), ())

        def hi_of(b):
            return as3(w_hi[b % 2][:, :], ND)

        def lo_of(b):
            return as3(w_lo[b % 3][:, :], ND)

        def chunk(c):
            return slice(c * ND // CHUNKS, (c + 1) * ND // CHUNKS)

        ident, ones = con[:, C_ID:C_ID + P], con[:, C_ONE:C_ONE + P]
        upper, upper_strict = con[:, C_UP:C_UP + P], con[:, C_UPS:C_UPS + P]
        causal, causal_t = con[:, C_CAUS:C_CAUS + P], con[:, C_CAUST:C_CAUST + P]
        eps_rms, eps_l2, one, minus_half = (con[:, C_EPS + n:C_EPS + n + 1] for n in range(1, 5))

        hT = as3(area[0][:, :], ND)
        h = as3(area[1][:, :], NT)
        aoT = hT
        ln_sq, ln_g, ln_b, ln_x = (area[5][:, 1024 * n:1024 * (n + 1)] for n in range(4))
        qkT = [as3(area[1][:, :], ND), as3(area[2][:, :], ND)]
        v_tok = as3(area[3][:, :], NT)
        ogT = as3(area[4][:, :], ND)
        cT = area[4][0:FOX_H, 0:SEQ]
        sq = as3(area[5][:, 0:1024], 2)
        qn = as3(area[5][:, 1024:2048], 2)
        s_buf = as3(area[5][:, 0:2048], 4)
        pT_buf = as3(area[5][:, 2048:3072], 2)
        c_buf = as3(area[5][:, 3072:4096], 2)
        xg = as3(area[2][:, 0:2048], 2)
        xT = area[2][:, 2048:3072]
        y_sb = as3(area[3][:, 0:2048], 2)
        sil, hid, hidT = (area[3][:, 2048 + 512 * n:2560 + 512 * n] for n in range(3))
        y_got = [as3(ring[3 + t // 2][:, :], 4)[:, 2 * (t % 2):2 * (t % 2) + 2, :] for t in range(NT)]
        pick = as3(area[3][:, 0:1024], 2 * NT)
        over_w = [as3(area[0][:, :], ND), as3(area[4][:, :], ND), as3(area[5][:, :], NFK)]
        qkvT = [as3(area[n][:, :], GDN_H) for n in (1, 2, 3)]
        qT, kT, vT = qkvT
        og_tok = as3(area[4][:, :], NT)
        conv_tmp = as3(area[5][:, 0:1024], 2)
        sq_l2 = as3(area[5][:, 1024:2048], 2)
        r_l2 = as3(area[5][:, 2048:3072], 2)
        conv_raw = area[5][0:CONV * NCT, 3072:3200]
        gT_sb = area[5][0:NT * GDN_H, 3200:3328]
        (inv, invT, tmpT, attnT, dec, q_dec, k_gate, k_tok, v_chunk, g_bc, mT, g_exp) = (
            as4(ring[3 + n // 4][:, n % 4 * 1024:(n % 4 + 1) * 1024], 2, NT) for n in range(12))
        mlT = [as4(area[5][:, 1024 * n:1024 * (n + 1)], 2, NT) for n in range(2)]
        o_tok = as4(area[5][:, 2048:3072], 2, NT)
        r_sb, vn_sb, st = (as3(area[5][:, 3072 + 256 * n:3328 + 256 * n], 2) for n in range(3))

        at = [0]

        def cols(n):
            at[0] += n
            assert at[0] <= SMALL
            return small[:, at[0] - n:at[0]]

        neg_mean, ssq, rstd, sum2 = cols(NT), cols(NT), cols(NT), cols(2 * NT)
        w_f, w_ab, router_w = (as3(cols(ND * 16), ND) for _ in range(3))
        conv_w = cols(CONV * NCT)
        bf_bc, gain, rb_bc = cols(NT * FOX_H), cols(2), cols(NT * NE)
        dt_bc, al_bc, ng_col = cols(NT * GDN_H), cols(NT * GDN_H), cols(1)
        lf, f_z, f_e, c_tok = (cols(NT * FOX_H) for _ in range(4))
        head_ss, head_r = as3(cols(16), 2), as3(cols(16), 2)
        neg_max, row_sum, row_inv = cols(4), cols(4), cols(4)
        probs, selv, oh0, oh1, rtmp, rkey = (cols(NT * NE) for _ in range(6))
        rmx, rsm = cols(NT), cols(NT)
        gr = [cols(NT * NG) for _ in range(8)]
        gate = [cols(NT), cols(NT)]
        gsum, exp_n, blk, cmax = cols(NT), cols(NT), cols(NT), cols(1)
        pos = [cols(NT), cols(NT)]
        row_f, empty_f = gr[2], gr[3]
        tok_f = cols(NE * NB)
        gc_tok, beta, g_z, g_e, g_t = (cols(NT * GDN_H) for _ in range(5))
        kd, egl, o_ss, o_r = (cols(8) for _ in range(4))
        i0 = 2 * NE * NB
        row_list, tok_of = smalli[:, 0:NE * NB], smalli[:, NE * NB:i0]
        addr_i, rowno_i = smalli[:, i0:i0 + 8], smalli[:, i0 + 8:i0 + 16]
        cnt_i, row_i, one_tok = (smalli[:, i0 + 16 + n:i0 + 17 + n] for n in range(3))
        first_row, first_tok = (smalli[:, i0 + 19 + NE * n:i0 + 19 + NE * (n + 1)] for n in range(2))

        con_in, fox_par_in, par_in = sem("con_in"), sem("fox_par_in"), sem("par_in")
        x_in = [sem(f"x_in{t}") for t in range(NT)]
        ring_in = [sem(f"ring_in{s}") for s in range(6)]
        ring_free = [sem(f"ring_free{s}") for s in range(6)]
        act_link, dve_link, pool_link = sem("act_link"), sem("dve_link"), sem("pool_link")
        tr_pe, tr_act, tr_dve = sem("tr_pe"), sem("tr_act"), sem("tr_dve")
        hT_hi_ev, hT_lo_ev = sem("hT_hi_ev"), sem("hT_lo_ev")
        w_hi_done, w_lo_done = sem("w_hi_done"), sem("w_lo_done")
        gain_ready, conv_pe, convw_ready = sem("gain_ready"), sem("conv_pe"), sem("convw_ready")
        fox_gates, gdn_gates, routing = sem("fox_gates"), sem("gdn_gates"), sem("routing")
        (F_PROD, F_COPIED, F_PE, F_ABS, F_LN, LF_READY, CSUM_PE, C_READY, CT_PE) = range(1, 10)
        (AB_PROD, AB_COPIED, AB_PE, BETA_EXP, G_ABS, G_EXP1, G_READY, GC_PE, GC_READY, GT_PE) = range(1, 11)
        (RT_PE, RT_SUB, RT_EXP, OH_READY, POS_PE, PICK_READY, LIST_PE, LIST_READY, ADDR_READY) = range(1, 10)
        ROUTE = 9
        c_st, g_st = sem("c_st"), sem("g_st")
        proj_pe, sq_done, head_sum, head_rs, qn_done, qT_pe, qT_ev, v_ev, og_exp, og_ready = (
            sem(n) for n in ("proj_pe", "sq_done", "head_sum", "head_rs", "qn_done", "qT_pe", "qT_ev", "v_ev", "og_exp", "og_ready"))
        c_in = [sem(f"c_in{n}") for n in range(2)]
        s_pe, s_sub, max_done, p_exp, p_ready, pT_pe, pT_ev, pv_pe, o_ev = (
            sem(n) for n in ("s_pe", "s_sub", "max_done", "p_exp", "p_ready", "pT_pe", "pT_ev", "pv_pe", "o_ev"))
        res_in, ln_in, out_pe, mix_acc = sem("res_in"), sem("ln_in"), sem("out_pe"), sem("mix_acc")
        mean_ready, ssq_ready, rstd_ready, h_ready = sem("mean_ready"), sem("ssq_ready"), sem("rstd_ready"), sem("h_ready")
        hrow_st, hmid_st, out_st = sem("hrow_st"), sem("hmid_st"), sem("out_st")
        list_zero = sem("list_zero")
        xg_in = [sem(f"xg_in{n}") for n in range(2)]
        y_st = [sem(f"y_st{n}") for n in range(2)]
        yg_in = [sem(f"yg_in{n}") for n in range(NT)]
        y_done, y0_gated, comb_done = sem("y_done"), sem("y0_gated"), sem("comb_done")
        EXPERT = ("gate_pe", "up_pe", "sil_done", "hid_done", "hidT_pe", "hidT_hi", "hidT_lo", "ya_pe", "yb_pe", "ya_ev", "yb_ev")
        ex = {n: (sem(n), 1, 1) for n in EXPERT}
        for n in ("pe", "hi", "lo"):
            both = sem(f"xT_{n}")
            ex |= {f"xT{half}_{n}": (both, 2, k + 1) for k, half in enumerate("ab")}
        hi_split, gu_lo_split, down_lo_split = sem("hi_split"), sem("gu_lo_split"), sem("down_lo_split")
        WCH = 4
        ov = []
        for l in range(2):
            steps = {"w_in": (sem(f"ov{l}_w_in"), 48, 48)}
            steps |= {n: (sem(f"ov{l}_{n}"), 16, 16) for n in ("x_in", "st")}
            steps["idx"] = (sem(f"ov{l}_idx"), 2, 4)
            steps["list"] = (sem(f"ov{l}_list"), 16, 16)
            for eng, names in (("pe", ("xTa_pe", "xTb_pe", "gate_pe", "up_pe", "hidT_pe", "ya_pe", "yb_pe")),
                               ("act", ("xTa_ev", "sil_done", "hidT_ev", "ya_ev")),
                               ("dve", ("xTb_ev", "hid_done", "yb_ev"))):
                done = sem(f"ov{l}_{eng}")
                steps |= {n: (done, len(names), k + 1) for k, n in enumerate(names)}
            ov.append(steps)
        cv_pe, conv_done, silu_done, sq2_done, ss_pe, rn_done, l2_done, ogg_pe, ogg_ev = (
            sem(n) for n in ("cv_pe", "conv_done", "silu_done", "sq2_done", "ss_pe", "rn_done", "l2_done", "ogg_pe", "ogg_ev"))
        gbc_in, kk_pe, dec_arg, dec_done, gexp_done, mT_done, att_done, kv_pe, kd_arg, k_ev, v_evg = (
            sem(n) for n in ("gbc_in", "kk_pe", "dec_arg", "dec_done", "gexp_done", "mT_done", "att_done", "kv_pe", "kd_arg", "k_ev", "v_evg"))
        ml_done, xT0, T_pe, T_ev, U_pe, X_ev, XT_ev = (
            sem(n) for n in ("ml_done", "xT0", "T_pe", "T_ev", "U_pe", "X_ev", "XT_ev"))
        R_pe, r_done, V_pe, vn_done, O_pe, K_pe, st_done, o_cp, or_done, on_done, oT_pe, gao_ev = (
            sem(n) for n in ("R_pe", "r_done", "V_pe", "vn_done", "O_pe", "K_pe", "st_done", "o_cp", "or_done", "on_done", "oT_pe", "gao_ev"))

        def ge(eng, s, v):
            if not isinstance(v, int) or v > 0:
                eng.wait_ge(s, v)

        def after(eng, v, step, n):
            s, per, first = v[step]
            ge(eng, s, n * per + first)

        def linker(eng, s):
            n = [0]

            def link(ins):
                n[0] += 1
                ins.then_inc(s, 1)
                eng.wait_ge(s, n[0])
            return link

        N_FOX_PAR, N_PAR = 7, 7
        MIX_LOADS = (4, 3, 3)

        def ring_no(l, s):
            return l * (8 + (MIX_LOADS[s] if s < 3 else 0))

        def expert_no(l, s):
            return ring_no(l, s) + (MIX_LOADS[s] if s < 3 else 0)

        block = ctx.enter_context(nc.Block())

        @block.sync
        def _(sp):
            sp.dma_start(con[:, :], io["con"]).then_inc(con_in, 16)
            for t in range(NT):
                sp.dma_start(h[:, t, :], io["x"][0, t * P:(t + 1) * P, :]).then_inc(x_in[t], 16)

            def mixer_block(l, b, w_in, w_out):
                s, n = b % 3, ring_no(l, b % 3) + b // 3
                ge(sp, ring_free[s], n)
                w = w_in[0, :, b * WB:(b + 1) * WB] if b < 8 else w_out[0, :, (b - 8) * WB:(b - 7) * WB]
                sp.dma_start(slot_k(s), w.rearrange("(k p) n -> p k n", p=P)).then_inc(ring_in[s], 16)

            def expert_load(l, e, i, par):
                for j, name in enumerate(("moe_w_gate", "moe_w_up", "moe_w_down")):
                    s = 3 * par + j
                    ge(sp, ring_free[s], expert_no(l, s) + i)
                    dst = slot_k(s) if j < 2 else as3(slot(s), NFK)
                    sp.dma_start(dst, io[name][l, e, :, :].rearrange("(k p) n -> p k n", p=P)).then_inc(ring_in[s], 16)

            for l, (w_in, w_out) in enumerate(((io["fox_w_in"], io["fox_w_out"]), (io["gdn_w_in"], io["gdn_w_out"]))):
                for b in range(3):
                    mixer_block(l, b, w_in, w_out)
                if l == 1:
                    for t in range(NT):
                        sp.wait_ge(h_ready, 8 * l - 4 + t + 1)
                        sp.dma_start(h_mid[t * P:(t + 1) * P, :], h[:, t, :]).then_inc(hmid_st, 16)
                for b in range(3, 10):
                    mixer_block(l, b, w_in, w_out)
                if l == 0:
                    sp.wait_ge(proj_pe, 32)
                    expert_load(0, 1, 0, 1)
                expert_load(l, 0, 0, 0)
                if l == 1:
                    sp.wait_ge(gao_ev, GDN_H)
                    expert_load(1, 1, 0, 1)
                for t in range(NT):
                    sp.wait_ge(h_ready, 8 * l + t + 1)
                    sp.dma_start(h_rows[l][t * P:(t + 1) * P, :], h[:, t, :]).then_inc(hrow_st, 16)
                with sp.Fori(1, NE // 2) as i:
                    for par in range(2):
                        expert_load(l, 2 * i + par, i, par)
                sp.wait_ge(y_done, l + 1)
                y_by_choice = y_rows[l].rearrange("(t a) d -> t a d", a=2)
                for t in range(NT):
                    for a in range(2):
                        sp.dma_start(y_got[t][:, a, :], y_by_choice[t * P:(t + 1) * P, a, :]).then_inc(yg_in[t], 16)
            for t in range(NT):
                sp.wait_ge(h_ready, 12 + t + 1)
                sp.dma_start(out[0, t * P:(t + 1) * P, :], h[:, t, :]).then_inc(out_st, 16)
            sp.wait_ge(out_st, 16 * NT)

        @block.gpsimd
        def _(pool):
            link = linker(pool, pool_link)
            link(nc.gpsimd.memset(row_list, EMPTY))
            for l in range(2):
                pool.dma_start(tok_list[l].rearrange("(p n) a -> p (n a)", p=P), row_list).then_inc(list_zero, 16)

            def layer_norm_params(q, g, b):
                pool.dma_start(ln_g, g.partition_broadcast(P)).then_inc(ln_in, 16)
                pool.dma_start(ln_b, b.partition_broadcast(P)).then_inc(ln_in, 16)

            def root_of_variance(q):
                for t in range(NT):
                    pool.wait_ge(ssq_ready, NT * q + t + 1)
                    link(nc.gpsimd.tensor_scalar(rstd[:, t:t + 1], ssq[:, t:t + 1], 1.0 / D, LN_EPS, ALU.mult, ALU.add))
                    nc.gpsimd.tensor_tensor(rstd[:, t:t + 1], rstd[:, t:t + 1], minus_half, ALU.pow).then_inc(rstd_ready, 1)

            def moe(l):
                def rows_in(dst, tokens, done):
                    nc.gpsimd.indirect_dma_start(
                        out=dst, out_offset=None, in_=h_rows[l], in_offset=bass.IndirectOffsetOnAxis(ap=tokens, axis=0),
                        bounds_check=SEQ - 1, oob_is_err=False).then_inc(done, 16)

                def rows_back(src, rows, done):
                    nc.gpsimd.indirect_dma_start(
                        out=y_rows[l], out_offset=bass.IndirectOffsetOnAxis(ap=rows, axis=0), in_=src, in_offset=None,
                        bounds_check=2 * SEQ - 1, oob_is_err=False).then_inc(done, 16)

                link(nc.gpsimd.memset(xg, 0.0))
                root_of_variance(2 * l)
                pool.wait_ge(routing, ROUTE * l + LIST_READY)
                pool.wait_ge(hrow_st, 64 * (l + 1))

                def gather(e):
                    if e >= 2:
                        after(pool, ex, "xTb_pe", NE * l + e - 2)
                    rows_in(xg[:, e % 2, :], first_tok[:, e:e + 1], xg_in[e % 2])

                gather(0)
                gather(1)
                for e in range(NE):
                    if e + 2 < NE:
                        gather(e + 2)
                    n = NE * l + e
                    for c in range(WCH):
                        pool.wait_ge(hi_split, WCH * (3 * n + 2) + c + 1)
                        s, part = 3 * (e % 2) + 2, slice(1024 * c, 1024 * (c + 1))
                        nc.gpsimd.tensor_tensor(w_lo[s][:, part], ring[s][:, part], ex_hi[2][:, part].bitcast(f32),
                                                ALU.subtract).then_inc(down_lo_split, 1)
                    after(pool, ex, "ya_ev", NE * l + e)
                    after(pool, ex, "yb_ev", NE * l + e)
                    rows_back(y_sb[:, e % 2, :], first_row[:, e:e + 1], y_st[e % 2])
                v = ov[l]
                for n in range(2):
                    pool.wait_ge(y_st[n], 16 * 8 * (l + 1))
                pool.wait_ge(routing, ROUTE * l + ADDR_READY)
                more = pool.value_load(cnt_i[0:1, 0:1], min_val=0, max_val=SEQ)
                with pool.If(more > TB):
                    pool.wait_ge(list_zero, 32)
                    for j in range(2 * NT):
                        nc.gpsimd.indirect_dma_start(
                            out=tok_list[l], out_offset=bass.IndirectOffsetOnAxis(ap=addr_i[:, j:j + 1], axis=0),
                            in_=rowno_i[:, j:j + 1], in_offset=None).then_inc(v["list"][0], 16)
                    pool.wait_ge(v["list"][0], 16 * 2 * NT)
                    pool.dma_start(row_list, tok_list[l].rearrange("(p n) a -> p (n a)", p=P)).then_inc(v["list"][0], 16)
                    pool.wait_ge(v["list"][0], 16 * (2 * NT + 1))
                    nc.gpsimd.tensor_scalar(tok_f, row_list, 0.5, -0.25, ALU.mult, ALU.add).then_inc(v["idx"][0], 1)
                    pool.wait_ge(v["idx"][0], 1)
                    nc.gpsimd.tensor_copy(tok_of, tok_f).then_inc(v["idx"][0], 1)
                    pool.wait_ge(v["idx"][0], 2)
                    with pool.Fori(0, NE) as e:
                        with pool.Fori(0, NB - 1) as b:
                            r = e * (NB - 1) + b
                            for dst, name in zip(over_w, ("moe_w_gate", "moe_w_up", "moe_w_down")):
                                pool.dma_start(dst, io[name][l, e, :, :].rearrange("(k p) n -> p k n", p=P)).then_inc(v["w_in"][0], 16)
                            nc.gpsimd.tensor_copy(one_tok, tok_of[:, bass.ds(e * NB + b + 1, 1)]).then_inc(v["idx"][0], 1)
                            nc.gpsimd.tensor_copy(row_i, row_list[:, bass.ds(e * NB + b + 1, 1)]).then_inc(v["idx"][0], 1)
                            after(pool, v, "idx", r)
                            pool.nop(nofuse=True)
                            rows_in(xg[:, 0, :], one_tok, v["x_in"][0])
                            after(pool, v, "yb_ev", r)
                            after(pool, v, "ya_ev", r)
                            pool.nop(nofuse=True)
                            rows_back(y_sb[:, 0, :], row_i, v["st"][0])
                            after(pool, v, "st", r)
                pool.sem_inc(y_done, 1)
                layer_norm_params(2 * l + 1, io["ln_ffn_g"][l, :], io["ln_ffn_b"][l, :])
                root_of_variance(2 * l + 1)

            def split_lo(l):
                for b in range(8):
                    for c in range(CHUNKS):
                        pool.wait_ge(w_hi_done, CHUNKS * (8 * l + b) + c + 1)
                        nc.gpsimd.tensor_tensor(lo_of(b)[:, chunk(c), :], slot_k(b % 3)[:, chunk(c), :],
                                                hi_of(b)[:, chunk(c), :].bitcast(f32), ALU.subtract).then_inc(w_lo_done, 1)

            split_lo(0)
            pool.wait_ge(c_st, 16)
            pool.wait_ge(qT_ev, 16)
            for hd in range(FOX_H):
                ge(pool, s_sub, NT * (hd - 1))
                pool.dma_start(c_buf[:, hd % 2, :], c_rows[hd, :].partition_broadcast(P)).then_inc(c_in[hd % 2], 16)
            pool.wait_ge(pv_pe, FOX_H * NT)
            for t in range(NT):
                pool.dma_start(h[:, t, :], io["x"][0, t * P:(t + 1) * P, :]).then_inc(res_in, 16)
            layer_norm_params(0, io["ln_mix_g"][0, :], io["ln_mix_b"][0, :])
            pool.wait_ge(par_in, 16 * N_PAR)
            moe(0)

            split_lo(1)
            pool.wait_ge(g_st, 16)
            pool.wait_ge(ogg_pe, 8)
            g_by_head = g_rows.rearrange("(n a) c -> a n c", a=GDN_H)
            for pr in range(NHP):
                ge(pool, gao_ev, 2 * pr)
                if pr == 0:
                    after(pool, ex, "yb_pe", NE - 1)
                for a in range(2):
                    pool.dma_start(g_bc[:, a, :, :], g_by_head[2 * pr + a, :, :].partition_broadcast(P)).then_inc(gbc_in, 16)
                pool.wait_ge(mT_done, pr + 1)
                for v in range(LEVELS):
                    ge(pool, T_pe, 14 * pr + 2 * (v - 1) if v >= 2 else 0)
                    if v == 2:
                        pool.wait_ge(xT0, pr + 1)
                    for a in range(2):
                        last = nc.gpsimd.tensor_tensor(
                            mlT[v % 2][:, a, :, :], mT[:, a, :, :],
                            con[:, C_LVL + v * P:C_LVL + (v + 1) * P].unsqueeze(1).broadcast_to([P, NT, P]), ALU.mult)
                    last.then_inc(ml_done, 1)
                    if v == 0:
                        pool.wait_ge(ml_done, 7 * pr + 1)
                        for a in range(2):
                            last = nc.gpsimd.tensor_tensor(invT[:, a, :, :], ident.unsqueeze(1).broadcast_to([P, NT, P]),
                                                           mlT[0][:, a, :, :], ALU.subtract)
                        last.then_inc(xT0, 1)
            pool.wait_ge(gao_ev, GDN_H)
            pool.wait_ge(hmid_st, 64)
            for t in range(NT):
                pool.dma_start(h[:, t, :], h_mid[t * P:(t + 1) * P, :]).then_inc(res_in, 16)
            layer_norm_params(2, io["ln_mix_g"][1, :], io["ln_mix_b"][1, :])
            moe(1)

        @block.tensor
        def _(pe):
            mm = nc.tensor.matmul

            def transpose_tile(k, t):
                if k == 0:
                    pe.wait_ge(x_in[t], 16)
                else:
                    pe.wait_ge(h_ready, NT * (k - 1) + t + 1)
                for g in range(2):
                    if k % 2:
                        ge(pe, (tr_act, tr_dve)[g], NT * (k // 2) + t)
                    else:
                        ge(pe, hT_lo_ev, 2 * (NT * (k // 2) + t - 1) + g + 1)
                    for j in range(4):
                        d = 4 * g + j
                        last = nc.tensor.transpose(ps[6 + g][:, j * P:(j + 1) * P], h[:, t, d * P:(d + 1) * P], ident)
                    last.then_inc(tr_pe, 1)

            def hT_ready(k, t):
                if k % 2:
                    pe.wait_ge(tr_act, NT * (k // 2) + t + 1)
                    pe.wait_ge(tr_dve, NT * (k // 2) + t + 1)
                else:
                    pe.wait_ge(hT_lo_ev, 2 * (NT * (k // 2) + t + 1))

            def router_tile(t):
                for k in range(ND):
                    last = mm(ps[4][:, 16 * t:16 * t + 16], hT[:, k, t * P:(t + 1) * P], router_w[:, k, :], start=k == 0, stop=k == ND - 1)
                return last

            def gate_logits(done):
                for part, (w, x) in enumerate(((gates_hi, hT_hi), (gates_hi, hT_lo), (gates_lo, hT_hi))):
                    for k in range(ND):
                        last = mm(ps[4][0:16, :], w[:, k, :], x[:, k, :], start=part == 0 and k == 0, stop=part == 2 and k == ND - 1)
                last.then_inc(done, 1)

            def gate_transposes(copied, done):
                pe.wait_ge(done, copied)
                for t in range(NT):
                    last = nc.tensor.transpose(ps[4][:, 16 * t:16 * t + 16], logits_T[:, t * P:(t + 1) * P], ident[0:16, 0:16])
                last.then_inc(done, 1)

            def transposes(k, narrow=None, done=None, first=0):
                for t in range(first, NT):
                    if t and narrow is not None:
                        hT_ready(k, t - 1)
                        narrow(t - 1)
                    transpose_tile(k, t)
                hT_ready(k, NT - 1)
                if narrow is not None:
                    narrow(NT - 1).then_inc(done, 1)

            def product(l, b, dst, t, channels):
                if t == 0:
                    pe.wait_ge(w_hi_done, CHUNKS * (8 * l + b + 1))
                for part, (x, w) in enumerate(((hT_hi, hi_of(b)), (hT_lo, hi_of(b)), (hT_hi, lo_of(b)))):
                    for k in range(ND):
                        if t == 0 and part == 2 and k % (ND // CHUNKS) == 0:
                            pe.wait_ge(w_lo_done, CHUNKS * (8 * l + b) + k // (ND // CHUNKS) + 1)
                        narrow, wide = (w, x) if channels else (x, w)
                        last = mm(dst, narrow[:, k, t * P:(t + 1) * P], wide[:, k, :],
                                  start=part == 0 and k == 0, stop=part == 2 and k == ND - 1)
                return last

            def out_projection(l):
                for t in range(NT):
                    if t >= 2:
                        if t == 3:
                            hT_ready(2 * l + 1, 0)
                            router_tile(0)
                        transpose_tile(2 * l + 1, t - 2)
                    for c in range(2):
                        s, n = (8 + c) % 3, ring_no(l, (8 + c) % 3) + (8 + c) // 3
                        if t == 0:
                            pe.wait_ge(ring_in[s], 16 * (n + 1))
                        j = 2 * t + c
                        ge(pe, mix_acc, 8 * l + j - 3 if l or j > 3 else 0)
                        for k in range(ND):
                            last = mm(ps[j % 4][:, :], aoT[:, k, t * P:(t + 1) * P], slot_k(s)[:, k, :], start=k == 0, stop=k == ND - 1)
                        last.then_inc(out_pe, 1)
                        if t == NT - 1:
                            pe.wait_ge(out_pe, 8 * l + j + 1)
                            pe.sem_inc(ring_free[s], 1)

            def x_transposes(x, v):
                for g, done in enumerate(("xTa_pe", "xTb_pe")):
                    for j in range(4):
                        d = 4 * g + j
                        last = nc.tensor.transpose(ps[4 + g][:, j * TB:(j + 1) * TB], x[0:TB, d * P:(d + 1) * P], ident[0:TB, 0:TB])
                    last.then_inc(v[done][0], 1)

            def gate_up_split(par, n):
                after(pe, ex, "xTb_lo", n)
                after(pe, ex, "hid_done", n - 1)
                for j, done in enumerate(("gate_pe", "up_pe")):
                    pe.wait_ge(hi_split, WCH * (3 * n + j + 1))
                    hi, lo = as3(ex_hi[j][:, :], ND), as3(w_lo[3 * par + j][:, :], ND)
                    for part, (x, w) in enumerate(((xT_hi, hi), (xT_lo, hi), (xT_hi, lo))):
                        if part == 2:
                            pe.wait_ge(gu_lo_split, WCH * (2 * n + j + 1))
                        for k in range(ND):
                            last = mm(ps[j][0:TB, :], x[:, k * TB:(k + 1) * TB], w[:, k, :],
                                      start=part == 0 and k == 0, stop=part == 2 and k == ND - 1)
                    last.then_inc(ex[done][0], 1)

            def down_split(par, n):
                after(pe, ex, "hidT_lo", n)
                pe.wait_ge(hi_split, WCH * (3 * n + 3))
                hi, lo = as3(ex_hi[2][:, :], NFK), as3(w_lo[3 * par + 2][:, :], NFK)
                for c, (ev, done) in enumerate((("ya_ev", "ya_pe"), ("yb_ev", "yb_pe"))):
                    after(pe, ex, ev, n - 1)
                    for part, (x, w) in enumerate(((hidT_hi, hi), (hidT_lo, hi), (hidT_hi, lo))):
                        if c == 0 and part == 2:
                            pe.wait_ge(down_lo_split, WCH * (n + 1))
                        for k in range(NFK):
                            last = mm(ps[2 + c][0:TB, :], x[:, k * TB:(k + 1) * TB], w[:, k, c * WB:(c + 1) * WB],
                                      start=part == 0 and k == 0, stop=part == 2 and k == NFK - 1)
                    last.then_inc(ex[done][0], 1)

            def hid_transposes(v, n):
                after(pe, v, "hid_done", n)
                for k in range(NFK):
                    last = nc.tensor.transpose(ps[6][:, k * TB:(k + 1) * TB], hid[0:TB, k * P:(k + 1) * P], ident[0:TB, 0:TB])
                last.then_inc(v["hidT_pe"][0], 1)

            def gate_up(x_t, w_gate, w_up, v, n):
                after(pe, v, "xTa_ev", n)
                after(pe, v, "xTb_ev", n)
                for bank, w, done in ((0, w_gate, "gate_pe"), (1, w_up, "up_pe")):
                    for k in range(ND):
                        last = mm(ps[bank][0:TB, :], x_t[:, k * TB:(k + 1) * TB], w[:, k, :], start=k == 0, stop=k == ND - 1)
                    last.then_inc(v[done][0], 1)

            def down(w_down, v, n):
                after(pe, v, "hidT_ev", n)
                for c, done in enumerate(("ya_pe", "yb_pe")):
                    for k in range(NFK):
                        last = mm(ps[2 + c][0:TB, :], hidT[:, k * TB:(k + 1) * TB], w_down[:, k, c * WB:(c + 1) * WB], start=k == 0, stop=k == NFK - 1)
                    last.then_inc(v[done][0], 1)

            def moe(l):
                transposes(2 * l + 1, router_tile, routing, first=NT - 2)
                pe.wait_ge(routing, ROUTE * l + OH_READY)
                mm(ps[5][:, 0:16], upper_strict, rkey[:, 0:16], start=True, stop=True)
                for j in range(NT):
                    last = mm(ps[5][:, 16 * (j + 1):80], ones, rkey[:, 16 * j:16 * (j + 1)].unsqueeze(1).broadcast_to([P, NT - j, NE]),
                       start=j == 0, stop=j == NT - 1)
                    if j == 0:
                        mm(ps[5][:, 16:64], upper_strict, rkey[:, 16:64], start=False, stop=False)
                last.then_inc(routing, 1)
                pe.wait_ge(routing, ROUTE * l + PICK_READY)
                for j in range(2 * NT):
                    last = mm(ps[5][:, 96:96 + NE], pick[:, j, :], (oh0, oh1)[j % 2][:, NE * (j // 2):NE * (j // 2 + 1)],
                              start=j == 0, stop=j == 2 * NT - 1)
                last.then_inc(routing, 1)
                pe.wait_ge(routing, ROUTE * l + ADDR_READY)
                pe.wait_ge(xg_in[0], 16 * (8 * l + 1))
                x_transposes(xg[:, 0, :], ex)

                def expert(i, par, more=True):
                    n = NE * l + 2 * i + par
                    gate_up_split(par, n)
                    if more:
                        pe.wait_ge(xg_in[1 - par], 16 * (8 * l + i + par + 1))
                        x_transposes(xg[:, 1 - par, :], ex)
                    hid_transposes(ex, n)
                    pe.sem_inc(ring_free[3 * par], 1)
                    pe.sem_inc(ring_free[3 * par + 1], 1)
                    down_split(par, n)
                    after(pe, ex, "yb_pe", n)
                    pe.sem_inc(ring_free[3 * par + 2], 1)

                expert(0, 0)
                expert(0, 1)
                with pe.Fori(1, NE // 2 - 1) as i:
                    expert(i, 0)
                    expert(i, 1)
                expert(NE // 2 - 1, 0)
                expert(NE // 2 - 1, 1, more=False)

                v = ov[l]
                more = pe.value_load(cnt_i[0:1, 0:1], min_val=0, max_val=SEQ)
                with pe.If(more > TB):
                    with pe.Fori(0, NE * (NB - 1)) as r:
                        after(pe, v, "x_in", r)
                        x_transposes(xg[:, 0, :], v)
                        after(pe, v, "w_in", r)
                        gate_up(xT, over_w[0], over_w[1], v, r)
                        hid_transposes(v, r)
                        down(over_w[2], v, r)

            pe.wait_ge(con_in, 16)
            transposes(0)

            def running_sums():
                pe.wait_ge(fox_gates, LF_READY)
                for t in range(NT):
                    for j in range(t + 1):
                        last = mm(ps[4][:, 64 + 16 * t:80 + 16 * t], upper if j == t else ones, lf[:, 16 * j:16 * j + 16], start=j == 0, stop=j == t)
                last.then_inc(fox_gates, 1)

            def sums_transposed():
                pe.wait_ge(convw_ready, 1)
                pe.wait_ge(fox_gates, C_READY)
                for t in range(NT):
                    last = nc.tensor.transpose(ps[5][0:FOX_H, t * P:(t + 1) * P], c_tok[:, 16 * t:16 * t + 16], ident)
                last.then_inc(fox_gates, 1)

            def head_transposes(n):
                pe.wait_ge(qn_done, n + 1)
                ge(pe, qT_ev, n - 1)
                for j in range(4):
                    last = nc.tensor.transpose(ps[2 + n % 2][:, j * P:(j + 1) * P], qn[:, n % 2, j * P:(j + 1) * P], ident)
                last.then_inc(qT_pe, 1)

            for b in range(8):
                s = b % 3
                for t in range(4):
                    n = 4 * b + t
                    if n < 18:
                        ge(pe, qn_done, n - 1)
                    elif n < 26:
                        pe.wait_ge(v_ev, n - 17)
                    else:
                        pe.wait_ge(og_exp, n - 25)
                    product(0, b, ps[n % 2][:, :], t, channels=b >= 6).then_inc(proj_pe, 1)
                    if 1 <= n <= 16:
                        head_transposes(n - 1)
                    if n == 3:
                        pe.wait_ge(fox_par_in, 16 * N_FOX_PAR)
                        nc.tensor.transpose(ps[5][:, 0:CONV * NCT], conv_raw, ident[0:CONV * NCT, 0:CONV * NCT]).then_inc(conv_pe, 1)
                        pe.wait_ge(gain_ready, 1)
                        gate_logits(fox_gates)
                    if n == 4:
                        gate_transposes(F_COPIED, fox_gates)
                    if n == 8:
                        running_sums()
                    if n == 11:
                        sums_transposed()
                pe.wait_ge(proj_pe, 4 * b + 4)
                pe.sem_inc(ring_free[s], 1)

            pe.wait_ge(qT_ev, 16)
            pe.wait_ge(og_exp, 8)

            def scores(m):
                hd, i = m // NT, m % NT
                lo = FOX_DH * (hd % 2)
                ge(pe, s_sub, m - 3)
                mm(s_banks[m % 4][:, 0:(i + 1) * P], qkT[0][lo:lo + FOX_DH, hd // 2, i * P:(i + 1) * P],
                   qkT[1][lo:lo + FOX_DH, hd // 2, 0:(i + 1) * P], start=True, stop=True).then_inc(s_pe, 1)

            def prob_transposes(m):
                pe.wait_ge(p_ready, m + 1)
                ge(pe, pT_ev, m - 1)
                for j in range(m % NT + 1):
                    last = nc.tensor.transpose(ps[3 + m % 2][:, j * P:(j + 1) * P], s_buf[:, m % 4, j * P:(j + 1) * P], ident)
                last.then_inc(pT_pe, 1)

            def weighted_values(m):
                hd, i = m // NT, m % NT
                lo = FOX_DH * (hd % 2)
                pe.wait_ge(pT_ev, m + 1)
                if i == 0:
                    ge(pe, o_ev, hd // 2 - 1)
                for j in range(i + 1):
                    last = mm(ps[5 + hd // 2 % 2][lo:lo + FOX_DH, i * P:(i + 1) * P], v_tok[:, j, hd * FOX_DH:(hd + 1) * FOX_DH],
                              pT_buf[:, m % 2, j * P:(j + 1) * P], start=j == 0, stop=j == i)
                last.then_inc(pv_pe, 1)

            M = FOX_H * NT
            for m in range(4):
                scores(m)
            for m in range(M):
                if m + 4 < M:
                    scores(m + 4)
                prob_transposes(m)
                if m >= 1:
                    weighted_values(m - 1)
            weighted_values(M - 1)
            pe.wait_ge(o_ev, NPAIR)
            pe.wait_ge(par_in, 16 * N_PAR)
            out_projection(0)
            moe(0)

            transposes(2)
            gate_logits(gdn_gates)

            def square_sums(ct):
                pe.wait_ge(sq2_done, ct + 1)
                ge(pe, rn_done, ct - 3)
                mm(sum_banks[ct % 4][:, :], ones, sq_l2[:, ct % 2, :], start=True, stop=True).then_inc(ss_pe, 1)

            for b in range(8):
                s = b % 3
                for t in range(4):
                    ct = 4 * b + t
                    if b < 6:
                        ge(pe, conv_done, ct - 1)
                        product(1, b, ps[ct % 2][:, :], t, channels=True).then_inc(cv_pe, 1)
                        if ct == 0:
                            gate_transposes(AB_COPIED, gdn_gates)
                        if ct == 2:
                            pe.wait_ge(gdn_gates, G_READY)
                            mm(ps[4][:, 64:96], upper, g_t, start=True, stop=True).then_inc(gdn_gates, 1)
                        if ct == 3:
                            pe.wait_ge(gdn_gates, GC_READY)
                            nc.tensor.transpose(ps[5][0:NT * GDN_H, 0:P], gc_tok, ident).then_inc(gdn_gates, 1)
                        if 1 <= ct <= 16:
                            square_sums(ct - 1)
                    else:
                        if ct < 26:
                            pe.wait_ge(conv_done, ct - 1)
                        else:
                            pe.wait_ge(ogg_ev, ct - 25)
                        product(1, b, ps[ct % 2][:, :], t, channels=False).then_inc(ogg_pe, 1)
                pe.wait_ge(cv_pe if b < 6 else ogg_pe, 4 * b + 4 if b < 6 else 4 * b - 20)
                pe.sem_inc(ring_free[s], 1)

            pe.wait_ge(l2_done, 16)
            pe.wait_ge(silu_done, NCT)
            pe.wait_ge(ogg_ev, 8)
            for pr in range(NHP):
                ge(pe, gao_ev, 2 * pr)
                for a in range(2):
                    for n in range(NT):
                        c = slice(n * P, (n + 1) * P)
                        mm(ps[a][:, c], kT[:, 2 * pr + a, c], kT[:, 2 * pr + a, c], start=True, stop=True)
                        last = mm(ps[2 + a][:, c], kT[:, 2 * pr + a, c], qT[:, 2 * pr + a, c], start=True, stop=True)
                last.then_inc(kk_pe, 1)
                for a in range(2):
                    for n in range(NT):
                        c = slice(n * P, (n + 1) * P)
                        nc.tensor.transpose(ps[4 + a][:, c], kT[:, 2 * pr + a, c], ident)
                        last = nc.tensor.transpose(ps[6 + a][:, c], vT[:, 2 * pr + a, c], ident)
                last.then_inc(kv_pe, 1)

                pe.wait_ge(mT_done, pr + 1)
                pe.wait_ge(att_done, pr + 1)
                pe.wait_ge(k_ev, pr + 1)
                for v in range(LEVELS):
                    pe.wait_ge(ml_done, 7 * pr + v + 1)
                    for a in range(2):
                        if v:
                            pe.wait_ge(X_ev, 12 * pr + 2 * (v - 1) + a + 1)
                        for n in range(NT):
                            last = mm(ps[a][:, n * P:(n + 1) * P], mlT[v % 2][:, a, n, :], inv[:, a, n, :] if v else ident, start=True, stop=True)
                        last.then_inc(T_pe, 1)
                    if v == 0:
                        continue
                    for a in range(2):
                        pe.wait_ge(T_ev, 12 * pr + 2 * (v - 1) + a + 1)
                        if v == 1:
                            pe.wait_ge(xT0, pr + 1)
                        else:
                            pe.wait_ge(XT_ev, 12 * pr + 2 * (v - 2) + a + 1)
                        for n in range(NT):
                            c = slice(n * P, (n + 1) * P)
                            if v < LEVELS - 1:
                                mm(ps[2 + a][:, c], invT[:, a, n, :], tmpT[:, a, n, :], start=True, stop=True)
                            last = mm(ps[4 + a][:, c], tmpT[:, a, n, :], invT[:, a, n, :], start=True, stop=True)
                        last.then_inc(U_pe, 1)

                pe.wait_ge(v_evg, pr + 1)
                pe.wait_ge(XT_ev, 12 * pr + 12)
                for n in range(NT):
                    for a in range(2):
                        if n:
                            pe.wait_ge(st_done, 6 * pr + 2 * (n - 1) + a + 1)
                            mm(ps[2 + a][:, 0:P], k_gate[:, a, n, :], st[:, a, :], start=True, stop=True).then_inc(R_pe, 1)
                            pe.wait_ge(o_cp, 8 * pr + 2 * (n - 1) + a + 1)
                            mm(ps[a][:, 0:P], q_dec[:, a, n, :], st[:, a, :], start=True, stop=False)
                    for a in range(2):
                        if n:
                            pe.wait_ge(r_done, 6 * pr + 2 * (n - 1) + a + 1)
                        mm(ps[4 + a][:, 0:P], invT[:, a, n, :], r_sb[:, a, :] if n else v_chunk[:, a, n, :], start=True, stop=True).then_inc(V_pe, 1)
                    for a in range(2):
                        pe.wait_ge(vn_done, 8 * pr + 2 * n + a + 1)
                        mm(ps[a][:, 0:P], attnT[:, a, n, :], vn_sb[:, a, :], start=n == 0, stop=True).then_inc(O_pe, 1)
                        if n < NT - 1:
                            mm(ps[6 + a][:, 0:P], k_tok[:, a, n, :], vn_sb[:, a, :], start=True, stop=True).then_inc(K_pe, 1)
                pe.wait_ge(on_done, pr + 1)
                for a in range(2):
                    for n in range(NT):
                        last = nc.tensor.transpose(ps[2 + a][:, n * P:(n + 1) * P], o_tok[:, a, n, :], ident)
                    last.then_inc(oT_pe, 1)
            pe.wait_ge(gao_ev, GDN_H)
            out_projection(1)
            moe(1)

        @block.scalar
        def _(act):
            fn = nc.scalar.activation
            link = linker(act, act_link)
            params = [
                (w_f, io["fox_w_in"][0, :, 4 * D:4 * D + FOX_H].rearrange("(k p) n -> p k n", p=P)),
                (conv_raw, io["gdn_conv_w"][0, :, :].rearrange("w (c p) -> (w c) p", p=P)),
                (as3(bf_bc, NT), io["fox_b_f"][0, :].unsqueeze(0).broadcast_to([NT, FOX_H]).partition_broadcast(P)),
                (gain[0:64, 0:1], io["fox_q_gain"][0, :].unsqueeze(1)),
                (gain[64:128, 0:1], io["fox_q_gain"][0, :].unsqueeze(1)),
                (gain[0:64, 1:2], io["fox_k_gain"][0, :].unsqueeze(1)),
                (gain[64:128, 1:2], io["fox_k_gain"][0, :].unsqueeze(1)),
            ]
            late_params = [
                (w_ab, io["gdn_w_in"][0, :, 4 * D:4 * D + 2 * GDN_H].rearrange("(k p) n -> p k n", p=P)),
                (router_w, io["router_w"].rearrange("(k p) n -> p k n", p=P)),
                (as3(rb_bc, NT), io["router_b"].unsqueeze(0).broadcast_to([NT, NE]).partition_broadcast(P)),
                (as3(dt_bc, NT), io["gdn_dt_bias"][0, :].unsqueeze(0).broadcast_to([NT, GDN_H]).partition_broadcast(P)),
                (as3(al_bc, NT), io["gdn_a_log"][0, :].unsqueeze(0).broadcast_to([NT, GDN_H]).partition_broadcast(P)),
                (ng_col, io["gdn_norm_g"][0, :].unsqueeze(1)),
                (rowno_i, io["rows"]),
            ]
            assert len(params) == N_FOX_PAR and len(late_params) == N_PAR
            for dst, src in params:
                act.dma_start(dst, src).then_inc(fox_par_in, 16)
            for dst, src in late_params:
                act.dma_start(dst, src).then_inc(par_in, 16)
            act.wait_ge(con_in, 16)

            def transposes_out(k, tiles=range(NT)):
                for t in tiles:
                    for g in range(1 if k % 2 else 2):
                        act.wait_ge(tr_pe, 8 * k + 2 * t + g + 1)
                        dst, done = (hT, tr_act) if k % 2 else (hT_hi, hT_hi_ev)
                        fn(dst[:, 4 * g:4 * g + 4, t * P:(t + 1) * P], as3(ps[6 + g][:, :], 4), ACT.Copy).then_inc(done, 1)

            def split_first(l, c):
                act.wait_ge(ring_in[0], 16 * (ring_no(l, 0) + 1))
                fn(hi_of(0)[:, chunk(c), :], slot_k(0)[:, chunk(c), :], ACT.Copy).then_inc(w_hi_done, 1)

            def inverse_root(dst, src, scale, eps, done):
                link(fn(dst, src, ACT.Ln, scale=scale, bias=eps))
                fn(dst, dst, ACT.Exp, scale=-0.5).then_inc(done, 1)

            def layer_norm(q):
                if q % 2:
                    weigh(q // 2, 0)
                for t in range(NT):
                    n = NT * q + t
                    if q % 2:
                        weigh(q // 2, t + 1)
                    act.wait_ge(mean_ready, n + 1)
                    ge(act, ssq_ready, n)
                    fn(ln_sq, h[:, t, :], ACT.Square, bias=neg_mean[:, t:t + 1], accum_out=ssq[:, t:t + 1]).then_inc(ssq_ready, 1)
                    if q % 2 == 0:
                        transposes_out(q + 1, range(max(t - 1, 0), t if t < NT - 1 else NT))
                    elif q == 1 and t >= 2:
                        transposes_out(2, (t - 2,))
                if q == 1:
                    act.wait_ge(comb_done, NT)
                    split_first(1, 0)
                    transposes_out(2, (NT - 2,))
                    split_first(1, 1)
                    transposes_out(2, (NT - 1,))
                    split_first(1, 2)
                    split_first(1, 3)

            def weigh(l, t):
                if t < NT:
                    act.wait_ge(yg_in[t], 32 * (l + 1))
                    fn(y_got[t][:, 0, :], y_got[t][:, 0, :], ACT.Copy, scale=gate[0][:, t:t + 1]).then_inc(y0_gated, 1)

            def x_out(x_t, v, n):
                after(act, v, "xTa_pe", n)
                fn(x_t[:, 0:4 * TB], ps[4][:, 0:4 * TB], ACT.Copy).then_inc(v["xTa_ev"][0], 1)

            def silu_gate(v, n):
                after(act, v, "gate_pe", n)
                fn(sil[0:TB, :], ps[0][0:TB, :], ACT.Silu).then_inc(v["sil_done"][0], 1)

            def hid_out(v, n):
                after(act, v, "hidT_pe", n)
                fn(hidT[:, 0:NFK * TB], ps[6][:, 0:NFK * TB], ACT.Copy).then_inc(v["hidT_ev"][0], 1)

            def rows_out(y, v, n):
                after(act, v, "ya_pe", n)
                fn(y[0:TB, 0:WB], ps[2][0:TB, :], ACT.Copy).then_inc(v["ya_ev"][0], 1)

            def moe(l):
                act.wait_ge(routing, ROUTE * l + RT_SUB)
                fn(probs, probs, ACT.Exp).then_inc(routing, 1)

                def split(j, i, par, n):
                    s = 3 * par + j
                    ge(act, ring_in[s], 16 * (expert_no(l, s) + i + 1))
                    after(act, ex, ("gate_pe", "up_pe", "yb_pe")[j], n - 1)
                    for c in range(WCH):
                        fn(ex_hi[j][:, 1024 * c:1024 * (c + 1)], slot(s)[:, 1024 * c:1024 * (c + 1)], ACT.Copy).then_inc(hi_split, 1)

                def x_hi(g, n):
                    after(act, ex, ("xTa_pe", "xTb_pe")[g], n)
                    fn(xT_hi[:, 4 * g * TB:4 * (g + 1) * TB], ps[4 + g][:, 0:4 * TB], ACT.Copy).then_inc(ex["xTa_hi"][0], 1)

                split(0, 0, 0, NE * l)
                x_hi(0, NE * l)
                x_hi(1, NE * l)
                split(1, 0, 0, NE * l)

                def expert(i, par, more=True):
                    n = NE * l + 2 * i + par
                    split(2, i, par, n)
                    after(act, ex, "hid_done", n - 1)
                    silu_gate(ex, n)
                    if more:
                        split(0, i + par, 1 - par, n + 1)
                        after(act, ex, "up_pe", n)
                        x_hi(0, n + 1)
                    after(act, ex, "yb_pe", n - 1)
                    after(act, ex, "hidT_pe", n)
                    fn(hidT_hi[:, :], ps[6][:, 0:NFK * TB], ACT.Copy).then_inc(ex["hidT_hi"][0], 1)
                    if more:
                        x_hi(1, n + 1)
                        split(1, i + par, 1 - par, n + 1)
                    ge(act, y_st[par], 16 * (8 * l + i))
                    rows_out(y_sb[:, par, :], ex, n)

                expert(0, 0)
                expert(0, 1)
                with act.Fori(1, NE // 2 - 1) as i:
                    expert(i, 0)
                    expert(i, 1)
                expert(NE // 2 - 1, 0)
                expert(NE // 2 - 1, 1, more=False)
                for n in range(2):
                    act.wait_ge(y_st[n], 16 * 8 * (l + 1))
                v = ov[l]
                more = act.value_load(cnt_i[0:1, 0:1], min_val=0, max_val=SEQ)
                with act.If(more > TB):
                    with act.Fori(0, NE * (NB - 1)) as r:
                        x_out(xT, v, r)
                        silu_gate(v, r)
                        hid_out(v, r)
                        rows_out(y_sb[:, 0, :], v, r)
                layer_norm(2 * l + 1)

            transposes_out(0)
            for c in range(CHUNKS):
                split_first(0, c)

            def logits_out(done, product):
                act.wait_ge(done, product)
                fn(logits_T, ps[4][0:16, :], ACT.Copy).then_inc(done, 1)

            def log_one_plus_exp(x, done):
                link(fn(x, x, ACT.Exp, scale=-1.0))
                fn(x, x, ACT.Ln, bias=one).then_inc(done, 1)

            def head_out(n):
                act.wait_ge(qT_pe, n + 1)
                which, b, t = n // 8, n // 4 % 2, n % 4
                if n == 0:
                    act.wait_ge(gain_ready, 1)
                fn(qkT[which][:, 4 * b:4 * b + 4, t * P:(t + 1) * P], as3(ps[2 + n % 2][:, :], 4), ACT.Copy,
                   scale=gain[:, which:which + 1]).then_inc(qT_ev, 1)

            for n in range(16):
                act.wait_ge(proj_pe, n + 1)
                ge(act, head_sum, n - 1)
                fn(sq[:, n % 2, :], ps[n % 2][:, :], ACT.Square).then_inc(sq_done, 1)
                act.wait_ge(head_sum, n + 1)
                ge(act, qn_done, n - 1)
                inverse_root(head_r[:, n % 2, :], head_ss[:, n % 2, :], 1.0 / FOX_DH, eps_rms, head_rs)
                if n:
                    head_out(n - 1)
                if n == 3:
                    act.wait_ge(conv_pe, 1)
                    fn(conv_w, ps[5][:, 0:CONV * NCT], ACT.Copy).then_inc(convw_ready, 1)
                    logits_out(fox_gates, F_PROD)
                if n == 5:
                    act.wait_ge(fox_gates, F_ABS)
                    log_one_plus_exp(f_e, fox_gates)
                if n == 12:
                    act.wait_ge(fox_gates, CT_PE)
                    link(fn(cT, ps[5][0:FOX_H, :], ACT.Copy))
                    act.dma_start(c_rows, cT).then_inc(c_st, 16)
            for n in range(16, 24):
                act.wait_ge(proj_pe, n + 1)
                fn(v_tok[:, n % 4, (n // 4 - 4) * WB:(n // 4 - 3) * WB], ps[n % 2][:, :], ACT.Copy).then_inc(v_ev, 1)
                if n == 16:
                    head_out(15)
            act.wait_ge(c_st, 16)
            for m in range(8):
                act.wait_ge(proj_pe, 25 + m)
                fn(ogT[:, m, :], ps[m % 2][:, :], ACT.Exp, scale=-1.0).then_inc(og_exp, 1)

            M = FOX_H * NT

            def exps(m):
                cols_m = (m % NT + 1) * P
                act.wait_ge(max_done, m + 1)
                ge(act, p_ready, m - 3)
                s = s_buf[:, m % 4, 0:cols_m]
                fn(s, s, ACT.Exp, bias=neg_max[:, m % 4:m % 4 + 1], accum_out=row_sum[:, m % 4:m % 4 + 1]).then_inc(p_exp, 1)

            def probs_out(m):
                cols_m = (m % NT + 1) * P
                act.wait_ge(pT_pe, m + 1)
                ge(act, pv_pe, m - 1)
                fn(pT_buf[:, m % 2, 0:cols_m], ps[3 + m % 2][:, 0:cols_m], ACT.Copy).then_inc(pT_ev, 1)

            exps(0)
            for m in range(M):
                if m + 1 < M:
                    exps(m + 1)
                probs_out(m)
            act.wait_ge(par_in, 16 * N_PAR)
            layer_norm(0)
            moe(0)

            logits_out(gdn_gates, AB_PROD)

            def gdn_gate_exps():
                act.wait_ge(gdn_gates, AB_PE)
                logits = as3(ps[4][:, 0:NT * 16], NT)
                fn(as3(beta, NT), logits[:, :, 0:GDN_H], ACT.Exp, scale=-1.0).then_inc(gdn_gates, 1)
                link(fn(al_bc, al_bc, ACT.Exp))
                act.wait_ge(gdn_gates, G_ABS)
                log_one_plus_exp(g_e, gdn_gates)

            def l2_roots(ct):
                ge(act, l2_done, ct)
                for j in range(2):
                    act.wait_ge(ss_pe, ct + j + 1)
                    last = fn(r_l2[:, j, :], sum_banks[(ct + j) % 4][:, :], ACT.Ln, bias=eps_l2)
                link(last)
                for j in range(2):
                    fn(r_l2[:, j, :], r_l2[:, j, :], ACT.Exp, scale=-0.5).then_inc(rn_done, 1)

            act.wait_ge(hmid_st, 64)
            for ct in range(NCT):
                act.wait_ge(conv_done, ct + 1)
                dst = qkvT[ct // 8][:, ct % 8, :]
                fn(dst, conv_tmp[:, ct % 2, :], ACT.Silu).then_inc(silu_done, 1)
                if ct < 16:
                    act.wait_ge(silu_done, ct + 1)
                    ge(act, ss_pe, ct - 1)
                    fn(sq_l2[:, ct % 2, :], dst, ACT.Square).then_inc(sq2_done, 1)
                if ct == 0:
                    gdn_gate_exps()
                if ct % 2 and 3 <= ct < 19:
                    l2_roots(ct - 3)
                if ct == 4:
                    act.wait_ge(gdn_gates, GT_PE)
                    link(fn(gT_sb, ps[5][0:NT * GDN_H, 0:P], ACT.Copy))
                    act.dma_start(g_rows, gT_sb).then_inc(g_st, 16)
            for n in range(8):
                act.wait_ge(ogg_pe, n + 1)
                fn(og_tok[:, n % 4, (n // 4) * WB:(n // 4 + 1) * WB], ps[n % 2][:, :], ACT.Silu).then_inc(ogg_ev, 1)

            for pr in range(NHP):
                act.wait_ge(gbc_in, 32 * (pr + 1))
                fn(g_exp, g_bc, ACT.Exp).then_inc(gexp_done, 1)
                act.wait_ge(dec_arg, pr + 1)
                fn(dec, dec, ACT.Exp).then_inc(dec_done, 1)
                act.wait_ge(kd_arg, pr + 1)
                fn(as3(egl, 2), g_bc[:, :, :, P - 1], ACT.Exp)
                link(fn(kd, kd, ACT.Exp))
                act.wait_ge(kv_pe, pr + 1)
                for a in range(2):
                    for n in range(NT):
                        last = fn(k_tok[:, a, n, :], ps[4 + a][:, n * P:(n + 1) * P], ACT.Copy, scale=kd[:, NT * a + n:NT * a + n + 1])
                last.then_inc(k_ev, 1)
                for a in range(2):
                    last = fn(v_chunk[:, a, :, :], as3(ps[6 + a][:, :], NT), ACT.Copy)
                last.then_inc(v_evg, 1)
                for v in range(1, LEVELS):
                    for a in range(2):
                        act.wait_ge(T_pe, 14 * pr + 2 * v + a + 1)
                        fn(tmpT[:, a, :, :], as3(ps[a][:, :], NT), ACT.Copy).then_inc(T_ev, 1)
                for n in range(NT):
                    for a in range(2):
                        act.wait_ge(V_pe, 8 * pr + 2 * n + a + 1)
                        hd = n * GDN_H + 2 * pr + a
                        fn(vn_sb[:, a, :], ps[4 + a][:, 0:P], ACT.Copy, scale=beta[:, hd:hd + 1]).then_inc(vn_done, 1)
                    for a in range(2):
                        act.wait_ge(O_pe, 8 * pr + 2 * n + a + 1)
                        fn(o_tok[:, a, n, :], ps[a][:, 0:P], ACT.Copy).then_inc(o_cp, 1)
                act.wait_ge(o_cp, 8 * (pr + 1))
                for a in range(2):
                    for n in range(NT):
                        c = NT * a + n
                        last = fn(tmpT[:, a, n, :], o_tok[:, a, n, :], ACT.Square, accum_out=o_ss[:, c:c + 1])
                link(last)
                inverse_root(o_r, o_ss, 1.0 / P, eps_rms, or_done)
                for a in range(2):
                    act.wait_ge(oT_pe, 2 * pr + a + 1)
                    fn(aoT[:, 2 * pr + a, :], ps[2 + a][:, :], ACT.Copy, scale=ng_col).then_inc(gao_ev, 1)
            layer_norm(2)
            moe(1)

        @block.vector
        def _(dve):
            tt, ts, stt = nc.vector.tensor_tensor, nc.vector.tensor_scalar, nc.vector.scalar_tensor_tensor
            red = nc.vector.tensor_reduce
            link = linker(dve, dve_link)

            def transposes_out(k, tiles=range(NT)):
                for t in tiles:
                    if k % 2:
                        dve.wait_ge(tr_pe, 8 * k + 2 * t + 2)
                        nc.vector.tensor_copy(hT[:, 4:8, t * P:(t + 1) * P], as3(ps[7][:, :], 4)).then_inc(tr_dve, 1)
                        continue
                    for g in range(2):
                        part = (slice(None), slice(4 * g, 4 * g + 4), slice(t * P, (t + 1) * P))
                        dve.wait_ge(hT_hi_ev, 2 * (NT * (k // 2) + t) + g + 1)
                        tt(hT_lo[part], as3(ps[6 + g][:, :], 4), hT_hi[part].bitcast(f32), ALU.subtract).then_inc(hT_lo_ev, 1)

            def split_hi(l, b, c):
                if c == 0:
                    dve.wait_ge(ring_in[b % 3], 16 * (ring_no(l, b % 3) + b // 3 + 1))
                    ge(dve, cv_pe if l else proj_pe, 4 * (b - 1))
                nc.vector.tensor_copy(hi_of(b)[:, chunk(c), :], slot_k(b % 3)[:, chunk(c), :]).then_inc(w_hi_done, 1)

            def split_gates(w):
                link(nc.vector.tensor_copy(gates_hi, w))
                link(tt(gates_lo, w, gates_hi.bitcast(f32), ALU.subtract))

            def mean(t):
                ts(neg_mean[:, t:t + 1], sum2[:, 2 * t:2 * t + 1], sum2[:, 2 * t + 1:2 * t + 2], -1.0 / D,
                   ALU.add, ALU.mult).then_inc(mean_ready, 1)

            def centred(q, t):
                dve.wait_ge(ln_in, 32 * (q + 1))
                ge(dve, h_ready, NT * q + t)
                link(stt(ln_x, h[:, t, :], neg_mean[:, t:t + 1], ln_g, ALU.add, ALU.mult))

            def scaled(q, t):
                dve.wait_ge(rstd_ready, NT * q + t + 1)
                stt(h[:, t, :], ln_x, rstd[:, t:t + 1], ln_b, ALU.mult, ALU.add).then_inc(h_ready, 1)

            def mixer_norm(l):
                dve.wait_ge(res_in, 64 * (l + 1))
                for t in range(NT):
                    for c in range(2):
                        dve.wait_ge(out_pe, 8 * l + 2 * t + c + 1)
                        hc = h[:, t, c * WB:(c + 1) * WB]
                        stt(hc, hc, ALPHA, ps[(2 * t + c) % 4][:, :], ALU.mult, ALU.add,
                            accum_out=sum2[:, 2 * t + c:2 * t + c + 1]).then_inc(mix_acc, 1)
                    dve.wait_ge(mix_acc, 8 * l + 2 * t + 2)
                    mean(t)
                    dve.wait_ge(mean_ready, 8 * l + t + 1)
                    centred(2 * l, t)
                    scaled(2 * l, t)
                    transposes_out(2 * l + 1, range(max(t - 1, 0), t if t < NT - 1 else NT))

            def router(l):
                def grp(x):
                    return as3(x, NT * NG)

                def tok(x):
                    return as3(x, NT)

                def bc(x, n):
                    return x.unsqueeze(2).broadcast_to([P, x.shape[1], n])

                dve.wait_ge(routing, ROUTE * l + RT_PE)
                link(red(rmx, tok(ps[4][:, 0:64]), X, ALU.max))
                tt(tok(probs), tok(ps[4][:, 0:64]), bc(rmx, NE), ALU.subtract).then_inc(routing, 1)
                dve.wait_ge(routing, ROUTE * l + RT_EXP)
                link(red(rsm, tok(probs), X, ALU.add))
                link(nc.vector.reciprocal(rsm, rsm))
                link(tt(tok(probs), tok(probs), bc(rsm, NE), ALU.mult))
                link(tt(selv, probs, rb_bc, ALU.add))
                s = [grp(selv)[:, :, k] for k in range(EPG)]
                link(tt(gr[0], s[0], s[1], ALU.max))
                link(tt(gr[1], s[0], s[1], ALU.min))
                link(tt(gr[2], s[2], s[3], ALU.max))
                link(tt(gr[3], s[2], s[3], ALU.min))
                link(tt(gr[4], gr[0], gr[2], ALU.max))
                link(tt(gr[0], gr[0], gr[2], ALU.min))
                link(tt(gr[1], gr[1], gr[3], ALU.max))
                link(tt(gr[0], gr[0], gr[1], ALU.max))
                link(tt(gr[0], gr[0], gr[4], ALU.add))

                def first_best(oh, val, key, weight, n):
                    link(red(rmx, tok(val), X, ALU.max))
                    link(tt(tok(key), tok(val), bc(rmx, n), ALU.is_equal))
                    link(tt(key, key, weight, ALU.mult))
                    link(red(rmx, tok(key), X, ALU.max))
                    link(tt(tok(oh), tok(key), bc(rmx, n), ALU.is_equal))

                first_best(gr[1], gr[0], gr[2], con[:, C_GW:C_EW], NG)
                link(ts(gr[1], gr[1], 1.0, BIG, ALU.subtract, ALU.mult))
                link(tt(grp(selv), grp(selv), bc(gr[1], EPG), ALU.add))
                first_best(oh0, selv, rkey, con[:, C_EW:C_EI], NE)
                link(stt(selv, oh0, -BIG, selv, ALU.mult, ALU.add))
                first_best(oh1, selv, rkey, con[:, C_EW:C_EI], NE)
                tt(rkey, oh0, oh1, ALU.add).then_inc(routing, 1)
                dve.wait_ge(routing, ROUTE * l + POS_PE)
                for a, oh in enumerate((oh0, oh1)):
                    link(tt(rtmp, ps[5][:, 0:64], oh, ALU.mult))
                    link(red(pos[a], tok(rtmp), X, ALU.add))
                for t in range(NT):
                    for a in range(2):
                        j = 2 * t + a
                        last = ts(pick[:, j, :], con[:, C_IOTA:C_ROW], pos[a][:, t:t + 1], con[:, C_ROW + j:C_ROW + j + 1],
                                  ALU.is_equal, ALU.mult)
                last.then_inc(routing, 1)
                for a, oh in enumerate((oh0, oh1)):
                    link(tt(rtmp, probs, oh, ALU.mult))
                    link(red(gate[a], tok(rtmp), X, ALU.add))
                link(tt(gsum, gate[0], gate[1], ALU.add))
                link(nc.vector.reciprocal(gsum, gsum))
                for a in range(2):
                    link(tt(gate[a], gate[a], gsum, ALU.mult))
                dve.wait_ge(routing, ROUTE * l + LIST_PE)
                link(ts(empty_f, ps[5][:, 96:96 + NE], 0.0, float(EMPTY + 1), ALU.is_equal, ALU.mult))
                link(stt(row_f, ps[5][:, 96:96 + NE], -1.0, empty_f, ALU.add, ALU.add))
                link(ts(empty_f, row_f, 0.5, -0.25, ALU.mult, ALU.add))
                link(nc.vector.tensor_copy(first_row, row_f))
                nc.vector.tensor_copy(first_tok, empty_f).then_inc(routing, 1)
                for a, oh in enumerate((oh0, oh1)):
                    link(tt(rtmp, con[:, C_EI:C_EPS], oh, ALU.mult))
                    link(red(exp_n, tok(rtmp), X, ALU.add))
                    link(ts(blk, pos[a], float(TB), None, ALU.is_ge))
                    for k in range(2, NB):
                        link(stt(blk, pos[a], float(k * TB), blk, ALU.is_ge, ALU.add))
                    link(stt(exp_n, exp_n, float(NB), blk, ALU.mult, ALU.add))
                    link(stt(pos[a], blk, -float(TB), pos[a], ALU.mult, ALU.add))
                    by_a = addr_i.rearrange("p (t a) -> p t a", a=2)[:, :, a]
                    link(stt(by_a, pos[a], float(NE * NB), exp_n, ALU.mult, ALU.add))
                link(red(cmax, ps[5][:, 64:80], X, ALU.max))
                nc.vector.tensor_copy(cnt_i, cmax).then_inc(routing, 1)

            def x_out(x_t, v, n):
                after(dve, v, "xTb_pe", n)
                nc.vector.tensor_copy(x_t[:, 4 * TB:8 * TB], ps[5][:, 0:4 * TB]).then_inc(v["xTb_ev"][0], 1)

            def hidden(v, n):
                after(dve, v, "sil_done", n)
                after(dve, v, "up_pe", n)
                tt(hid[0:TB, :], ps[1][0:TB, :], sil[0:TB, :], ALU.mult).then_inc(v["hid_done"][0], 1)

            def rows_out(y, v, n):
                after(dve, v, "yb_pe", n)
                nc.vector.tensor_copy(y[0:TB, WB:2 * WB], ps[3][0:TB, :]).then_inc(v["yb_ev"][0], 1)

            def moe(l):
                router(l)
                def split(j, par, n, chunks=range(WCH)):
                    for c in chunks:
                        s, part = 3 * par + j, slice(1024 * c, 1024 * (c + 1))
                        ge(dve, hi_split, WCH * (3 * n + j) + c + 1)
                        tt(w_lo[s][:, part], ring[s][:, part], ex_hi[j][:, part].bitcast(f32), ALU.subtract).then_inc(gu_lo_split, 1)

                def x_lo(g, n):
                    after(dve, ex, ("xTa_hi", "xTb_hi")[g], n)
                    part = (slice(None), slice(4 * g * TB, 4 * (g + 1) * TB))
                    tt(xT_lo[part], ps[4 + g][:, 0:4 * TB], xT_hi[part].bitcast(f32), ALU.subtract).then_inc(ex["xTa_lo"][0], 1)

                split(0, 0, NE * l)
                x_lo(0, NE * l)
                x_lo(1, NE * l)
                split(1, 0, NE * l)

                def expert(i, par, more=True):
                    n = NE * l + 2 * i + par
                    if more:
                        split(0, 1 - par, n + 1, range(WCH - 1))
                    after(dve, ex, "hidT_pe", n - 1)
                    hidden(ex, n)
                    if more:
                        split(0, 1 - par, n + 1, (WCH - 1,))
                        x_lo(0, n + 1)
                    after(dve, ex, "hidT_hi", n)
                    tt(hidT_lo[:, :], ps[6][:, 0:NFK * TB], hidT_hi[:, :].bitcast(f32), ALU.subtract).then_inc(ex["hidT_lo"][0], 1)
                    if more:
                        x_lo(1, n + 1)
                        split(1, 1 - par, n + 1)
                    ge(dve, y_st[par], 16 * (8 * l + i))
                    rows_out(y_sb[:, par, :], ex, n)

                expert(0, 0)
                expert(0, 1)
                with dve.Fori(1, NE // 2 - 1) as i:
                    expert(i, 0)
                    expert(i, 1)
                expert(NE // 2 - 1, 0)
                expert(NE // 2 - 1, 1, more=False)
                for n in range(2):
                    dve.wait_ge(y_st[n], 16 * 8 * (l + 1))
                v = ov[l]
                more = dve.value_load(cnt_i[0:1, 0:1], min_val=0, max_val=SEQ)
                with dve.If(more > TB):
                    with dve.Fori(0, NE * (NB - 1)) as r:
                        x_out(xT, v, r)
                        hidden(v, r)
                        rows_out(y_sb[:, 0, :], v, r)
                q = 2 * l + 1
                for t in range(NT):
                    dve.wait_ge(yg_in[t], 32 * (l + 1))
                    dve.wait_ge(y0_gated, NT * l + t + 1)
                    y0, y1 = y_got[t][:, 0, :], y_got[t][:, 1, :]
                    link(stt(y1, y1, gate[1][:, t:t + 1], y0, ALU.mult, ALU.add))
                    stt(h[:, t, :], h[:, t, :], ALPHA, y1, ALU.mult, ALU.add,
                        accum_out=sum2[:, 2 * t:2 * t + 1]).then_inc(comb_done, 1)
                    dve.wait_ge(comb_done, NT * l + t + 1)
                    ts(neg_mean[:, t:t + 1], sum2[:, 2 * t:2 * t + 1], -1.0 / D, None, ALU.mult).then_inc(mean_ready, 1)
                    if t:
                        scaled(q, t - 1)
                    dve.wait_ge(mean_ready, NT * q + t + 1)
                    centred(q, t)
                    if q == 1 and t >= 2:
                        transposes_out(2, (t - 2,))
                scaled(q, NT - 1)

            dve.wait_ge(con_in, 16)
            transposes_out(0)
            dve.wait_ge(fox_par_in, 16 * N_FOX_PAR)
            split_gates(w_f)
            ts(gain[:, 0:1], gain[:, 0:1], FOX_DH ** -0.5, None, ALU.mult).then_inc(gain_ready, 1)

            def bc64(x):
                return x.unsqueeze(2).broadcast_to([P, 8, FOX_DH])

            for n in range(16):
                dve.wait_ge(sq_done, n + 1)
                red(head_ss[:, n % 2, :], as3(sq[:, n % 2, :], 8), X, ALU.add).then_inc(head_sum, 1)
                if n == 5:
                    dve.wait_ge(fox_gates, F_PE)
                    link(tt(f_z, ps[4][:, 0:64], bf_bc, ALU.add))
                    stt(f_e, f_z, -1.0, f_z, ALU.mult, ALU.max).then_inc(fox_gates, 1)
                if n == 7:
                    dve.wait_ge(fox_gates, F_LN)
                    stt(lf, f_z, 0.0, f_e, ALU.min, ALU.subtract).then_inc(fox_gates, 1)
                if n == 10:
                    dve.wait_ge(fox_gates, CSUM_PE)
                    nc.vector.tensor_copy(c_tok, ps[4][:, 64:128]).then_inc(fox_gates, 1)
                dve.wait_ge(head_rs, n + 1)
                ge(dve, qT_pe, n - 1)
                tt(as3(qn[:, n % 2, :], 8), as3(ps[n % 2][:, :], 8), bc64(head_r[:, n % 2, :]), ALU.mult).then_inc(qn_done, 1)
                for c in AHEAD[n % 4]:
                    split_hi(0, n // 4 + 1, c)
            for b in range(5, 8):
                for c in range(CHUNKS):
                    split_hi(0, b, c)
            for m in range(8):
                dve.wait_ge(og_exp, m + 1)
                link(ts(ogT[:, m, :], ogT[:, m, :], 1.0, None, ALU.add))
                link(nc.vector.reciprocal(ogT[:, m, :], ogT[:, m, :]))

            M = FOX_H * NT

            def shifted(m):
                hd, i = m // NT, m % NT
                n = (i + 1) * P
                s = s_buf[:, m % 4, :]
                dve.wait_ge(s_pe, m + 1)
                if i == 0:
                    dve.wait_ge(c_in[hd % 2], 16 * (hd // 2 + 1))
                ge(dve, pT_pe, m - 3)
                stt(s[:, 0:n], s_banks[m % 4][:, 0:n], c_tok[:, 16 * i + hd:16 * i + hd + 1], c_buf[:, hd % 2, 0:n],
                    ALU.add, ALU.subtract).then_inc(s_sub, 1)
                dve.wait_ge(s_sub, m + 1)
                link(tt(s[:, n - P:n], s[:, n - P:n], causal, ALU.add))
                red(neg_max[:, m % 4:m % 4 + 1], s[:, 0:n], X, ALU.max, negate=True).then_inc(max_done, 1)

            def normalised(m):
                n = (m % NT + 1) * P
                dve.wait_ge(p_exp, m + 1)
                r = row_inv[:, m % 4:m % 4 + 1]
                link(nc.vector.reciprocal(r, row_sum[:, m % 4:m % 4 + 1]))
                s = s_buf[:, m % 4, 0:n]
                ts(s, s, r, None, ALU.mult).then_inc(p_ready, 1)

            def gated(pr):
                dve.wait_ge(pv_pe, 8 * (pr + 1))
                tt(aoT[:, pr, :], ps[5 + pr % 2][:, :], ogT[:, pr, :], ALU.mult).then_inc(o_ev, 1)

            shifted(0)
            shifted(1)
            for m in range(M):
                if m + 2 < M:
                    shifted(m + 2)
                normalised(m)
                if m % 8 == 1 and m > 8:
                    gated(m // 8 - 1)
            gated(NPAIR - 1)
            dve.wait_ge(par_in, 16 * N_PAR)
            mixer_norm(0)
            moe(0)

            dve.wait_ge(h_ready, 2 * NT)
            split_gates(w_ab)
            transposes_out(2, range(NT - 2, NT))

            def gdn_gates_first():
                dve.wait_ge(gdn_gates, BETA_EXP)
                link(ts(beta, beta, 1.0, None, ALU.add))
                link(nc.vector.reciprocal(beta, beta))
                link(tt(as3(g_z, NT), as3(ps[4][:, 0:NT * 16], NT)[:, :, GDN_H:2 * GDN_H], as3(dt_bc, NT), ALU.add))
                stt(g_e, g_z, -1.0, g_z, ALU.mult, ALU.max).then_inc(gdn_gates, 1)

            def gdn_gates_second():
                dve.wait_ge(gdn_gates, G_EXP1)
                link(stt(g_t, g_z, 0.0, g_e, ALU.max, ALU.add))
                stt(g_t, g_t, -1.0, al_bc, ALU.mult, ALU.mult).then_inc(gdn_gates, 1)

            def l2_apply(ct):
                dve.wait_ge(rn_done, ct + 1)
                x = qkvT[ct // 8][:, ct % 8, :]
                stt(x, r_l2[:, ct % 2, :], P ** -0.5 if ct < 8 else 1.0, x, ALU.mult, ALU.mult).then_inc(l2_done, 1)

            for ct in range(NCT):
                dve.wait_ge(cv_pe, ct + 1)
                ge(dve, silu_done, ct - 1)
                x, y = ps[ct % 2], conv_tmp[:, ct % 2, :]

                def tap(w):
                    return conv_w[:, w * NCT + ct:w * NCT + ct + 1]

                link(ts(y, x[:, :], tap(CONV - 1), None, ALU.mult))
                for d in range(1, CONV):
                    last = stt(y[:, d:SEQ], x[:, 0:SEQ - d], tap(CONV - 1 - d), y[:, d:SEQ], ALU.mult, ALU.add)
                    if d < CONV - 1:
                        link(last)
                last.then_inc(conv_done, 1)
                if ct == 0:
                    gdn_gates_first()
                if ct == 1:
                    gdn_gates_second()
                if ct == 2:
                    dve.wait_ge(gdn_gates, GC_PE)
                    nc.vector.tensor_copy(gc_tok, ps[4][:, 64:96]).then_inc(gdn_gates, 1)
                for c in AHEAD[ct % 4]:
                    split_hi(1, ct // 4 + 1, c)
                if ct % 2 == 0 and 4 <= ct < 20:
                    l2_apply(ct - 4)
                    l2_apply(ct - 3)
            for c in range(CHUNKS):
                split_hi(1, 7, c)

            for pr in range(NHP):
                dve.wait_ge(gbc_in, 32 * (pr + 1))
                for a in range(2):
                    for n in range(NT):
                        hd = n * GDN_H + 2 * pr + a
                        last = stt(dec[:, a, n, :], g_bc[:, a, n, :], gc_tok[:, hd:hd + 1], causal_t, ALU.subtract, ALU.add)
                last.then_inc(dec_arg, 1)
                tt(as3(kd, 2), g_bc[:, :, :, P - 1], gc_tok.rearrange("p (n a) -> p a n", a=GDN_H)[:, 2 * pr:2 * pr + 2, :],
                   ALU.subtract).then_inc(kd_arg, 1)
                dve.wait_ge(kk_pe, pr + 1)
                dve.wait_ge(dec_done, pr + 1)
                for a in range(2):
                    for n in range(NT):
                        hd = n * GDN_H + 2 * pr + a
                        last = stt(mT[:, a, n, :], ps[a][:, n * P:(n + 1) * P], beta[:, hd:hd + 1], dec[:, a, n, :], ALU.mult, ALU.mult)
                last.then_inc(mT_done, 1)
                for a in range(2):
                    last = tt(attnT[:, a, :, :], as3(ps[2 + a][:, :], NT), dec[:, a, :, :], ALU.mult)
                last.then_inc(att_done, 1)

                def with_gates():
                    dve.wait_ge(gexp_done, pr + 1)
                    for a in range(2):
                        tt(q_dec[:, a, :, :], as3(qT[:, 2 * pr + a, :], NT), g_exp[:, a, :, :], ALU.mult)
                        tt(k_gate[:, a, :, :], as3(kT[:, 2 * pr + a, :], NT), g_exp[:, a, :, :], ALU.mult)

                for a in range(2):
                    dve.wait_ge(T_pe, 14 * pr + a + 1)
                    tt(inv[:, a, :, :], ident.unsqueeze(1).broadcast_to([P, NT, P]), as3(ps[a][:, :], NT), ALU.subtract).then_inc(X_ev, 1)
                with_gates()
                dve.wait_ge(xT0, pr + 1)
                for v in range(1, LEVELS):
                    for a in range(2):
                        dve.wait_ge(U_pe, 12 * pr + 2 * (v - 1) + a + 1)
                        if v < LEVELS - 1:
                            tt(inv[:, a, :, :], inv[:, a, :, :], as3(ps[2 + a][:, :], NT), ALU.subtract).then_inc(X_ev, 1)
                        tt(invT[:, a, :, :], invT[:, a, :, :], as3(ps[4 + a][:, :], NT), ALU.subtract).then_inc(XT_ev, 1)
                for n in range(NT):
                    for a in range(2):
                        if n:
                            dve.wait_ge(R_pe, 6 * pr + 2 * (n - 1) + a + 1)
                            tt(r_sb[:, a, :], v_chunk[:, a, n, :], ps[2 + a][:, 0:P], ALU.subtract).then_inc(r_done, 1)
                    for a in range(2):
                        if n < NT - 1:
                            dve.wait_ge(K_pe, 6 * pr + 2 * n + a + 1)
                            if n == 0:
                                nc.vector.tensor_copy(st[:, a, :], ps[6 + a][:, 0:P]).then_inc(st_done, 1)
                            else:
                                stt(st[:, a, :], st[:, a, :], egl[:, NT * a + n:NT * a + n + 1], ps[6 + a][:, 0:P],
                                    ALU.mult, ALU.add).then_inc(st_done, 1)
                dve.wait_ge(or_done, pr + 1)
                for a in range(2):
                    for n in range(NT):
                        c, hd = NT * a + n, 2 * pr + a
                        last = stt(o_tok[:, a, n, :], o_tok[:, a, n, :], o_r[:, c:c + 1], og_tok[:, n, hd * P:(hd + 1) * P], ALU.mult, ALU.mult)
                last.then_inc(on_done, 1)
            mixer_norm(1)
            moe(1)


INPUTS = ("x", "ln_mix_g", "ln_mix_b", "ln_ffn_g", "ln_ffn_b", "router_w", "router_b", "fox_w_in", "fox_b_f",
          "fox_q_gain", "fox_k_gain", "fox_w_out", "gdn_w_in", "gdn_conv_w", "gdn_a_log", "gdn_dt_bias",
          "gdn_norm_g", "gdn_w_out", "moe_w_gate", "moe_w_up", "moe_w_down")


def kernel(**inputs):
    import concourse.bacc as bacc
    from concourse.bass_utils import run_bass_kernel_spmd

    nc = bacc.Bacc("TRN2", target_bir_lowering=False, num_devices=1)
    arrays = {name: np.ascontiguousarray(inputs[name]) for name in INPUTS}
    arrays["con"], arrays["rows"] = constants(), row_numbers()
    io = {name: nc.dram_tensor(f"in_{name}", a.shape, mybir.dt.from_np(a.dtype), kind="ExternalInput").ap()
          for name, a in arrays.items()}
    out = nc.dram_tensor("out", (1, SEQ, D), mybir.dt.float32, kind="ExternalOutput").ap()
    hybrid_trunk(nc, io, out)
    result = run_bass_kernel_spmd(nc, [{f"in_{name}": a for name, a in arrays.items()}], core_ids=[0])
    return result.results[0]["out"]
```

```python
import math
from contextlib import ExitStack

import numpy as np

import concourse.bass as bass
from concourse import mybir

D = 1024
SEQ = 512
P = 128
NT = SEQ // P
ND = D // P
WB = 512
FOX_H, FOX_DH = 16, 64
NPAIR = FOX_H // 2
GDN_H = 8
NHP = GDN_H // 2
CONV = 4
NCT = 3 * ND
NE, NG, EPG = 16, 4, 4
DF = D // 2
NFK = DF // P
TB = 128
NB = -(-SEQ // TB)
ALPHA = (2.0 * 2) ** 0.25
LN_EPS, RMS_EPS, L2_EPS = 1e-5, 1e-6, 1e-6
BIG = 1e30
EMPTY = 4 * SEQ
LEVELS = 7

C_ID, C_ONE, C_UP, C_UPS = 0, 128, 256, 384
C_CAUS, C_CAUST = 512, 640
C_LVL = 768
C_GW = C_LVL + LEVELS * P
C_EW = C_GW + NT * NG
C_EI = C_EW + NT * NE
C_EPS = C_EI + NT * NE
C_IOTA = C_EPS + 5
C_ROW = C_IOTA + P
C_TOT = C_ROW + 2 * NT
SMALL = 1808


def constants():
    c = np.zeros((P, C_TOT), np.float32)
    i, j = np.arange(P)[:, None], np.arange(P)[None, :]
    c[:, C_ID:C_ID + P] = i == j
    c[:, C_ONE:C_ONE + P] = 1.0
    c[:, C_UP:C_UP + P] = i <= j
    c[:, C_UPS:C_UPS + P] = i < j
    c[:, C_CAUS:C_CAUS + P] = np.where(j <= i, 0.0, -BIG)
    c[:, C_CAUST:C_CAUST + P] = np.where(i <= j, 0.0, -BIG)
    for v in range(LEVELS):
        b = 1 << v
        c[:, C_LVL + v * P:C_LVL + (v + 1) * P] = ((i >> v) % 2 == 0) & ((j >> v) == (i >> v) + 1)
    c[:, C_GW:C_EW] = np.tile(np.arange(NG, 0, -1), NT)
    c[:, C_EW:C_EI] = np.tile(np.arange(NE, 0, -1), NT)
    c[:, C_EI:C_EPS] = np.tile(np.arange(NE), NT)
    c[:, C_EPS:C_IOTA] = [LN_EPS, RMS_EPS, L2_EPS, 1.0, -0.5]
    c[:, C_IOTA:C_ROW] = j
    c[:, C_ROW:] = row_numbers() + 1
    return c


def row_numbers():
    t = np.arange(P)[:, None, None] + P * np.arange(NT)[None, :, None]
    return (2 * t + np.arange(2)[None, None, :]).reshape(P, 2 * NT).astype(np.int32)


def hybrid_trunk(nc, io, out):
    f32, f32r, i32 = mybir.dt.float32, mybir.dt.float32r, mybir.dt.int32
    ALU, ACT, X = mybir.AluOpType, mybir.ActivationFunctionType, mybir.AxisListType.X
    ctx = ExitStack()
    with ctx:
        def sb(name, cols, dt=f32, rows=P):
            return ctx.enter_context(nc.sbuf_tensor(name, [rows, cols], dt))

        def sem(name):
            return ctx.enter_context(nc.semaphore(name))

        def scratch(name, shape, dt=f32):
            return nc.dram_tensor(name, shape, dt, kind="Internal").ap()

        def as3(ap, n):
            return ap.rearrange("p (a b) -> p a b", a=n)

        def as4(ap, a, n):
            return ap.rearrange("p (a n c) -> p a n c", a=a, n=n)

        h_rows = [scratch(f"h_rows{l}", (SEQ, D)) for l in range(2)]
        h_mid = scratch("h_mid", (SEQ, D))
        y_rows = [scratch(f"y_rows{l}", (2 * SEQ, D)) for l in range(2)]
        tok_list = [scratch(f"tok_list{l}", (P * NE * NB, 1), i32) for l in range(2)]
        c_rows = scratch("c_rows", (FOX_H, SEQ))
        g_rows = scratch("g_rows", (NT * GDN_H, P))

        ring = [sb(f"ring{s}", 4096) for s in range(6)]
        ring_at = [nc.sbuf_base - 4 * 4096 * (6 - s) for s in range(6)]
        area = [sb(f"area{n}", 4096) for n in range(6)]
        area_at = [nc.sbuf_base - 4 * 4096 * (6 - n) for n in range(6)]
        con = sb("con", C_TOT)
        small = sb("small", SMALL)
        smalli = sb("smalli", 2 * NE * NB + 2 * 2 * NT + 3 + 2 * NE, i32)
        ps = [ctx.enter_context(nc.psum_tensor(f"ps{n}", [P, 512], f32)) for n in range(8)]

        sum_banks = (ps[2], ps[3], ps[6], ps[7])
        s_banks = (ps[0], ps[1], ps[2], ps[7])

        def slot(s):
            return ring[s][:, :]

        def slot_k(s):
            return as3(slot(s), ND)

        def split_part(name, cols, at):
            return nc.alloc_sbuf_tensor_at(name, [P, cols], f32r, offset=at)

        w_lo = [split_part(f"w_lo{s}", 4096, ring_at[s]) for s in range(6)]
        w_hi = [split_part(f"w_hi{s}", 4096, ring_at[3 + s]) for s in range(2)]
        hT_lo = as3(split_part("hT_lo", 4096, ring_at[5])[:, :], ND)
        hT_hi = as3(split_part("hT_hi", 4096, area_at[0])[:, :], ND)
        gates_hi = as3(split_part("gates_hi", ND * 16, area_at[5] + 4 * 3328)[:, :], ND)
        gates_lo = as3(split_part("gates_lo", ND * 16, area_at[5] + 4 * 3456)[:, :], ND)
        ex_hi = [split_part(f"ex_hi{j}", 4096, area_at[n]) for j, n in enumerate((4, 5, 0))]
        xT_hi, xT_lo = (split_part(f"xT_{n}", 8 * TB, area_at[2] + 4 * (2048 + 1024 * j)) for j, n in enumerate(("hi", "lo")))
        hidT_hi, hidT_lo = (split_part(f"hidT_{n}", NFK * TB, area_at[3] + 4 * (3072 + 512 * j)) for j, n in enumerate(("hi", "lo")))
        logits_T = area[5][0:16, 3584:4096]
        CHUNKS = 4
        AHEAD = ((0, 1), (2, 3), (), ())

        def hi_of(b):
            return as3(w_hi[b % 2][:, :], ND)

        def lo_of(b):
            return as3(w_lo[b % 3][:, :], ND)

        def chunk(c):
            return slice(c * ND // CHUNKS, (c + 1) * ND // CHUNKS)

        ident, ones = con[:, C_ID:C_ID + P], con[:, C_ONE:C_ONE + P]
        upper, upper_strict = con[:, C_UP:C_UP + P], con[:, C_UPS:C_UPS + P]
        causal, causal_t = con[:, C_CAUS:C_CAUS + P], con[:, C_CAUST:C_CAUST + P]
        eps_rms, eps_l2, one, minus_half = (con[:, C_EPS + n:C_EPS + n + 1] for n in range(1, 5))

        hT = as3(area[0][:, :], ND)
        h = as3(area[1][:, :], NT)
        aoT = hT
        ln_sq, ln_g, ln_b, ln_x = (area[5][:, 1024 * n:1024 * (n + 1)] for n in range(4))
        qkT = [as3(area[1][:, :], ND), as3(area[2][:, :], ND)]
        v_tok = as3(area[3][:, :], NT)
        ogT = as3(area[4][:, :], ND)
        cT = area[4][0:FOX_H, 0:SEQ]
        sq = as3(area[5][:, 0:1024], 2)
        qn = as3(area[5][:, 1024:2048], 2)
        s_buf = as3(area[5][:, 0:2048], 4)
        pT_buf = as3(area[5][:, 2048:3072], 2)
        c_buf = as3(area[5][:, 3072:4096], 2)
        xg = as3(area[2][:, 0:2048], 2)
        xT = area[2][:, 2048:3072]
        y_sb = as3(area[3][:, 0:2048], 2)
        sil, hid, hidT = (area[3][:, 2048 + 512 * n:2560 + 512 * n] for n in range(3))
        y_got = [as3(ring[3 + t // 2][:, :], 4)[:, 2 * (t % 2):2 * (t % 2) + 2, :] for t in range(NT)]
        pick = as3(area[3][:, 0:1024], 2 * NT)
        over_w = [as3(area[0][:, :], ND), as3(area[4][:, :], ND), as3(ring[5][:, :], NFK)]
        qkvT = [as3(area[n][:, :], GDN_H) for n in (1, 2, 3)]
        qT, kT, vT = qkvT
        og_tok = as3(area[4][:, :], NT)
        conv_tmp = as3(area[5][:, 0:1024], 2)
        sq_l2 = as3(area[5][:, 1024:2048], 2)
        r_l2 = as3(area[5][:, 2048:3072], 2)
        conv_raw = area[5][0:CONV * NCT, 3072:3200]
        gT_sb = area[5][0:NT * GDN_H, 3200:3328]
        (inv, invT, tmpT, attnT, dec, q_dec, k_gate, k_tok, v_chunk, g_bc, mT, g_exp) = (
            as4(ring[3 + n // 4][:, n % 4 * 1024:(n % 4 + 1) * 1024], 2, NT) for n in range(12))
        mlT = [as4(area[5][:, 1024 * n:1024 * (n + 1)], 2, NT) for n in range(2)]
        o_tok = as4(area[5][:, 2048:3072], 2, NT)
        r_sb, vn_sb, st, sq_o = (as3(area[5][:, 3072 + 256 * n:3328 + 256 * n], 2) for n in range(4))

        at = [0]

        def cols(n):
            at[0] += n
            assert at[0] <= SMALL
            return small[:, at[0] - n:at[0]]

        neg_mean, ssq, rstd, sum2 = cols(NT), cols(NT), cols(NT), cols(2 * NT)
        w_f, w_ab, router_w = (as3(cols(ND * 16), ND) for _ in range(3))
        conv_w = cols(CONV * NCT)
        bf_bc, gain, rb_bc = cols(NT * FOX_H), cols(2), cols(NT * NE)
        dt_bc, al_bc, ng_col = cols(NT * GDN_H), cols(NT * GDN_H), cols(1)
        lf, f_z, f_e, c_tok = (cols(NT * FOX_H) for _ in range(4))
        head_ss, head_r = as3(cols(16), 2), as3(cols(16), 2)
        neg_max, row_sum, row_inv = cols(4), cols(4), cols(4)
        probs, selv, oh0, oh1, rtmp, rkey = (cols(NT * NE) for _ in range(6))
        rmx, rsm = cols(NT), cols(NT)
        gr = [cols(NT * NG) for _ in range(8)]
        gate = [cols(NT), cols(NT)]
        gsum, exp_n, blk, cmax = cols(NT), cols(NT), cols(NT), cols(1)
        pos = [cols(NT), cols(NT)]
        row_f, empty_f = gr[2], gr[3]
        tok_f = cols(NE * NB)
        gc_tok, beta, g_z, g_e, g_t = (cols(NT * GDN_H) for _ in range(5))
        kd, o_ss, o_r = (cols(8) for _ in range(3))
        egl = [cols(8), cols(8)]
        i0 = 2 * NE * NB
        row_list, tok_of = smalli[:, 0:NE * NB], smalli[:, NE * NB:i0]
        addr_i, rowno_i = smalli[:, i0:i0 + 8], smalli[:, i0 + 8:i0 + 16]
        cnt_i, row_i, one_tok = (smalli[:, i0 + 16 + n:i0 + 17 + n] for n in range(3))
        first_row, first_tok = (smalli[:, i0 + 19 + NE * n:i0 + 19 + NE * (n + 1)] for n in range(2))

        ident_in, con_in, fox_par_in, par_in = sem("ident_in"), sem("con_in"), sem("fox_par_in"), sem("par_in")
        x_in = [sem(f"x_in{t}") for t in range(NT)]
        ring_in = [sem(f"ring_in{s}") for s in range(6)]
        ring_free = [sem(f"ring_free{s}") for s in range(6)]
        act_link, dve_link, pool_link = sem("act_link"), sem("dve_link"), sem("pool_link")
        tr_pe, tr_act, tr_dve = sem("tr_pe"), sem("tr_act"), sem("tr_dve")
        hT_hi_ev, hT_lo_ev = sem("hT_hi_ev"), sem("hT_lo_ev")
        w_hi_done, w_lo_done = sem("w_hi_done"), sem("w_lo_done")
        ao_split = sem("ao_split")
        gain_ready, conv_weights = sem("gain_ready"), sem("conv_weights")
        fox_gates, gdn_gates, routing = sem("fox_gates"), sem("gdn_gates"), sem("routing")
        (F_PROD, F_COPIED, F_PE, F_ABS, F_LN, LF_READY, CSUM_PE, C_READY, CT_PE) = range(1, 10)
        (AB_PROD, AB_COPIED, AB_PE, BETA_EXP, G_ABS, G_EXP1, G_READY, GC_PE, GC_READY, GT_PE) = range(1, 11)
        (RT_PE, RT_SUB, RT_EXP, OH_READY, POS_PE, PICK_READY, LIST_PE, LIST_READY, ADDR_READY) = range(1, 10)
        ROUTE = 9
        c_st, g_st = sem("c_st"), sem("g_st")
        proj_pe, sq_done, head_sum, head_rs, qn_done, qT_pe, qT_ev, v_ev, og_ev, inv_ready = (
            sem(n) for n in ("proj_pe", "sq_done", "head_sum", "head_rs", "qn_done", "qT_pe", "qT_ev", "v_ev", "og_ev", "inv_ready"))
        c_in = [sem(f"c_in{n}") for n in range(2)]
        s_pe, s_sub, max_done, p_exp, p_ready, pT_pe, pT_ev, pv_pe, o_ev = (
            sem(n) for n in ("s_pe", "s_sub", "max_done", "p_exp", "p_ready", "pT_pe", "pT_ev", "pv_pe", "o_ev"))
        res_in, ln_in, out_pe, mix_acc = sem("res_in"), sem("ln_in"), sem("out_pe"), sem("mix_acc")
        mean_ready, ssq_ready, rstd_ready, h_ready = sem("mean_ready"), sem("ssq_ready"), sem("rstd_ready"), sem("h_ready")
        hrow_st, hmid_st, out_st = sem("hrow_st"), sem("hmid_st"), sem("out_st")
        list_zero = sem("list_zero")
        xg_in = [sem(f"xg_in{n}") for n in range(2)]
        y_st = [sem(f"y_st{n}") for n in range(2)]
        yg_in = [sem(f"yg_in{n}") for n in range(NT)]
        y_done, y_gated, y_sum, comb_done = sem("y_done"), sem("y_gated"), sem("y_sum"), sem("comb_done")
        EXPERT = ("gate_pe", "up_pe", "sil_done", "hid_done", "hidT_pe", "hidT_hi", "hidT_lo", "ya_pe", "yb_pe", "ya_ev", "yb_ev")
        ex = {n: (sem(n), 1, 1) for n in EXPERT}
        for n in ("pe", "hi", "lo"):
            both = sem(f"xT_{n}")
            ex |= {f"xT{half}_{n}": (both, 2, k + 1) for k, half in enumerate("ab")}
        hi_split, gu_lo_split, down_lo_split = sem("hi_split"), sem("gu_lo_split"), sem("down_lo_split")
        WCH = 4
        SLOT_OF = (1, 0, 2)
        ov = []
        for l in range(2):
            steps = {"w_in": (sem(f"ov{l}_w_in"), 48, 48)}
            steps |= {n: (sem(f"ov{l}_{n}"), 16, 16) for n in ("x_in", "st")}
            steps["idx"] = (sem(f"ov{l}_idx"), 2, 4)
            steps["list"] = (sem(f"ov{l}_list"), 16, 16)
            for eng, names in (("pe", ("xTa_pe", "xTb_pe", "gate_pe", "up_pe", "hidT_pe", "ya_pe", "yb_pe")),
                               ("act", ("xTa_ev", "sil_done", "hidT_ev", "ya_ev")),
                               ("dve", ("xTb_ev", "hid_done", "yb_ev"))):
                done = sem(f"ov{l}_{eng}")
                steps |= {n: (done, len(names), k + 1) for k, n in enumerate(names)}
            ov.append(steps)
        cv_pe, conv_done, silu_done, sq2_done, ss_pe, rn_done, l2_done, ogg_pe, ogg_ev = (
            sem(n) for n in ("cv_pe", "conv_done", "silu_done", "sq2_done", "ss_pe", "rn_done", "l2_done", "ogg_pe", "ogg_ev"))
        gbc_in, kk_pe, dec_arg, dec_done, gexp_done, mT_done, att_done, kT_pe, vT_pe, kd_arg, k_ev, v_evg = (
            sem(n) for n in ("gbc_in", "kk_pe", "dec_arg", "dec_done", "gexp_done", "mT_done", "att_done", "kT_pe", "vT_pe", "kd_arg", "k_ev", "v_evg"))
        ml_done, xT0, T_pe, T_ev, U_pe, X_ev, XT_ev = (
            sem(n) for n in ("ml_done", "xT0", "T_pe", "T_ev", "U_pe", "X_ev", "XT_ev"))
        R_pe, r_done, V_pe, vn_done, O_pe, K_pe, st_done, o_cp, o_sq, or_done, on_done, oT_pe, gao_ev = (
            sem(n) for n in ("R_pe", "r_done", "V_pe", "vn_done", "O_pe", "K_pe", "st_done", "o_cp", "o_sq", "or_done", "on_done", "oT_pe", "gao_ev"))

        def ge(eng, s, v):
            if not isinstance(v, int) or v > 0:
                eng.wait_ge(s, v)

        def after(eng, v, step, n):
            s, per, first = v[step]
            ge(eng, s, n * per + first)

        def linker(eng, s):
            n = [0]

            def link(ins):
                n[0] += 1
                ins.then_inc(s, 1)
                eng.wait_ge(s, n[0])
            return link

        N_FOX_PAR, N_PAR = 7, 7
        MIX_LOADS = (4, 3, 3)

        def ring_no(l, s):
            return l * (8 + (MIX_LOADS[s] if s < 3 else 0))

        def expert_no(l, s):
            return ring_no(l, s) + (MIX_LOADS[s] if s < 3 else 0)

        block = ctx.enter_context(nc.Block())

        @block.sync
        def _(sp):
            params = [
                (w_f, io["fox_w_in"][0, :, 4 * D:4 * D + FOX_H].rearrange("(k p) n -> p k n", p=P)),
                (conv_raw, io["gdn_conv_w"][0, :, :].rearrange("w (c p) -> (w c) p", p=P)),
                (as3(bf_bc, NT), io["fox_b_f"][0, :].unsqueeze(0).broadcast_to([NT, FOX_H]).partition_broadcast(P)),
                (gain[0:64, 0:1], io["fox_q_gain"][0, :].unsqueeze(1)),
                (gain[64:128, 0:1], io["fox_q_gain"][0, :].unsqueeze(1)),
                (gain[0:64, 1:2], io["fox_k_gain"][0, :].unsqueeze(1)),
                (gain[64:128, 1:2], io["fox_k_gain"][0, :].unsqueeze(1)),
            ]
            late_params = [
                (w_ab, io["gdn_w_in"][0, :, 4 * D:4 * D + 2 * GDN_H].rearrange("(k p) n -> p k n", p=P)),
                (router_w, io["router_w"].rearrange("(k p) n -> p k n", p=P)),
                (as3(rb_bc, NT), io["router_b"].unsqueeze(0).broadcast_to([NT, NE]).partition_broadcast(P)),
                (as3(dt_bc, NT), io["gdn_dt_bias"][0, :].unsqueeze(0).broadcast_to([NT, GDN_H]).partition_broadcast(P)),
                (as3(al_bc, NT), io["gdn_a_log"][0, :].unsqueeze(0).broadcast_to([NT, GDN_H]).partition_broadcast(P)),
                (ng_col, io["gdn_norm_g"][0, :].unsqueeze(1)),
                (rowno_i, io["rows"]),
            ]
            assert len(params) == N_FOX_PAR and len(late_params) == N_PAR
            sp.dma_start(con[:, 0:P], io["con"][:, 0:P]).then_inc(ident_in, 16)
            for t in range(NT):
                sp.dma_start(h[:, t, :], io["x"][0, t * P:(t + 1) * P, :]).then_inc(x_in[t], 16)

            def mixer_block(l, b, w_in, w_out):
                s, n = b % 3, ring_no(l, b % 3) + b // 3
                ge(sp, ring_free[s], n)
                w = w_in[0, :, b * WB:(b + 1) * WB] if b < 8 else w_out[0, :, (b - 8) * WB:(b - 7) * WB]
                sp.dma_start(slot_k(s), w.rearrange("(k p) n -> p k n", p=P)).then_inc(ring_in[s], 16)

            def expert_load(l, e, i, par, matrices=(0, 1, 2)):
                for j in matrices:
                    s, name = 3 * par + SLOT_OF[j], ("moe_w_gate", "moe_w_up", "moe_w_down")[j]
                    ge(sp, ring_free[s], expert_no(l, s) + i)
                    dst = slot_k(s) if j < 2 else as3(slot(s), NFK)
                    sp.dma_start(dst, io[name][l, e, :, :].rearrange("(k p) n -> p k n", p=P)).then_inc(ring_in[s], 16)

            def rows_store(l, tiles):
                for t in tiles:
                    sp.wait_ge(h_ready, 8 * l + t + 1)
                    sp.dma_start(h_rows[l][t * P:(t + 1) * P, :], h[:, t, :]).then_inc(hrow_st, 16)

            for l, (w_in, w_out) in enumerate(((io["fox_w_in"], io["fox_w_out"]), (io["gdn_w_in"], io["gdn_w_out"]))):
                for b in range(3):
                    mixer_block(l, b, w_in, w_out)
                    if l == b == 0:
                        sp.dma_start(con[:, P:], io["con"][:, P:]).then_inc(con_in, 16)
                        for dst, src in params:
                            sp.dma_start(dst, src).then_inc(fox_par_in, 16)
                if l == 0:
                    for dst, src in late_params:
                        sp.dma_start(dst, src).then_inc(par_in, 16)
                if l == 1:
                    for t in range(NT):
                        sp.wait_ge(h_ready, 8 * l - 4 + t + 1)
                        sp.dma_start(h_mid[t * P:(t + 1) * P, :], h[:, t, :]).then_inc(hmid_st, 16)
                for b in range(3, 10):
                    mixer_block(l, b, w_in, w_out)
                if l:
                    sp.wait_ge(gao_ev, GDN_H)
                    sp.wait_ge(res_in, 64 * (l + 1))
                    sp.wait_ge(ln_in, 32 * (2 * l + 1))
                expert_load(l, 0, 0, 0, (0,))
                if l:
                    expert_load(l, 1, 0, 1)
                rows_store(l, range(NT - 1))
                expert_load(l, 0, 0, 0, (1, 2))
                rows_store(l, (NT - 1,))
                if l == 0:
                    sp.wait_ge(out_pe, 8)
                    expert_load(l, 1, 0, 1)
                with sp.Fori(1, NE // 2) as i:
                    for par in range(2):
                        expert_load(l, 2 * i + par, i, par)
                sp.wait_ge(y_done, l + 1)
                y_by_choice = y_rows[l].rearrange("(t a) d -> t a d", a=2)
                for t in range(NT):
                    for a in range(2):
                        sp.dma_start(y_got[t][:, a, :], y_by_choice[t * P:(t + 1) * P, a, :]).then_inc(yg_in[t], 16)
            for t in range(NT):
                sp.wait_ge(h_ready, 12 + t + 1)
                sp.dma_start(out[0, t * P:(t + 1) * P, :], h[:, t, :]).then_inc(out_st, 16)
            sp.wait_ge(out_st, 16 * NT)

        @block.gpsimd
        def _(pool):
            link = linker(pool, pool_link)
            link(nc.gpsimd.memset(row_list, EMPTY))
            for l in range(2):
                pool.dma_start(tok_list[l].rearrange("(p n) a -> p (n a)", p=P), row_list).then_inc(list_zero, 16)

            def layer_norm_params(q, g, b):
                pool.dma_start(ln_g, g.partition_broadcast(P)).then_inc(ln_in, 16)
                pool.dma_start(ln_b, b.partition_broadcast(P)).then_inc(ln_in, 16)

            def root_of_variance(q, tiles=range(NT)):
                for t in tiles:
                    pool.wait_ge(ssq_ready, NT * q + t + 1)
                    link(nc.gpsimd.tensor_scalar(rstd[:, t:t + 1], ssq[:, t:t + 1], 1.0 / D, LN_EPS, ALU.mult, ALU.add))
                    nc.gpsimd.tensor_tensor(rstd[:, t:t + 1], rstd[:, t:t + 1], minus_half, ALU.pow).then_inc(rstd_ready, 1)

            def moe(l):
                def rows_in(dst, tokens, done):
                    nc.gpsimd.indirect_dma_start(
                        out=dst, out_offset=None, in_=h_rows[l], in_offset=bass.IndirectOffsetOnAxis(ap=tokens, axis=0),
                        bounds_check=SEQ - 1, oob_is_err=False).then_inc(done, 16)

                def rows_back(src, rows, done):
                    nc.gpsimd.indirect_dma_start(
                        out=y_rows[l], out_offset=bass.IndirectOffsetOnAxis(ap=rows, axis=0), in_=src, in_offset=None,
                        bounds_check=2 * SEQ - 1, oob_is_err=False).then_inc(done, 16)

                link(nc.gpsimd.memset(xg, 0.0))
                root_of_variance(2 * l)
                pool.wait_ge(routing, ROUTE * l + LIST_READY)
                pool.wait_ge(hrow_st, 64 * (l + 1))

                def gather(e):
                    if e >= 2:
                        after(pool, ex, "xTb_pe", NE * l + e - 2)
                    rows_in(xg[:, e % 2, :], first_tok[:, e:e + 1], xg_in[e % 2])

                gather(0)
                gather(1)
                for e in range(NE):
                    if e + 2 < NE:
                        gather(e + 2)
                    n = NE * l + e
                    for c in range(WCH if e < NE - 1 else WCH // 2):
                        pool.wait_ge(hi_split, WCH * (3 * n + 2) + c + 1)
                        s, part = 3 * (e % 2) + 2, slice(1024 * c, 1024 * (c + 1))
                        nc.gpsimd.tensor_tensor(w_lo[s][:, part], ring[s][:, part], ex_hi[2][:, part].bitcast(f32),
                                                ALU.subtract).then_inc(down_lo_split, 1)
                    if e == NE - 1:
                        after(pool, ex, "up_pe", n)
                        layer_norm_params(2 * l + 1, io["ln_ffn_g"][l, :], io["ln_ffn_b"][l, :])
                    after(pool, ex, "ya_ev", NE * l + e)
                    after(pool, ex, "yb_ev", NE * l + e)
                    rows_back(y_sb[:, e % 2, :], first_row[:, e:e + 1], y_st[e % 2])
                v = ov[l]
                for n in range(2):
                    pool.wait_ge(y_st[n], 16 * 8 * (l + 1))
                pool.wait_ge(routing, ROUTE * l + ADDR_READY)
                more = pool.value_load(cnt_i[0:1, 0:1], min_val=0, max_val=SEQ)
                with pool.If(more > TB):
                    pool.wait_ge(list_zero, 32)
                    for j in range(2 * NT):
                        nc.gpsimd.indirect_dma_start(
                            out=tok_list[l], out_offset=bass.IndirectOffsetOnAxis(ap=addr_i[:, j:j + 1], axis=0),
                            in_=rowno_i[:, j:j + 1], in_offset=None).then_inc(v["list"][0], 16)
                    pool.wait_ge(v["list"][0], 16 * 2 * NT)
                    pool.dma_start(row_list, tok_list[l].rearrange("(p n) a -> p (n a)", p=P)).then_inc(v["list"][0], 16)
                    pool.wait_ge(v["list"][0], 16 * (2 * NT + 1))
                    nc.gpsimd.tensor_scalar(tok_f, row_list, 0.5, -0.25, ALU.mult, ALU.add).then_inc(v["idx"][0], 1)
                    pool.wait_ge(v["idx"][0], 1)
                    nc.gpsimd.tensor_copy(tok_of, tok_f).then_inc(v["idx"][0], 1)
                    pool.wait_ge(v["idx"][0], 2)
                    with pool.Fori(0, NE) as e:
                        with pool.Fori(0, NB - 1) as b:
                            r = e * (NB - 1) + b
                            for dst, name in zip(over_w, ("moe_w_gate", "moe_w_up", "moe_w_down")):
                                pool.dma_start(dst, io[name][l, e, :, :].rearrange("(k p) n -> p k n", p=P)).then_inc(v["w_in"][0], 16)
                            nc.gpsimd.tensor_copy(one_tok, tok_of[:, bass.ds(e * NB + b + 1, 1)]).then_inc(v["idx"][0], 1)
                            nc.gpsimd.tensor_copy(row_i, row_list[:, bass.ds(e * NB + b + 1, 1)]).then_inc(v["idx"][0], 1)
                            after(pool, v, "idx", r)
                            pool.nop(nofuse=True)
                            rows_in(xg[:, 0, :], one_tok, v["x_in"][0])
                            after(pool, v, "yb_ev", r)
                            after(pool, v, "ya_ev", r)
                            pool.nop(nofuse=True)
                            rows_back(y_sb[:, 0, :], row_i, v["st"][0])
                            after(pool, v, "st", r)
                pool.sem_inc(y_done, 1)


                def chosen_sum(t):
                    pool.wait_ge(y_gated, 2 * (NT * l + t + 1))
                    nc.gpsimd.tensor_tensor(y_got[t][:, 0, :], y_got[t][:, 0, :], y_got[t][:, 1, :], ALU.add).then_inc(y_sum, 1)

                chosen_sum(0)
                for t in range(NT):
                    if t + 1 < NT:
                        chosen_sum(t + 1)
                    root_of_variance(2 * l + 1, (t,))

            def split_lo(l, blocks=range(8)):
                for b in blocks:
                    for c in range(CHUNKS if b else CHUNKS // 2):
                        pool.wait_ge(w_hi_done, CHUNKS * (10 * l + b) + c + 1)
                        nc.gpsimd.tensor_tensor(lo_of(b)[:, chunk(c), :], slot_k(b % 3)[:, chunk(c), :],
                                                hi_of(b)[:, chunk(c), :].bitcast(f32), ALU.subtract).then_inc(w_lo_done, 1)

            def fox_out_split(pr, part):
                if part == 0:
                    pool.wait_ge(o_ev, pr + 1)
                    link(nc.gpsimd.tensor_copy(hT_hi[:, pr, :], ogT[:, pr, :]))
                else:
                    nc.gpsimd.tensor_tensor(hT_lo[:, pr, :], ogT[:, pr, :], hT_hi[:, pr, :].bitcast(f32), ALU.subtract).then_inc(ao_split, 1)

            split_lo(0, range(9))
            pool.wait_ge(c_st, 16)
            pool.wait_ge(qT_ev, 16)
            for hd in range(FOX_H):
                ge(pool, s_sub, NT * (hd - 1))
                pool.dma_start(c_buf[:, hd % 2, :], c_rows[hd, :].partition_broadcast(P)).then_inc(c_in[hd % 2], 16)
                if hd == 1:
                    split_lo(0, (9,))
                if hd >= 3:
                    fox_out_split((hd - 3) // 2, (hd - 3) % 2)
            fox_out_split(NPAIR - 2, 1)
            for part in range(2):
                fox_out_split(NPAIR - 1, part)
            pool.wait_ge(pv_pe, FOX_H * NT)
            for t in range(NT):
                pool.dma_start(h[:, t, :], io["x"][0, t * P:(t + 1) * P, :]).then_inc(res_in, 16)
            layer_norm_params(0, io["ln_mix_g"][0, :], io["ln_mix_b"][0, :])
            pool.wait_ge(par_in, 16 * N_PAR)
            moe(0)

            split_lo(1)
            pool.wait_ge(g_st, 16)
            pool.wait_ge(ogg_pe, 8)
            g_by_head = g_rows.rearrange("(n a) c -> a n c", a=GDN_H)

            def decays_in(pr):
                for a in range(2):
                    pool.dma_start(g_bc[:, a, :, :], g_by_head[2 * pr + a, :, :].partition_broadcast(P)).then_inc(gbc_in, 16)

            decays_in(0)
            for pr in range(NHP):
                pool.wait_ge(mT_done, pr + 1)
                for v in range(LEVELS):
                    ge(pool, T_pe, 14 * pr + 2 * (v - 1) if v >= 2 else 0)
                    if v == 2:
                        pool.wait_ge(xT0, pr + 1)
                    for a in range(2):
                        last = nc.gpsimd.tensor_tensor(
                            mlT[v % 2][:, a, :, :], mT[:, a, :, :],
                            con[:, C_LVL + v * P:C_LVL + (v + 1) * P].unsqueeze(1).broadcast_to([P, NT, P]), ALU.mult)
                    last.then_inc(ml_done, 1)
                    if v == 1 and pr + 1 < NHP:
                        pool.wait_ge(k_ev, pr + 1)
                        pool.wait_ge(kd_arg, pr + 1)
                        decays_in(pr + 1)
                for n in range(NT):
                    of_n = [as3(x, 2)[:, :, n] for x in (o_ss, o_r)]
                    pool.wait_ge(o_sq, 8 * pr + 2 * n + 2)
                    link(nc.gpsimd.tensor_scalar(of_n[1], of_n[0], 1.0 / P, RMS_EPS, ALU.mult, ALU.add))
                    nc.gpsimd.tensor_tensor(of_n[1], of_n[1], minus_half.broadcast_to([P, 2]), ALU.pow).then_inc(or_done, 1)
            pool.wait_ge(gao_ev, GDN_H)
            pool.wait_ge(hmid_st, 64)
            for t in range(NT):
                pool.dma_start(h[:, t, :], h_mid[t * P:(t + 1) * P, :]).then_inc(res_in, 16)
            layer_norm_params(2, io["ln_mix_g"][1, :], io["ln_mix_b"][1, :])
            moe(1)

        @block.tensor
        def _(pe):
            mm = nc.tensor.matmul

            def transpose_tile(k, t):
                if k == 0:
                    pe.wait_ge(x_in[t], 16)
                else:
                    pe.wait_ge(h_ready, NT * (k - 1) + t + 1)
                for g in range(2):
                    if k % 2:
                        ge(pe, (tr_act, tr_dve)[g], NT * (k // 2) + t)
                    else:
                        ge(pe, hT_lo_ev, 2 * (NT * (k // 2) + t - 1) + g + 1)
                    for j in range(4):
                        d = 4 * g + j
                        last = nc.tensor.transpose(ps[6 + g][:, j * P:(j + 1) * P], h[:, t, d * P:(d + 1) * P], ident)
                    last.then_inc(tr_pe, 1)

            def hT_ready(k, t):
                if k % 2:
                    pe.wait_ge(tr_act, NT * (k // 2) + t + 1)
                    pe.wait_ge(tr_dve, NT * (k // 2) + t + 1)
                else:
                    pe.wait_ge(hT_lo_ev, 2 * (NT * (k // 2) + t + 1))

            def router_tile(t):
                for k in range(ND):
                    last = mm(ps[4][:, 16 * t:16 * t + 16], hT[:, k, t * P:(t + 1) * P], router_w[:, k, :], start=k == 0, stop=k == ND - 1)
                return last

            def gate_logits(done):
                for part, (w, x) in enumerate(((gates_hi, hT_hi), (gates_hi, hT_lo), (gates_lo, hT_hi))):
                    for k in range(ND):
                        last = mm(ps[4][0:16, :], w[:, k, :], x[:, k, :], start=part == 0 and k == 0, stop=part == 2 and k == ND - 1)
                last.then_inc(done, 1)

            def gate_transposes(copied, done):
                pe.wait_ge(done, copied)
                for t in range(NT):
                    last = nc.tensor.transpose(ps[4][:, 16 * t:16 * t + 16], logits_T[:, t * P:(t + 1) * P], ident[0:16, 0:16])
                last.then_inc(done, 1)

            def transposes(k, narrow=None, done=None, first=0):
                for t in range(first, NT):
                    if t and narrow is not None:
                        hT_ready(k, t - 1)
                        narrow(t - 1)
                    transpose_tile(k, t)
                hT_ready(k, NT - 1)
                if narrow is not None:
                    narrow(NT - 1).then_inc(done, 1)

            def product(l, b, dst, t, channels):
                if t == 0:
                    pe.wait_ge(w_hi_done, CHUNKS * (10 * l + b + 1))
                for part, (x, w) in enumerate(((hT_hi, hi_of(b)), (hT_lo, hi_of(b)), (hT_hi, lo_of(b)))):
                    for k in range(ND):
                        if t == 0 and part == 2 and k % (ND // CHUNKS) == 0:
                            pe.wait_ge(w_lo_done, CHUNKS * (10 * l + b) + (k // (ND // CHUNKS) + 1 if b else CHUNKS))
                        if t == part == 0 and b == 8:
                            pe.wait_ge(ao_split, k + 1)
                        narrow, wide = (w, x) if channels else (x, w)
                        last = mm(dst, narrow[:, k, t * P:(t + 1) * P], wide[:, k, :],
                                  start=part == 0 and k == 0, stop=part == 2 and k == ND - 1)
                return last

            def out_projection(l):
                for t in range(NT):
                    for c in range(2):
                        s, n = (8 + c) % 3, ring_no(l, (8 + c) % 3) + (8 + c) // 3
                        if t == 0 and l:
                            pe.wait_ge(ring_in[s], 16 * (n + 1))
                        j = 2 * t + c
                        ge(pe, mix_acc, 8 * l + j - 3 if l or j > 3 else 0)
                        if l == 0:
                            last = product(0, 8 + c, ps[j % 4][:, :], t, channels=False)
                        else:
                            for k in range(ND):
                                last = mm(ps[j % 4][:, :], aoT[:, k, t * P:(t + 1) * P], slot_k(s)[:, k, :], start=k == 0, stop=k == ND - 1)
                        last.then_inc(out_pe, 1)
                        if c == 0 and t:
                            transpose_tile(2 * l + 1, t - 1)
                            if t >= 2:
                                hT_ready(2 * l + 1, t - 2)
                                router_tile(t - 2)
                        if t == NT - 1:
                            pe.wait_ge(out_pe, 8 * l + j + 1)
                            pe.sem_inc(ring_free[s], 1)

            def x_transposes(x, v):
                for g, done in enumerate(("xTa_pe", "xTb_pe")):
                    for j in range(4):
                        d = 4 * g + j
                        last = nc.tensor.transpose(ps[4 + g][:, j * TB:(j + 1) * TB], x[0:TB, d * P:(d + 1) * P], ident[0:TB, 0:TB])
                    last.then_inc(v[done][0], 1)

            def gate_up_split(par, n):
                after(pe, ex, "xTb_lo", n)
                after(pe, ex, "hid_done", n - 1)
                for j, done in enumerate(("gate_pe", "up_pe")):
                    pe.wait_ge(hi_split, WCH * (3 * n + j + 1))
                    hi, lo = as3(ex_hi[j][:, :], ND), as3(w_lo[3 * par + SLOT_OF[j]][:, :], ND)
                    for part, (x, w) in enumerate(((xT_hi, hi), (xT_lo, hi), (xT_hi, lo))):
                        if part == 2:
                            pe.wait_ge(gu_lo_split, WCH * (2 * n + j + 1))
                        if j == 1 and part == 0:
                            after(pe, ex, "gate_pe", n)
                            pe.sem_inc(ring_free[3 * par + SLOT_OF[0]], 1)
                        for k in range(ND):
                            last = mm(ps[j][0:TB, :], x[:, k * TB:(k + 1) * TB], w[:, k, :],
                                      start=part == 0 and k == 0, stop=part == 2 and k == ND - 1)
                    last.then_inc(ex[done][0], 1)

            def down_split(par, n):
                after(pe, ex, "hidT_lo", n)
                pe.wait_ge(hi_split, WCH * (3 * n + 3))
                hi, lo = as3(ex_hi[2][:, :], NFK), as3(w_lo[3 * par + 2][:, :], NFK)
                for c, (ev, done) in enumerate((("ya_ev", "ya_pe"), ("yb_ev", "yb_pe"))):
                    after(pe, ex, ev, n - 1)
                    for part, (x, w) in enumerate(((hidT_hi, hi), (hidT_lo, hi), (hidT_hi, lo))):
                        if c == 0 and part == 2:
                            pe.wait_ge(down_lo_split, WCH * (n + 1))
                        for k in range(NFK):
                            last = mm(ps[2 + c][0:TB, :], x[:, k * TB:(k + 1) * TB], w[:, k, c * WB:(c + 1) * WB],
                                      start=part == 0 and k == 0, stop=part == 2 and k == NFK - 1)
                    last.then_inc(ex[done][0], 1)

            def hid_transposes(v, n):
                after(pe, v, "hid_done", n)
                for k in range(NFK):
                    last = nc.tensor.transpose(ps[6][:, k * TB:(k + 1) * TB], hid[0:TB, k * P:(k + 1) * P], ident[0:TB, 0:TB])
                last.then_inc(v["hidT_pe"][0], 1)

            def gate_up(x_t, w_gate, w_up, v, n):
                after(pe, v, "xTa_ev", n)
                after(pe, v, "xTb_ev", n)
                for bank, w, done in ((0, w_gate, "gate_pe"), (1, w_up, "up_pe")):
                    for k in range(ND):
                        last = mm(ps[bank][0:TB, :], x_t[:, k * TB:(k + 1) * TB], w[:, k, :], start=k == 0, stop=k == ND - 1)
                    last.then_inc(v[done][0], 1)

            def down(w_down, v, n):
                after(pe, v, "hidT_ev", n)
                for c, done in enumerate(("ya_pe", "yb_pe")):
                    for k in range(NFK):
                        last = mm(ps[2 + c][0:TB, :], hidT[:, k * TB:(k + 1) * TB], w_down[:, k, c * WB:(c + 1) * WB], start=k == 0, stop=k == NFK - 1)
                    last.then_inc(v[done][0], 1)

            def moe(l):
                transposes(2 * l + 1, router_tile, routing, first=NT - 1)
                pe.wait_ge(routing, ROUTE * l + OH_READY)
                mm(ps[5][:, 0:16], upper_strict, rkey[:, 0:16], start=True, stop=True)
                for j in range(NT):
                    last = mm(ps[5][:, 16 * (j + 1):80], ones, rkey[:, 16 * j:16 * (j + 1)].unsqueeze(1).broadcast_to([P, NT - j, NE]),
                       start=j == 0, stop=j == NT - 1)
                    if j == 0:
                        mm(ps[5][:, 16:64], upper_strict, rkey[:, 16:64], start=False, stop=False)
                last.then_inc(routing, 1)
                pe.wait_ge(routing, ROUTE * l + PICK_READY)
                for j in range(2 * NT):
                    last = mm(ps[5][:, 96:96 + NE], pick[:, j, :], (oh0, oh1)[j % 2][:, NE * (j // 2):NE * (j // 2 + 1)],
                              start=j == 0, stop=j == 2 * NT - 1)
                last.then_inc(routing, 1)
                pe.wait_ge(routing, ROUTE * l + ADDR_READY)
                pe.wait_ge(xg_in[0], 16 * (8 * l + 1))
                x_transposes(xg[:, 0, :], ex)

                def expert(i, par, more=True):
                    n = NE * l + 2 * i + par
                    gate_up_split(par, n)
                    if more:
                        pe.wait_ge(xg_in[1 - par], 16 * (8 * l + i + par + 1))
                        x_transposes(xg[:, 1 - par, :], ex)
                    after(pe, ex, "up_pe", n)
                    pe.sem_inc(ring_free[3 * par + SLOT_OF[1]], 1)
                    hid_transposes(ex, n)
                    down_split(par, n)
                    after(pe, ex, "yb_pe", n)
                    pe.sem_inc(ring_free[3 * par + 2], 1)

                expert(0, 0)
                expert(0, 1)
                with pe.Fori(1, NE // 2 - 1) as i:
                    expert(i, 0)
                    expert(i, 1)
                expert(NE // 2 - 1, 0)
                expert(NE // 2 - 1, 1, more=False)

                v = ov[l]
                more = pe.value_load(cnt_i[0:1, 0:1], min_val=0, max_val=SEQ)
                with pe.If(more > TB):
                    with pe.Fori(0, NE * (NB - 1)) as r:
                        after(pe, v, "x_in", r)
                        x_transposes(xg[:, 0, :], v)
                        after(pe, v, "w_in", r)
                        gate_up(xT, over_w[0], over_w[1], v, r)
                        hid_transposes(v, r)
                        down(over_w[2], v, r)

            pe.wait_ge(ident_in, 16)
            transposes(0)
            pe.wait_ge(con_in, 16)

            def running_sums():
                pe.wait_ge(fox_gates, LF_READY)
                for t in range(NT):
                    for j in range(t + 1):
                        last = mm(ps[4][:, 64 + 16 * t:80 + 16 * t], upper if j == t else ones, lf[:, 16 * j:16 * j + 16], start=j == 0, stop=j == t)
                last.then_inc(fox_gates, 1)

            def sums_transposed():
                pe.wait_ge(conv_weights, 2)
                pe.wait_ge(fox_gates, C_READY)
                for t in range(NT):
                    last = nc.tensor.transpose(ps[5][0:FOX_H, t * P:(t + 1) * P], c_tok[:, 16 * t:16 * t + 16], ident)
                last.then_inc(fox_gates, 1)

            def head_transposes(n):
                pe.wait_ge(qn_done, n + 1)
                ge(pe, qT_ev, n - 1)
                for j in range(4):
                    last = nc.tensor.transpose(ps[2 + n % 2][:, j * P:(j + 1) * P], qn[:, n % 2, j * P:(j + 1) * P], ident)
                last.then_inc(qT_pe, 1)

            for b in range(8):
                s = b % 3
                for t in range(4):
                    n = 4 * b + t
                    if n < 18:
                        ge(pe, qn_done, n - 1)
                    elif n < 26:
                        pe.wait_ge(v_ev, n - 17)
                    else:
                        pe.wait_ge(og_ev, n - 25)
                    product(0, b, ps[n % 2][:, :], t, channels=b >= 6).then_inc(proj_pe, 1)
                    if 1 <= n <= 16:
                        head_transposes(n - 1)
                    if n == 3:
                        pe.wait_ge(fox_par_in, 16 * N_FOX_PAR)
                        nc.tensor.transpose(ps[5][:, 0:CONV * NCT], conv_raw, ident[0:CONV * NCT, 0:CONV * NCT]).then_inc(conv_weights, 1)
                        pe.wait_ge(gain_ready, 1)
                        gate_logits(fox_gates)
                    if n == 4:
                        gate_transposes(F_COPIED, fox_gates)
                    if n == 8:
                        running_sums()
                    if n == 11:
                        sums_transposed()
                pe.wait_ge(proj_pe, 4 * b + 4)
                pe.sem_inc(ring_free[s], 1)

            pe.wait_ge(qT_ev, 16)
            pe.wait_ge(og_ev, 8)

            def scores(m):
                hd, i = m // NT, m % NT
                lo = FOX_DH * (hd % 2)
                ge(pe, s_sub, m - 3)
                mm(s_banks[m % 4][:, 0:(i + 1) * P], qkT[0][lo:lo + FOX_DH, hd // 2, i * P:(i + 1) * P],
                   qkT[1][lo:lo + FOX_DH, hd // 2, 0:(i + 1) * P], start=True, stop=True).then_inc(s_pe, 1)

            def prob_transposes(m):
                pe.wait_ge(p_ready, m + 1)
                ge(pe, pT_ev, m - 1)
                for j in range(m % NT + 1):
                    last = nc.tensor.transpose(ps[3 + m % 2][:, j * P:(j + 1) * P], s_buf[:, m % 4, j * P:(j + 1) * P], ident)
                last.then_inc(pT_pe, 1)

            def weighted_values(m):
                hd, i = m // NT, m % NT
                lo = FOX_DH * (hd % 2)
                pe.wait_ge(pT_ev, m + 1)
                if i == 0:
                    ge(pe, o_ev, hd // 2 - 1)
                for j in range(i + 1):
                    last = mm(ps[5 + hd // 2 % 2][lo:lo + FOX_DH, i * P:(i + 1) * P], v_tok[:, j, hd * FOX_DH:(hd + 1) * FOX_DH],
                              pT_buf[:, m % 2, j * P:(j + 1) * P], start=j == 0, stop=j == i)
                last.then_inc(pv_pe, 1)

            M = FOX_H * NT
            for m in range(4):
                scores(m)
            for m in range(M):
                if m + 4 < M:
                    scores(m + 4)
                prob_transposes(m)
                if m >= 1:
                    weighted_values(m - 1)
            weighted_values(M - 1)
            pe.wait_ge(o_ev, NPAIR)
            pe.wait_ge(par_in, 16 * N_PAR)
            out_projection(0)
            moe(0)

            transposes(2)
            gate_logits(gdn_gates)

            def square_sums(ct):
                pe.wait_ge(sq2_done, ct + 1)
                ge(pe, rn_done, ct - 3)
                mm(sum_banks[ct % 4][:, :], ones, sq_l2[:, ct % 2, :], start=True, stop=True).then_inc(ss_pe, 1)

            for b in range(8):
                s = b % 3
                for t in range(4):
                    ct = 4 * b + t
                    if b < 6:
                        ge(pe, conv_done, ct - 1)
                        product(1, b, ps[ct % 2][:, :], t, channels=True).then_inc(cv_pe, 1)
                        if ct == 0:
                            gate_transposes(AB_COPIED, gdn_gates)
                        if ct == 2:
                            pe.wait_ge(gdn_gates, G_READY)
                            mm(ps[4][:, 64:96], upper, g_t, start=True, stop=True).then_inc(gdn_gates, 1)
                        if ct == 3:
                            pe.wait_ge(gdn_gates, GC_READY)
                            nc.tensor.transpose(ps[5][0:NT * GDN_H, 0:P], gc_tok, ident).then_inc(gdn_gates, 1)
                        if 1 <= ct <= 16:
                            square_sums(ct - 1)
                    else:
                        if ct < 26:
                            pe.wait_ge(conv_done, ct - 1)
                        else:
                            pe.wait_ge(ogg_ev, ct - 25)
                        product(1, b, ps[ct % 2][:, :], t, channels=False).then_inc(ogg_pe, 1)
                pe.wait_ge(cv_pe if b < 6 else ogg_pe, 4 * b + 4 if b < 6 else 4 * b - 20)
                pe.sem_inc(ring_free[s], 1)

            def outputs_transposed(pr):
                pe.wait_ge(r_done, 6 * (pr + 1))
                pe.wait_ge(on_done, NT * (pr + 1))
                for a in range(2):
                    for n in range(NT):
                        last = nc.tensor.transpose(ps[2 + a][:, n * P:(n + 1) * P], o_tok[:, a, n, :], ident)
                    last.then_inc(oT_pe, 1)

            pe.wait_ge(l2_done, 16)
            pe.wait_ge(silu_done, NCT)
            pe.wait_ge(ogg_ev, 8)
            for pr in range(NHP):
                ge(pe, vn_done, 8 * pr)
                for a in range(2):
                    for n in range(NT):
                        c = slice(n * P, (n + 1) * P)
                        last = mm(ps[4 + a][:, c], kT[:, 2 * pr + a, c], kT[:, 2 * pr + a, c], start=True, stop=True)
                last.then_inc(kk_pe, 1)
                ge(pe, o_cp, 8 * pr)
                for a in range(2):
                    for n in range(NT):
                        c = slice(n * P, (n + 1) * P)
                        last = nc.tensor.transpose(ps[a][:, c], kT[:, 2 * pr + a, c], ident)
                last.then_inc(kT_pe, 1)
                ge(pe, st_done, 6 * pr)
                for a in range(2):
                    for n in range(NT):
                        c = slice(n * P, (n + 1) * P)
                        last = mm(ps[6 + a][:, c], kT[:, 2 * pr + a, c], qT[:, 2 * pr + a, c], start=True, stop=True)
                last.then_inc(kk_pe, 1)
                if pr:
                    outputs_transposed(pr - 1)
                    pe.wait_ge(gao_ev, 2 * pr)
                for a in range(2):
                    for n in range(NT):
                        c = slice(n * P, (n + 1) * P)
                        last = nc.tensor.transpose(ps[2 + a][:, c], vT[:, 2 * pr + a, c], ident)
                last.then_inc(vT_pe, 1)

                pe.wait_ge(k_ev, pr + 1)
                for v in range(LEVELS):
                    pe.wait_ge(ml_done, 7 * pr + v + 1)
                    for a in range(2):
                        if v:
                            pe.wait_ge(X_ev, 12 * pr + 2 * (v - 1) + a + 1)
                        for n in range(NT):
                            c = slice(n * P, (n + 1) * P)
                            if v:
                                last = mm(ps[a][:, c], mlT[v % 2][:, a, n, :], inv[:, a, n, :], start=True, stop=True)
                            else:
                                last = nc.tensor.transpose(ps[a][:, c], mlT[0][:, a, n, :], ident)
                        last.then_inc(T_pe, 1)
                    if v == 0:
                        pe.wait_ge(v_evg, pr + 1)
                        pe.wait_ge(mT_done, pr + 1)
                        continue
                    for a in range(2):
                        pe.wait_ge(T_ev, 12 * pr + 2 * (v - 1) + a + 1)
                        if v == 1:
                            pe.wait_ge(xT0, pr + 1)
                        else:
                            pe.wait_ge(XT_ev, 12 * pr + 2 * (v - 2) + a + 1)
                        for n in range(NT):
                            c = slice(n * P, (n + 1) * P)
                            if v < LEVELS - 1:
                                mm(ps[2 + a][:, c], invT[:, a, n, :], tmpT[:, a, n, :], start=True, stop=True)
                            last = mm(ps[4 + a][:, c], tmpT[:, a, n, :], invT[:, a, n, :], start=True, stop=True)
                        last.then_inc(U_pe, 1)

                pe.wait_ge(att_done, pr + 1)
                pe.wait_ge(XT_ev, 12 * pr + 12)
                for n in range(NT):
                    for a in range(2):
                        if n:
                            pe.wait_ge(st_done, 6 * pr + 2 * (n - 1) + a + 1)
                            mm(ps[2 + a][:, 0:P], k_gate[:, a, n, :], st[:, a, :], start=True, stop=True).then_inc(R_pe, 1)
                            pe.wait_ge(o_cp, 8 * pr + 2 * (n - 1) + a + 1)
                            mm(ps[a][:, 0:P], q_dec[:, a, n, :], st[:, a, :], start=True, stop=False)
                    for a in range(2):
                        if n:
                            pe.wait_ge(r_done, 6 * pr + 2 * (n - 1) + a + 1)
                        mm(ps[4 + a][:, 0:P], invT[:, a, n, :], r_sb[:, a, :] if n else v_chunk[:, a, n, :], start=True, stop=True).then_inc(V_pe, 1)
                    for a in range(2):
                        pe.wait_ge(vn_done, 8 * pr + 2 * n + a + 1)
                        mm(ps[a][:, 0:P], attnT[:, a, n, :], vn_sb[:, a, :], start=n == 0, stop=True).then_inc(O_pe, 1)
                        if n < NT - 1:
                            mm(ps[6 + a][:, 0:P], k_tok[:, a, n, :], vn_sb[:, a, :], start=True, stop=True).then_inc(K_pe, 1)
            outputs_transposed(NHP - 1)
            pe.wait_ge(gao_ev, GDN_H)
            out_projection(1)
            moe(1)

        @block.scalar
        def _(act):
            fn = nc.scalar.activation
            link = linker(act, act_link)

            def transposes_out(k, tiles=range(NT)):
                for t in tiles:
                    for g in range(1 if k % 2 else 2):
                        act.wait_ge(tr_pe, 8 * k + 2 * t + g + 1)
                        dst, done = (hT, tr_act) if k % 2 else (hT_hi, hT_hi_ev)
                        fn(dst[:, 4 * g:4 * g + 4, t * P:(t + 1) * P], as3(ps[6 + g][:, :], 4), ACT.Copy).then_inc(done, 1)

            def split_first(l, c):
                act.wait_ge(ring_in[0], 16 * (ring_no(l, 0) + 1))
                fn(hi_of(0)[:, chunk(c), :], slot_k(0)[:, chunk(c), :], ACT.Copy).then_inc(w_hi_done, 1)

            def inverse_root(dst, src, scale, eps, done):
                link(fn(dst, src, ACT.Ln, scale=scale, bias=eps))
                fn(dst, dst, ACT.Exp, scale=-0.5).then_inc(done, 1)

            def split(l, j, i, par, n):
                s = 3 * par + SLOT_OF[j]
                ge(act, ring_in[s], 16 * (expert_no(l, s) + i + 1))
                after(act, ex, ("gate_pe", "up_pe", "yb_pe")[j], n - 1)
                for c in range(WCH):
                    fn(ex_hi[j][:, 1024 * c:1024 * (c + 1)], slot(s)[:, 1024 * c:1024 * (c + 1)], ACT.Copy).then_inc(hi_split, 1)

            def layer_norm(q):
                if q % 2:
                    weigh(q // 2, 0)
                for t in range(NT):
                    n = NT * q + t
                    if q % 2:
                        weigh(q // 2, t + 1)
                    elif t:
                        transposes_out(q + 1, (t - 1,))
                    act.wait_ge(mean_ready, n + 1)
                    ge(act, ssq_ready, n)
                    fn(ln_sq, h[:, t, :], ACT.Square, bias=neg_mean[:, t:t + 1], accum_out=ssq[:, t:t + 1]).then_inc(ssq_ready, 1)
                    if q % 2 == 0:
                        if t == NT - 1:
                            transposes_out(q + 1, (t,))
                        if t == 1:
                            split(q // 2, 0, 0, 0, NE * (q // 2))
                    elif q == 1 and t >= 2:
                        transposes_out(2, (t - 2,))
                if q == 1:
                    act.wait_ge(comb_done, NT)
                    split_first(1, 0)
                    transposes_out(2, (NT - 2,))
                    split_first(1, 1)
                    transposes_out(2, (NT - 1,))
                    split_first(1, 2)
                    split_first(1, 3)

            def weigh(l, t):
                if t < NT:
                    act.wait_ge(yg_in[t], 32 * (l + 1))
                    for a in range(2):
                        fn(y_got[t][:, a, :], y_got[t][:, a, :], ACT.Copy, scale=gate[a][:, t:t + 1]).then_inc(y_gated, 1)

            def x_out(x_t, v, n):
                after(act, v, "xTa_pe", n)
                fn(x_t[:, 0:4 * TB], ps[4][:, 0:4 * TB], ACT.Copy).then_inc(v["xTa_ev"][0], 1)

            def silu_gate(v, n):
                after(act, v, "gate_pe", n)
                fn(sil[0:TB, :], ps[0][0:TB, :], ACT.Silu).then_inc(v["sil_done"][0], 1)

            def hid_out(v, n):
                after(act, v, "hidT_pe", n)
                fn(hidT[:, 0:NFK * TB], ps[6][:, 0:NFK * TB], ACT.Copy).then_inc(v["hidT_ev"][0], 1)

            def rows_out(y, v, n):
                after(act, v, "ya_pe", n)
                fn(y[0:TB, 0:WB], ps[2][0:TB, :], ACT.Copy).then_inc(v["ya_ev"][0], 1)

            def moe(l):
                act.wait_ge(routing, ROUTE * l + RT_SUB)
                fn(probs, probs, ACT.Exp).then_inc(routing, 1)

                def x_hi(g, n):
                    after(act, ex, ("xTa_pe", "xTb_pe")[g], n)
                    fn(xT_hi[:, 4 * g * TB:4 * (g + 1) * TB], ps[4 + g][:, 0:4 * TB], ACT.Copy).then_inc(ex["xTa_hi"][0], 1)

                split(l, 1, 0, 0, NE * l)
                x_hi(0, NE * l)
                x_hi(1, NE * l)

                def expert(i, par, more=True):
                    n = NE * l + 2 * i + par
                    split(l, 2, i, par, n)
                    after(act, ex, "hid_done", n - 1)
                    silu_gate(ex, n)
                    if more:
                        split(l, 0, i + par, 1 - par, n + 1)
                        after(act, ex, "up_pe", n)
                        x_hi(0, n + 1)
                    after(act, ex, "yb_pe", n - 1)
                    after(act, ex, "hidT_pe", n)
                    fn(hidT_hi[:, :], ps[6][:, 0:NFK * TB], ACT.Copy).then_inc(ex["hidT_hi"][0], 1)
                    if more:
                        x_hi(1, n + 1)
                        split(l, 1, i + par, 1 - par, n + 1)
                    ge(act, y_st[par], 16 * (8 * l + i))
                    rows_out(y_sb[:, par, :], ex, n)

                expert(0, 0)
                expert(0, 1)
                with act.Fori(1, NE // 2 - 1) as i:
                    expert(i, 0)
                    expert(i, 1)
                expert(NE // 2 - 1, 0)
                expert(NE // 2 - 1, 1, more=False)
                for n in range(2):
                    act.wait_ge(y_st[n], 16 * 8 * (l + 1))
                v = ov[l]
                more = act.value_load(cnt_i[0:1, 0:1], min_val=0, max_val=SEQ)
                with act.If(more > TB):
                    with act.Fori(0, NE * (NB - 1)) as r:
                        x_out(xT, v, r)
                        silu_gate(v, r)
                        hid_out(v, r)
                        rows_out(y_sb[:, 0, :], v, r)
                layer_norm(2 * l + 1)

            transposes_out(0)
            for c in range(CHUNKS):
                split_first(0, c)
            act.wait_ge(con_in, 16)

            def logits_out(done, product):
                act.wait_ge(done, product)
                fn(logits_T, ps[4][0:16, :], ACT.Copy).then_inc(done, 1)

            def log_one_plus_exp(x, done):
                link(fn(x, x, ACT.Exp, scale=-1.0))
                fn(x, x, ACT.Ln, bias=one).then_inc(done, 1)

            def head_out(n):
                act.wait_ge(qT_pe, n + 1)
                which, b, t = n // 8, n // 4 % 2, n % 4
                if n == 0:
                    act.wait_ge(gain_ready, 1)
                fn(qkT[which][:, 4 * b:4 * b + 4, t * P:(t + 1) * P], as3(ps[2 + n % 2][:, :], 4), ACT.Copy,
                   scale=gain[:, which:which + 1]).then_inc(qT_ev, 1)

            for n in range(16):
                act.wait_ge(proj_pe, n + 1)
                ge(act, head_sum, n - 1)
                fn(sq[:, n % 2, :], ps[n % 2][:, :], ACT.Square).then_inc(sq_done, 1)
                act.wait_ge(head_sum, n + 1)
                ge(act, qn_done, n - 1)
                inverse_root(head_r[:, n % 2, :], head_ss[:, n % 2, :], 1.0 / FOX_DH, eps_rms, head_rs)
                if n:
                    head_out(n - 1)
                if n == 3:
                    act.wait_ge(conv_weights, 1)
                    fn(conv_w, ps[5][:, 0:CONV * NCT], ACT.Copy).then_inc(conv_weights, 1)
                    logits_out(fox_gates, F_PROD)
                if n == 5:
                    act.wait_ge(fox_gates, F_ABS)
                    log_one_plus_exp(f_e, fox_gates)
                if n == 12:
                    act.wait_ge(fox_gates, CT_PE)
                    link(fn(cT, ps[5][0:FOX_H, :], ACT.Copy))
                    act.dma_start(c_rows, cT).then_inc(c_st, 16)
            for n in range(16, 24):
                act.wait_ge(proj_pe, n + 1)
                fn(v_tok[:, n % 4, (n // 4 - 4) * WB:(n // 4 - 3) * WB], ps[n % 2][:, :], ACT.Copy).then_inc(v_ev, 1)
                if n == 16:
                    head_out(15)
            act.wait_ge(c_st, 16)
            for m in range(8):
                act.wait_ge(proj_pe, 25 + m)
                fn(ogT[:, m, :], ps[m % 2][:, :], ACT.Sigmoid).then_inc(og_ev, 1)

            M = FOX_H * NT

            def exps(m):
                cols_m = (m % NT + 1) * P
                act.wait_ge(max_done, m + 1)
                ge(act, inv_ready, m - 3)
                s = s_buf[:, m % 4, 0:cols_m]
                fn(s, s, ACT.Exp, bias=neg_max[:, m % 4:m % 4 + 1], accum_out=row_sum[:, m % 4:m % 4 + 1]).then_inc(p_exp, 1)

            def normalised(m):
                s = s_buf[:, m % 4, 0:(m % NT + 1) * P]
                act.wait_ge(inv_ready, m + 1)
                fn(s, s, ACT.Copy, scale=row_inv[:, m % 4:m % 4 + 1]).then_inc(p_ready, 1)

            def probs_out(m):
                cols_m = (m % NT + 1) * P
                act.wait_ge(pT_pe, m + 1)
                ge(act, pv_pe, m - 1)
                fn(pT_buf[:, m % 2, 0:cols_m], ps[3 + m % 2][:, 0:cols_m], ACT.Copy).then_inc(pT_ev, 1)

            exps(0)
            normalised(0)
            exps(1)
            for m in range(M):
                if m + 1 < M:
                    normalised(m + 1)
                if m + 2 < M:
                    exps(m + 2)
                probs_out(m)
            act.wait_ge(par_in, 16 * N_PAR)
            layer_norm(0)
            moe(0)

            logits_out(gdn_gates, AB_PROD)

            def gdn_gate_exps():
                act.wait_ge(gdn_gates, AB_PE)
                logits = as3(ps[4][:, 0:NT * 16], NT)
                fn(as3(beta, NT), logits[:, :, 0:GDN_H], ACT.Exp, scale=-1.0).then_inc(gdn_gates, 1)
                link(fn(al_bc, al_bc, ACT.Exp))
                act.wait_ge(gdn_gates, G_ABS)
                log_one_plus_exp(g_e, gdn_gates)

            def l2_roots(ct):
                ge(act, l2_done, ct)
                for j in range(2):
                    act.wait_ge(ss_pe, ct + j + 1)
                    last = fn(r_l2[:, j, :], sum_banks[(ct + j) % 4][:, :], ACT.Ln, bias=eps_l2)
                link(last)
                for j in range(2):
                    fn(r_l2[:, j, :], r_l2[:, j, :], ACT.Exp, scale=-0.5).then_inc(rn_done, 1)

            act.wait_ge(hmid_st, 64)
            for ct in range(NCT):
                act.wait_ge(conv_done, ct + 1)
                dst = qkvT[ct // 8][:, ct % 8, :]
                fn(dst, conv_tmp[:, ct % 2, :], ACT.Silu).then_inc(silu_done, 1)
                if ct < 16:
                    act.wait_ge(silu_done, ct + 1)
                    ge(act, ss_pe, ct - 1)
                    fn(sq_l2[:, ct % 2, :], dst, ACT.Square).then_inc(sq2_done, 1)
                if ct == 0:
                    gdn_gate_exps()
                if ct % 2 and 3 <= ct < 19:
                    l2_roots(ct - 3)
                if ct == 4:
                    act.wait_ge(gdn_gates, GT_PE)
                    link(fn(gT_sb, ps[5][0:NT * GDN_H, 0:P], ACT.Copy))
                    act.dma_start(g_rows, gT_sb).then_inc(g_st, 16)
            for n in range(8):
                act.wait_ge(ogg_pe, n + 1)
                fn(og_tok[:, n % 4, (n // 4) * WB:(n // 4 + 1) * WB], ps[n % 2][:, :], ACT.Silu).then_inc(ogg_ev, 1)

            def decay_exps(pr):
                act.wait_ge(gbc_in, 32 * (pr + 1))
                if pr:
                    act.wait_ge(XT_ev, 12 * (pr - 1) + 1)
                fn(g_exp, g_bc, ACT.Exp).then_inc(gexp_done, 1)
                act.wait_ge(dec_arg, pr + 1)
                fn(dec, dec, ACT.Exp).then_inc(dec_done, 1)
                act.wait_ge(kd_arg, pr + 1)
                fn(as3(egl[pr % 2], 2), g_bc[:, :, :, P - 1], ACT.Exp)
                link(fn(kd, kd, ACT.Exp))

            def outputs_out(pr):
                for a in range(2):
                    act.wait_ge(oT_pe, 2 * pr + a + 1)
                    fn(aoT[:, 2 * pr + a, :], ps[2 + a][:, :], ACT.Copy, scale=ng_col).then_inc(gao_ev, 1)

            decay_exps(0)
            for pr in range(NHP):
                act.wait_ge(kT_pe, pr + 1)
                for a in range(2):
                    for n in range(NT):
                        last = fn(k_tok[:, a, n, :], ps[a][:, n * P:(n + 1) * P], ACT.Copy, scale=kd[:, NT * a + n:NT * a + n + 1])
                last.then_inc(k_ev, 1)
                if pr:
                    outputs_out(pr - 1)
                act.wait_ge(vT_pe, pr + 1)
                for a in range(2):
                    last = fn(v_chunk[:, a, :, :], as3(ps[2 + a][:, :], NT), ACT.Copy)
                last.then_inc(v_evg, 1)
                for v in range(1, LEVELS):
                    for a in range(2):
                        act.wait_ge(T_pe, 14 * pr + 2 * v + a + 1)
                        fn(tmpT[:, a, :, :], as3(ps[a][:, :], NT), ACT.Copy).then_inc(T_ev, 1)
                    if v == 4 and pr + 1 < NHP:
                        decay_exps(pr + 1)
                for n in range(NT):
                    for a in range(2):
                        act.wait_ge(V_pe, 8 * pr + 2 * n + a + 1)
                        hd = n * GDN_H + 2 * pr + a
                        fn(vn_sb[:, a, :], ps[4 + a][:, 0:P], ACT.Copy, scale=beta[:, hd:hd + 1]).then_inc(vn_done, 1)
                    for a in range(2):
                        act.wait_ge(O_pe, 8 * pr + 2 * n + a + 1)
                        fn(o_tok[:, a, n, :], ps[a][:, 0:P], ACT.Copy).then_inc(o_cp, 1)
                    act.wait_ge(o_cp, 8 * pr + 2 * n + 2)
                    ge(act, o_sq, 8 * pr + 2 * n)
                    for a in range(2):
                        c = NT * a + n
                        fn(sq_o[:, a, :], o_tok[:, a, n, :], ACT.Square, accum_out=o_ss[:, c:c + 1]).then_inc(o_sq, 1)
            outputs_out(NHP - 1)
            layer_norm(2)
            moe(1)

        @block.vector
        def _(dve):
            tt, ts, stt = nc.vector.tensor_tensor, nc.vector.tensor_scalar, nc.vector.scalar_tensor_tensor
            red = nc.vector.tensor_reduce
            link = linker(dve, dve_link)

            def transposes_out(k, tiles=range(NT)):
                for t in tiles:
                    if k % 2:
                        dve.wait_ge(tr_pe, 8 * k + 2 * t + 2)
                        nc.vector.tensor_copy(hT[:, 4:8, t * P:(t + 1) * P], as3(ps[7][:, :], 4)).then_inc(tr_dve, 1)
                        continue
                    for g in range(2):
                        part = (slice(None), slice(4 * g, 4 * g + 4), slice(t * P, (t + 1) * P))
                        dve.wait_ge(hT_hi_ev, 2 * (NT * (k // 2) + t) + g + 1)
                        tt(hT_lo[part], as3(ps[6 + g][:, :], 4), hT_hi[part].bitcast(f32), ALU.subtract).then_inc(hT_lo_ev, 1)

            def split_hi(l, b, c):
                if c == 0:
                    dve.wait_ge(ring_in[b % 3], 16 * (ring_no(l, b % 3) + b // 3 + 1))
                    ge(dve, cv_pe if l else proj_pe, 4 * (b - 1))
                nc.vector.tensor_copy(hi_of(b)[:, chunk(c), :], slot_k(b % 3)[:, chunk(c), :]).then_inc(w_hi_done, 1)

            def split_first_lo(l):
                for c in range(CHUNKS // 2, CHUNKS):
                    dve.wait_ge(w_hi_done, CHUNKS * 10 * l + c + 1)
                    tt(lo_of(0)[:, chunk(c), :], slot_k(0)[:, chunk(c), :], hi_of(0)[:, chunk(c), :].bitcast(f32),
                       ALU.subtract).then_inc(w_lo_done, 1)

            def split_gates(w):
                link(nc.vector.tensor_copy(gates_hi, w))
                link(tt(gates_lo, w, gates_hi.bitcast(f32), ALU.subtract))

            def mean(t):
                ts(neg_mean[:, t:t + 1], sum2[:, 2 * t:2 * t + 1], sum2[:, 2 * t + 1:2 * t + 2], -1.0 / D,
                   ALU.add, ALU.mult).then_inc(mean_ready, 1)

            def centred(q, t):
                dve.wait_ge(ln_in, 32 * (q + 1))
                ge(dve, h_ready, NT * q + t)
                link(stt(ln_x, h[:, t, :], neg_mean[:, t:t + 1], ln_g, ALU.add, ALU.mult))

            def scaled(q, t):
                dve.wait_ge(rstd_ready, NT * q + t + 1)
                stt(h[:, t, :], ln_x, rstd[:, t:t + 1], ln_b, ALU.mult, ALU.add).then_inc(h_ready, 1)

            def split(j, par, n, chunks=range(WCH)):
                for c in chunks:
                    s, part = 3 * par + SLOT_OF[j], slice(1024 * c, 1024 * (c + 1))
                    ge(dve, hi_split, WCH * (3 * n + j) + c + 1)
                    tt(w_lo[s][:, part], ring[s][:, part], ex_hi[j][:, part].bitcast(f32), ALU.subtract).then_inc(gu_lo_split, 1)

            def mixer_norm(l):
                dve.wait_ge(res_in, 64 * (l + 1))
                for t in range(NT):
                    for c in range(2):
                        if c and t:
                            transposes_out(2 * l + 1, (t - 1,))
                        dve.wait_ge(out_pe, 8 * l + 2 * t + c + 1)
                        hc = h[:, t, c * WB:(c + 1) * WB]
                        stt(hc, hc, ALPHA, ps[(2 * t + c) % 4][:, :], ALU.mult, ALU.add,
                            accum_out=sum2[:, 2 * t + c:2 * t + c + 1]).then_inc(mix_acc, 1)
                    dve.wait_ge(mix_acc, 8 * l + 2 * t + 2)
                    mean(t)
                    dve.wait_ge(mean_ready, 8 * l + t + 1)
                    centred(2 * l, t)
                    scaled(2 * l, t)
                    if t == 1:
                        split(0, 0, NE * l)
                transposes_out(2 * l + 1, (NT - 1,))

            def router(l):
                def grp(x):
                    return as3(x, NT * NG)

                def tok(x):
                    return as3(x, NT)

                def bc(x, n):
                    return x.unsqueeze(2).broadcast_to([P, x.shape[1], n])

                dve.wait_ge(routing, ROUTE * l + RT_PE)
                link(red(rmx, tok(ps[4][:, 0:64]), X, ALU.max))
                tt(tok(probs), tok(ps[4][:, 0:64]), bc(rmx, NE), ALU.subtract).then_inc(routing, 1)
                dve.wait_ge(routing, ROUTE * l + RT_EXP)
                link(red(rsm, tok(probs), X, ALU.add))
                link(nc.vector.reciprocal(rsm, rsm))
                link(tt(tok(probs), tok(probs), bc(rsm, NE), ALU.mult))
                link(tt(selv, probs, rb_bc, ALU.add))
                s = [grp(selv)[:, :, k] for k in range(EPG)]
                link(tt(gr[0], s[0], s[1], ALU.max))
                link(tt(gr[1], s[0], s[1], ALU.min))
                link(tt(gr[2], s[2], s[3], ALU.max))
                link(tt(gr[3], s[2], s[3], ALU.min))
                link(tt(gr[4], gr[0], gr[2], ALU.max))
                link(tt(gr[0], gr[0], gr[2], ALU.min))
                link(tt(gr[1], gr[1], gr[3], ALU.max))
                link(tt(gr[0], gr[0], gr[1], ALU.max))
                link(tt(gr[0], gr[0], gr[4], ALU.add))

                def first_best(oh, val, key, weight, n):
                    link(red(rmx, tok(val), X, ALU.max))
                    link(tt(tok(key), tok(val), bc(rmx, n), ALU.is_equal))
                    link(tt(key, key, weight, ALU.mult))
                    link(red(rmx, tok(key), X, ALU.max))
                    link(tt(tok(oh), tok(key), bc(rmx, n), ALU.is_equal))

                first_best(gr[1], gr[0], gr[2], con[:, C_GW:C_EW], NG)
                link(ts(gr[1], gr[1], 1.0, BIG, ALU.subtract, ALU.mult))
                link(tt(grp(selv), grp(selv), bc(gr[1], EPG), ALU.add))
                first_best(oh0, selv, rkey, con[:, C_EW:C_EI], NE)
                link(stt(selv, oh0, -BIG, selv, ALU.mult, ALU.add))
                first_best(oh1, selv, rkey, con[:, C_EW:C_EI], NE)
                tt(rkey, oh0, oh1, ALU.add).then_inc(routing, 1)
                dve.wait_ge(routing, ROUTE * l + POS_PE)
                for a, oh in enumerate((oh0, oh1)):
                    link(tt(rtmp, ps[5][:, 0:64], oh, ALU.mult))
                    link(red(pos[a], tok(rtmp), X, ALU.add))
                for t in range(NT):
                    for a in range(2):
                        j = 2 * t + a
                        last = ts(pick[:, j, :], con[:, C_IOTA:C_ROW], pos[a][:, t:t + 1], con[:, C_ROW + j:C_ROW + j + 1],
                                  ALU.is_equal, ALU.mult)
                last.then_inc(routing, 1)
                for a, oh in enumerate((oh0, oh1)):
                    link(tt(rtmp, probs, oh, ALU.mult))
                    link(red(gate[a], tok(rtmp), X, ALU.add))
                link(tt(gsum, gate[0], gate[1], ALU.add))
                link(nc.vector.reciprocal(gsum, gsum))
                for a in range(2):
                    link(tt(gate[a], gate[a], gsum, ALU.mult))
                dve.wait_ge(routing, ROUTE * l + LIST_PE)
                link(ts(empty_f, ps[5][:, 96:96 + NE], 0.0, float(EMPTY + 1), ALU.is_equal, ALU.mult))
                link(stt(row_f, ps[5][:, 96:96 + NE], -1.0, empty_f, ALU.add, ALU.add))
                link(ts(empty_f, row_f, 0.5, -0.25, ALU.mult, ALU.add))
                link(nc.vector.tensor_copy(first_row, row_f))
                nc.vector.tensor_copy(first_tok, empty_f).then_inc(routing, 1)
                for a, oh in enumerate((oh0, oh1)):
                    link(tt(rtmp, con[:, C_EI:C_EPS], oh, ALU.mult))
                    link(red(exp_n, tok(rtmp), X, ALU.add))
                    link(ts(blk, pos[a], float(TB), None, ALU.is_ge))
                    for k in range(2, NB):
                        link(stt(blk, pos[a], float(k * TB), blk, ALU.is_ge, ALU.add))
                    link(stt(exp_n, exp_n, float(NB), blk, ALU.mult, ALU.add))
                    link(stt(pos[a], blk, -float(TB), pos[a], ALU.mult, ALU.add))
                    by_a = addr_i.rearrange("p (t a) -> p t a", a=2)[:, :, a]
                    link(stt(by_a, pos[a], float(NE * NB), exp_n, ALU.mult, ALU.add))
                link(red(cmax, ps[5][:, 64:80], X, ALU.max))
                nc.vector.tensor_copy(cnt_i, cmax).then_inc(routing, 1)

            def x_out(x_t, v, n):
                after(dve, v, "xTb_pe", n)
                nc.vector.tensor_copy(x_t[:, 4 * TB:8 * TB], ps[5][:, 0:4 * TB]).then_inc(v["xTb_ev"][0], 1)

            def hidden(v, n):
                after(dve, v, "sil_done", n)
                after(dve, v, "up_pe", n)
                tt(hid[0:TB, :], ps[1][0:TB, :], sil[0:TB, :], ALU.mult).then_inc(v["hid_done"][0], 1)

            def rows_out(y, v, n):
                after(dve, v, "yb_pe", n)
                nc.vector.tensor_copy(y[0:TB, WB:2 * WB], ps[3][0:TB, :]).then_inc(v["yb_ev"][0], 1)

            def moe(l):
                router(l)
                def x_lo(g, n):
                    after(dve, ex, ("xTa_hi", "xTb_hi")[g], n)
                    part = (slice(None), slice(4 * g * TB, 4 * (g + 1) * TB))
                    tt(xT_lo[part], ps[4 + g][:, 0:4 * TB], xT_hi[part].bitcast(f32), ALU.subtract).then_inc(ex["xTa_lo"][0], 1)

                split(1, 0, NE * l, (0, 1))
                x_lo(0, NE * l)
                x_lo(1, NE * l)
                split(1, 0, NE * l, (2, 3))

                def expert(i, par, more=True):
                    n = NE * l + 2 * i + par
                    if more:
                        split(0, 1 - par, n + 1, range(WCH - 1))
                    after(dve, ex, "hidT_pe", n - 1)
                    hidden(ex, n)
                    if more:
                        split(0, 1 - par, n + 1, (WCH - 1,))
                        x_lo(0, n + 1)
                    after(dve, ex, "hidT_hi", n)
                    tt(hidT_lo[:, :], ps[6][:, 0:NFK * TB], hidT_hi[:, :].bitcast(f32), ALU.subtract).then_inc(ex["hidT_lo"][0], 1)
                    if more:
                        x_lo(1, n + 1)
                        split(1, 1 - par, n + 1)
                    else:
                        for c in range(WCH // 2, WCH):
                            part = slice(1024 * c, 1024 * (c + 1))
                            dve.wait_ge(hi_split, WCH * (3 * n + 2) + c + 1)
                            tt(w_lo[5][:, part], ring[5][:, part], ex_hi[2][:, part].bitcast(f32), ALU.subtract).then_inc(down_lo_split, 1)
                    ge(dve, y_st[par], 16 * (8 * l + i))
                    rows_out(y_sb[:, par, :], ex, n)

                expert(0, 0)
                expert(0, 1)
                with dve.Fori(1, NE // 2 - 1) as i:
                    expert(i, 0)
                    expert(i, 1)
                expert(NE // 2 - 1, 0)
                expert(NE // 2 - 1, 1, more=False)
                for n in range(2):
                    dve.wait_ge(y_st[n], 16 * 8 * (l + 1))
                v = ov[l]
                more = dve.value_load(cnt_i[0:1, 0:1], min_val=0, max_val=SEQ)
                with dve.If(more > TB):
                    with dve.Fori(0, NE * (NB - 1)) as r:
                        x_out(xT, v, r)
                        hidden(v, r)
                        rows_out(y_sb[:, 0, :], v, r)
                q = 2 * l + 1
                for t in range(NT):
                    dve.wait_ge(y_sum, NT * l + t + 1)
                    stt(h[:, t, :], h[:, t, :], ALPHA, y_got[t][:, 0, :], ALU.mult, ALU.add,
                        accum_out=sum2[:, 2 * t:2 * t + 1]).then_inc(comb_done, 1)
                    dve.wait_ge(comb_done, NT * l + t + 1)
                    ts(neg_mean[:, t:t + 1], sum2[:, 2 * t:2 * t + 1], -1.0 / D, None, ALU.mult).then_inc(mean_ready, 1)
                    if t:
                        scaled(q, t - 1)
                    dve.wait_ge(mean_ready, NT * q + t + 1)
                    centred(q, t)
                    if q == 1 and t >= 2:
                        transposes_out(2, (t - 2,))
                scaled(q, NT - 1)

            transposes_out(0)
            split_first_lo(0)
            dve.wait_ge(con_in, 16)
            dve.wait_ge(fox_par_in, 16 * N_FOX_PAR)
            split_gates(w_f)
            ts(gain[:, 0:1], gain[:, 0:1], FOX_DH ** -0.5, None, ALU.mult).then_inc(gain_ready, 1)

            def bc64(x):
                return x.unsqueeze(2).broadcast_to([P, 8, FOX_DH])

            for n in range(16):
                dve.wait_ge(sq_done, n + 1)
                red(head_ss[:, n % 2, :], as3(sq[:, n % 2, :], 8), X, ALU.add).then_inc(head_sum, 1)
                if n == 5:
                    dve.wait_ge(fox_gates, F_PE)
                    link(tt(f_z, ps[4][:, 0:64], bf_bc, ALU.add))
                    stt(f_e, f_z, -1.0, f_z, ALU.mult, ALU.max).then_inc(fox_gates, 1)
                if n == 7:
                    dve.wait_ge(fox_gates, F_LN)
                    stt(lf, f_z, 0.0, f_e, ALU.min, ALU.subtract).then_inc(fox_gates, 1)
                if n == 10:
                    dve.wait_ge(fox_gates, CSUM_PE)
                    nc.vector.tensor_copy(c_tok, ps[4][:, 64:128]).then_inc(fox_gates, 1)
                dve.wait_ge(head_rs, n + 1)
                ge(dve, qT_pe, n - 1)
                tt(as3(qn[:, n % 2, :], 8), as3(ps[n % 2][:, :], 8), bc64(head_r[:, n % 2, :]), ALU.mult).then_inc(qn_done, 1)
                for c in AHEAD[n % 4]:
                    split_hi(0, n // 4 + 1, c)
            for b in range(5, 9):
                for c in range(CHUNKS):
                    split_hi(0, b, c)
            for c in range(CHUNKS):
                split_hi(0, 9, c)

            M = FOX_H * NT

            def shifted(m):
                hd, i = m // NT, m % NT
                n = (i + 1) * P
                s = s_buf[:, m % 4, :]
                dve.wait_ge(s_pe, m + 1)
                if i == 0:
                    dve.wait_ge(c_in[hd % 2], 16 * (hd // 2 + 1))
                ge(dve, pT_pe, m - 3)
                stt(s[:, 0:n], s_banks[m % 4][:, 0:n], c_tok[:, 16 * i + hd:16 * i + hd + 1], c_buf[:, hd % 2, 0:n],
                    ALU.add, ALU.subtract).then_inc(s_sub, 1)
                dve.wait_ge(s_sub, m + 1)
                link(tt(s[:, n - P:n], s[:, n - P:n], causal, ALU.add))
                red(neg_max[:, m % 4:m % 4 + 1], s[:, 0:n], X, ALU.max, negate=True).then_inc(max_done, 1)

            def inverse_sum(m):
                dve.wait_ge(p_exp, m + 1)
                nc.vector.reciprocal(row_inv[:, m % 4:m % 4 + 1], row_sum[:, m % 4:m % 4 + 1]).then_inc(inv_ready, 1)

            def gated(pr):
                dve.wait_ge(og_ev, pr + 1)
                dve.wait_ge(pv_pe, 8 * (pr + 1))
                tt(ogT[:, pr, :], ps[5 + pr % 2][:, :], ogT[:, pr, :], ALU.mult).then_inc(o_ev, 1)

            shifted(0)
            shifted(1)
            inverse_sum(0)
            shifted(2)
            for m in range(M):
                if m + 1 < M:
                    inverse_sum(m + 1)
                if m + 3 < M:
                    shifted(m + 3)
                if m % 8 == 1 and m > 8:
                    gated(m // 8 - 1)
            gated(NPAIR - 1)
            dve.wait_ge(par_in, 16 * N_PAR)
            mixer_norm(0)
            moe(0)

            dve.wait_ge(h_ready, 2 * NT)
            split_gates(w_ab)
            transposes_out(2, range(NT - 2, NT))
            split_first_lo(1)

            def gdn_gates_first():
                dve.wait_ge(gdn_gates, BETA_EXP)
                link(ts(beta, beta, 1.0, None, ALU.add))
                link(nc.vector.reciprocal(beta, beta))
                link(tt(as3(g_z, NT), as3(ps[4][:, 0:NT * 16], NT)[:, :, GDN_H:2 * GDN_H], as3(dt_bc, NT), ALU.add))
                stt(g_e, g_z, -1.0, g_z, ALU.mult, ALU.max).then_inc(gdn_gates, 1)

            def gdn_gates_second():
                dve.wait_ge(gdn_gates, G_EXP1)
                link(stt(g_t, g_z, 0.0, g_e, ALU.max, ALU.add))
                stt(g_t, g_t, -1.0, al_bc, ALU.mult, ALU.mult).then_inc(gdn_gates, 1)

            def l2_apply(ct):
                dve.wait_ge(rn_done, ct + 1)
                x = qkvT[ct // 8][:, ct % 8, :]
                stt(x, r_l2[:, ct % 2, :], P ** -0.5 if ct < 8 else 1.0, x, ALU.mult, ALU.mult).then_inc(l2_done, 1)

            for ct in range(NCT):
                dve.wait_ge(cv_pe, ct + 1)
                ge(dve, silu_done, ct - 1)
                x, y = ps[ct % 2], conv_tmp[:, ct % 2, :]

                def tap(w):
                    return conv_w[:, w * NCT + ct:w * NCT + ct + 1]

                link(ts(y, x[:, :], tap(CONV - 1), None, ALU.mult))
                for d in range(1, CONV):
                    last = stt(y[:, d:SEQ], x[:, 0:SEQ - d], tap(CONV - 1 - d), y[:, d:SEQ], ALU.mult, ALU.add)
                    if d < CONV - 1:
                        link(last)
                last.then_inc(conv_done, 1)
                if ct == 0:
                    gdn_gates_first()
                if ct == 1:
                    gdn_gates_second()
                if ct == 2:
                    dve.wait_ge(gdn_gates, GC_PE)
                    nc.vector.tensor_copy(gc_tok, ps[4][:, 64:96]).then_inc(gdn_gates, 1)
                for c in AHEAD[ct % 4]:
                    split_hi(1, ct // 4 + 1, c)
                if ct % 2 == 0 and 4 <= ct < 20:
                    l2_apply(ct - 4)
                    l2_apply(ct - 3)
            for c in range(CHUNKS):
                split_hi(1, 7, c)

            def decay_args(pr):
                dve.wait_ge(gbc_in, 32 * (pr + 1))
                if pr:
                    dve.wait_ge(att_done, pr)
                    dve.wait_ge(k_ev, pr)
                for a in range(2):
                    for n in range(NT):
                        hd = n * GDN_H + 2 * pr + a
                        last = stt(dec[:, a, n, :], g_bc[:, a, n, :], gc_tok[:, hd:hd + 1], causal_t, ALU.subtract, ALU.add)
                last.then_inc(dec_arg, 1)
                tt(as3(kd, 2), g_bc[:, :, :, P - 1], gc_tok.rearrange("p (n a) -> p a n", a=GDN_H)[:, 2 * pr:2 * pr + 2, :],
                   ALU.subtract).then_inc(kd_arg, 1)

            def outputs_gated(pr, n):
                dve.wait_ge(or_done, NT * pr + n + 1)
                for a in range(2):
                    c, hd = NT * a + n, 2 * pr + a
                    last = stt(o_tok[:, a, n, :], o_tok[:, a, n, :], o_r[:, c:c + 1], og_tok[:, n, hd * P:(hd + 1) * P], ALU.mult, ALU.mult)
                last.then_inc(on_done, 1)

            decay_args(0)
            for pr in range(NHP):
                dve.wait_ge(kk_pe, 2 * pr + 1)
                dve.wait_ge(dec_done, pr + 1)
                for a in range(2):
                    for n in range(NT):
                        hd = n * GDN_H + 2 * pr + a
                        last = stt(mT[:, a, n, :], ps[4 + a][:, n * P:(n + 1) * P], beta[:, hd:hd + 1], dec[:, a, n, :], ALU.mult, ALU.mult)
                last.then_inc(mT_done, 1)
                if pr:
                    outputs_gated(pr - 1, NT - 1)
                dve.wait_ge(kk_pe, 2 * pr + 2)
                for a in range(2):
                    last = tt(attnT[:, a, :, :], as3(ps[6 + a][:, :], NT), dec[:, a, :, :], ALU.mult)
                last.then_inc(att_done, 1)
                dve.wait_ge(ml_done, 7 * pr + 1)
                for a in range(2):
                    last = tt(invT[:, a, :, :], ident.unsqueeze(1).broadcast_to([P, NT, P]), mlT[0][:, a, :, :], ALU.subtract)
                last.then_inc(xT0, 1)

                def with_gates():
                    dve.wait_ge(gexp_done, pr + 1)
                    for a in range(2):
                        tt(q_dec[:, a, :, :], as3(qT[:, 2 * pr + a, :], NT), g_exp[:, a, :, :], ALU.mult)
                        tt(k_gate[:, a, :, :], as3(kT[:, 2 * pr + a, :], NT), g_exp[:, a, :, :], ALU.mult)

                for a in range(2):
                    dve.wait_ge(T_pe, 14 * pr + a + 1)
                    tt(inv[:, a, :, :], ident.unsqueeze(1).broadcast_to([P, NT, P]), as3(ps[a][:, :], NT), ALU.subtract).then_inc(X_ev, 1)
                with_gates()
                dve.wait_ge(xT0, pr + 1)
                for v in range(1, LEVELS):
                    for a in range(2):
                        dve.wait_ge(U_pe, 12 * pr + 2 * (v - 1) + a + 1)
                        if v < LEVELS - 1:
                            tt(inv[:, a, :, :], inv[:, a, :, :], as3(ps[2 + a][:, :], NT), ALU.subtract).then_inc(X_ev, 1)
                        tt(invT[:, a, :, :], invT[:, a, :, :], as3(ps[4 + a][:, :], NT), ALU.subtract).then_inc(XT_ev, 1)
                    if v == 3 and pr + 1 < NHP:
                        decay_args(pr + 1)
                for n in range(NT):
                    for a in range(2):
                        if n:
                            dve.wait_ge(R_pe, 6 * pr + 2 * (n - 1) + a + 1)
                            tt(r_sb[:, a, :], v_chunk[:, a, n, :], ps[2 + a][:, 0:P], ALU.subtract).then_inc(r_done, 1)
                    if n:
                        outputs_gated(pr, n - 1)
                    for a in range(2):
                        if n < NT - 1:
                            dve.wait_ge(K_pe, 6 * pr + 2 * n + a + 1)
                            if n == 0:
                                nc.vector.tensor_copy(st[:, a, :], ps[6 + a][:, 0:P]).then_inc(st_done, 1)
                            else:
                                stt(st[:, a, :], st[:, a, :], egl[pr % 2][:, NT * a + n:NT * a + n + 1], ps[6 + a][:, 0:P],
                                    ALU.mult, ALU.add).then_inc(st_done, 1)
            outputs_gated(NHP - 1, NT - 1)
            mixer_norm(1)
            moe(1)


INPUTS = ("x", "ln_mix_g", "ln_mix_b", "ln_ffn_g", "ln_ffn_b", "router_w", "router_b", "fox_w_in", "fox_b_f",
          "fox_q_gain", "fox_k_gain", "fox_w_out", "gdn_w_in", "gdn_conv_w", "gdn_a_log", "gdn_dt_bias",
          "gdn_norm_g", "gdn_w_out", "moe_w_gate", "moe_w_up", "moe_w_down")


def kernel(**inputs):
    import concourse.bacc as bacc
    from concourse.bass_utils import run_bass_kernel_spmd

    nc = bacc.Bacc("TRN2", target_bir_lowering=False, num_devices=1)
    arrays = {name: np.ascontiguousarray(inputs[name]) for name in INPUTS}
    arrays["con"], arrays["rows"] = constants(), row_numbers()
    io = {name: nc.dram_tensor(f"in_{name}", a.shape, mybir.dt.from_np(a.dtype), kind="ExternalInput").ap()
          for name, a in arrays.items()}
    out = nc.dram_tensor("out", (1, SEQ, D), mybir.dt.float32, kind="ExternalOutput").ap()
    hybrid_trunk(nc, io, out)
    result = run_bass_kernel_spmd(nc, [{f"in_{name}": a for name, a in arrays.items()}], core_ids=[0])
    return result.results[0]["out"]
```
